# Optimizing a Trainium2 kernel written in Bass

```python
import jax, jax.numpy as jnp
from jax import lax
import numpy as np

D_MODEL = 1024
BATCH = 1
SEQ = 256
DEPTH = 2

GRID_W = 64
CTX_LEN = 256
EPS = 1e-6
GLA_HEADS = 4
GLA_DV = D_MODEL // 2 // GLA_HEADS
GLA_DK = GLA_DV // 2
GLA_RANK = 16
GLA_NORMALIZER = 16.0
GLA_CHUNK = 64
CONV_CH = D_MODEL // 2
CONV_WIDTH = 31
ATT_HEAD_DIM = 128
ATT_HEADS = D_MODEL // ATT_HEAD_DIM
ATT_KV_HEADS = max(1, ATT_HEADS // 4)
ATT_BLOCK = 128
ROPE_THETA = 10000.0
MOE_GROUPS = 4
MOE_EXPERTS_PER_GROUP = 4
MOE_EXPERTS = MOE_GROUPS * MOE_EXPERTS_PER_GROUP
MOE_TOP_K = 2
MOE_HIDDEN = D_MODEL // 2
N_EVEN = (DEPTH + 1) // 2
N_ODD = DEPTH // 2
EVEN_SPLITS = [GLA_HEADS * GLA_DK, GLA_HEADS * GLA_DK, GLA_HEADS * GLA_DV, GLA_HEADS * GLA_DV,
               GLA_RANK, GLA_RANK, CONV_CH, CONV_CH]
EVEN_IN = int(sum(EVEN_SPLITS))
EVEN_MIX = GLA_HEADS * GLA_DV + CONV_CH
ODD_IN = (ATT_HEADS + 2 * ATT_KV_HEADS) * ATT_HEAD_DIM
ODD_MIX = ATT_HEADS * ATT_HEAD_DIM

kernel_name = "hybrid_gla_conv_gqa_hmoe_dit"

def rms_norm(x):
    xf = x.astype(jnp.float32)
    return (xf * lax.rsqrt(jnp.mean(xf * xf, axis=-1, keepdims=True) + EPS)).astype(x.dtype)

def layer_norm(x, g, b):
    xf = x.astype(jnp.float32)
    mu = jnp.mean(xf, axis=-1, keepdims=True)
    var = jnp.mean(jnp.square(xf - mu), axis=-1, keepdims=True)
    return ((xf - mu) * lax.rsqrt(var + EPS)).astype(x.dtype) * g + b

def modulate(x, shift, scale):
    return rms_norm(x) * (1.0 + scale) + shift

def gla_chunked(q, k, v, log_a, s0):
    b_, h_, t_, dk = q.shape
    dv = v.shape[-1]
    n = t_ // GLA_CHUNK
    qc = q.reshape(b_, h_, n, GLA_CHUNK, dk)
    kc = k.reshape(b_, h_, n, GLA_CHUNK, dk)
    vc = v.reshape(b_, h_, n, GLA_CHUNK, dv)
    cum = jnp.cumsum(log_a.astype(jnp.float32).reshape(b_, h_, n, GLA_CHUNK, dk), axis=3)
    last = cum[:, :, :, -1:, :]
    q_t = qc * jnp.exp(cum)
    k_t = kc * jnp.exp(-cum)
    k_end = kc * jnp.exp(last - cum)
    mask = jnp.tril(jnp.ones((GLA_CHUNK, GLA_CHUNK), dtype=bool))
    att = jnp.where(mask, jnp.einsum('bhnid,bhnjd->bhnij', q_t, k_t), 0.0)
    o_intra = jnp.einsum('bhnij,bhnjv->bhniv', att, vc)
    u = jnp.einsum('bhnjd,bhnjv->bhndv', k_end, vc).astype(jnp.float32)
    chunk_decay = jnp.exp(last[:, :, :, 0, :])

    def step(s, inp):
        dec, uu = inp
        return dec[..., None] * s + uu, s

    s_final, s_prev = lax.scan(step, s0, (jnp.moveaxis(chunk_decay, 2, 0), jnp.moveaxis(u, 2, 0)))
    s_prev = jnp.moveaxis(s_prev, 0, 2)
    o_inter = jnp.einsum('bhnid,bhndv->bhniv', q_t, s_prev)
    o = (o_intra + o_inter).reshape(b_, h_, t_, dv).astype(v.dtype)
    return o, s_final

def even_mixer(h, s0_f, s0_b, w_in, dec_w_f, dec_b_f, dec_w_b, dec_b_b, gla_norm_g,
               conv_w, conv_b, conv_norm_g, conv_norm_b, w_out):
    b_, t_, _ = h.shape
    p = h @ w_in
    q, k, v, r, zf, zb, ca, cg = jnp.split(p, np.cumsum(EVEN_SPLITS)[:-1].tolist(), axis=-1)

    def heads(y, d):
        return y.reshape(b_, t_, GLA_HEADS, d).transpose(0, 2, 1, 3)

    q = heads(q, GLA_DK) * (GLA_DK ** -0.5)
    k = heads(k, GLA_DK)
    v = heads(v, GLA_DV)
    la_f = heads(jax.nn.log_sigmoid((zf @ dec_w_f + dec_b_f).astype(jnp.float32)) / GLA_NORMALIZER, GLA_DK)
    la_b = heads(jax.nn.log_sigmoid((zb @ dec_w_b + dec_b_b).astype(jnp.float32)) / GLA_NORMALIZER, GLA_DK)
    o_f, s_f = gla_chunked(q, k, v, la_f, s0_f)
    flip = lambda y: jnp.flip(y, axis=2)
    o_b, s_b = gla_chunked(flip(q), flip(k), flip(v), flip(la_b), s0_b)
    o = rms_norm(o_f + flip(o_b)) * gla_norm_g
    o = o.transpose(0, 2, 1, 3).reshape(b_, t_, GLA_HEADS * GLA_DV) * jax.nn.silu(r)
    u = ca * jax.nn.sigmoid(cg)
    u = lax.conv_general_dilated(u, conv_w, window_strides=(1,),
                                 padding=[(CONV_WIDTH // 2, CONV_WIDTH // 2)],
                                 dimension_numbers=('NWC', 'WIO', 'NWC'),
                                 feature_group_count=CONV_CH) + conv_b
    u = jax.nn.silu(layer_norm(u, conv_norm_g, conv_norm_b))
    out = jnp.concatenate([o, u.astype(o.dtype)], axis=-1) @ w_out
    return out, s_f, s_b

def axial_rope_tables(t_len):
    t = jnp.arange(t_len)
    row = (t // GRID_W).astype(jnp.float32)
    col = (t % GRID_W).astype(jnp.float32)
    pairs_per_axis = ATT_HEAD_DIM // 4
    inv = ROPE_THETA ** (-jnp.arange(pairs_per_axis, dtype=jnp.float32) / pairs_per_axis)
    ang = jnp.concatenate([row[:, None] * inv, col[:, None] * inv], axis=-1)
    return jnp.cos(ang), jnp.sin(ang)

def apply_rope(x, cos, sin):
    xf = x.astype(jnp.float32).reshape(*x.shape[:-1], -1, 2)
    x0, x1 = xf[..., 0], xf[..., 1]
    out = jnp.stack([x0 * cos - x1 * sin, x0 * sin + x1 * cos], axis=-1).reshape(x.shape)
    return out.astype(x.dtype)

def attn_project(h, w_in, q_norm_g, k_norm_g):
    b_, t_, _ = h.shape
    q, k, v = jnp.split(h @ w_in, [ATT_HEADS * ATT_HEAD_DIM, (ATT_HEADS + ATT_KV_HEADS) * ATT_HEAD_DIM], axis=-1)
    q = rms_norm(q.reshape(b_, t_, ATT_HEADS, ATT_HEAD_DIM)) * q_norm_g
    k = rms_norm(k.reshape(b_, t_, ATT_KV_HEADS, ATT_HEAD_DIM)) * k_norm_g
    v = v.reshape(b_, t_, ATT_KV_HEADS, ATT_HEAD_DIM)
    return q.transpose(0, 2, 1, 3), k.transpose(0, 2, 1, 3), v.transpose(0, 2, 1, 3)

def block_attention(q, k, v):
    b_, hq, tq, hd = q.shape
    kvh = k.shape[1]
    g = hq // kvh
    nb = tq // ATT_BLOCK
    qb = q.reshape(b_, kvh, g, nb, ATT_BLOCK, hd).transpose(3, 0, 1, 2, 4, 5)
    scale = hd ** -0.5

    def one_block(qi):
        s = jnp.einsum('bkgqd,bksd->bkgqs', qi, k).astype(jnp.float32) * scale
        p = jax.nn.softmax(s, axis=-1).astype(v.dtype)
        return jnp.einsum('bkgqs,bksd->bkgqd', p, v)

    o = lax.map(one_block, qb)
    return o.transpose(1, 0, 4, 2, 3, 5).reshape(b_, tq, hq * hd)

def odd_mixer(h_lat, h_ctx, cos, sin, w_in, q_norm_g, k_norm_g, w_out, need_ctx):
    q_c, k_c, v_c = attn_project(h_ctx, w_in, q_norm_g, k_norm_g)
    q_l, k_l, v_l = attn_project(h_lat, w_in, q_norm_g, k_norm_g)
    q_l = apply_rope(q_l, cos, sin)
    k_l = apply_rope(k_l, cos, sin)
    k_all = jnp.concatenate([k_c, k_l], axis=2)
    v_all = jnp.concatenate([v_c, v_l], axis=2)
    o_lat = block_attention(q_l, k_all, v_all) @ w_out
    o_ctx = block_attention(q_c, k_c, v_c) @ w_out if need_ctx else None
    return o_lat, o_ctx

def hier_moe(x, w_group, b_group, w_router, b_router, w_gate, w_up, w_down):
    g_logits = (x @ w_group).astype(jnp.float32) + b_group
    g_prob = jax.nn.softmax(g_logits, axis=-1)
    _, g_idx = lax.top_k(g_logits, 1)
    p_group = jnp.take_along_axis(g_prob, g_idx, axis=-1)
    e_all = jnp.einsum('nd,dge->nge', x, w_router).astype(jnp.float32) + b_router
    e_logits = jnp.einsum('ng,nge->ne', jax.nn.one_hot(g_idx[:, 0], MOE_GROUPS, dtype=jnp.float32), e_all)
    e_prob = jax.nn.softmax(e_logits, axis=-1)
    top_p, top_i = lax.top_k(e_prob, MOE_TOP_K)
    weights = p_group * top_p / jnp.sum(top_p, axis=-1, keepdims=True)
    expert_id = g_idx * MOE_EXPERTS_PER_GROUP + top_i
    combine = jnp.einsum('nk,nke->ne', weights, jax.nn.one_hot(expert_id, MOE_EXPERTS, dtype=jnp.float32))
    combine = combine.astype(x.dtype)
    y = jnp.zeros_like(x)
    for e in range(MOE_EXPERTS):
        hdn = jax.nn.silu(x @ w_gate[e]) * (x @ w_up[e])
        y = y + combine[:, e:e + 1] * (hdn @ w_down[e])
    return y

def setup_inputs(seed: int = 0) -> dict:
    key = jax.random.key(seed)
    ks = iter(jax.random.split(key, 40))

    def nrm(shape, s):
        return jax.random.normal(next(ks), shape, jnp.float32) * s

    D = D_MODEL
    return {
        "x": nrm((BATCH, SEQ, D), 1.0),
        "c": nrm((BATCH, D), 1.0),
        "ctx": nrm((BATCH, CTX_LEN, D), 1.0),
        "c_ctx": nrm((D,), 1.0),
        "ada_w": nrm((DEPTH, D, 6 * D), 0.5 * D ** -0.5),
        "ada_b": nrm((DEPTH, 6 * D), 0.02),
        "even_w_in": nrm((N_EVEN, D, EVEN_IN), D ** -0.5),
        "even_dec_w_f": nrm((N_EVEN, GLA_RANK, GLA_HEADS * GLA_DK), GLA_RANK ** -0.5),
        "even_dec_b_f": nrm((N_EVEN, GLA_HEADS * GLA_DK), 0.1),
        "even_dec_w_b": nrm((N_EVEN, GLA_RANK, GLA_HEADS * GLA_DK), GLA_RANK ** -0.5),
        "even_dec_b_b": nrm((N_EVEN, GLA_HEADS * GLA_DK), 0.1),
        "even_gla_norm_g": 1.0 + nrm((N_EVEN, GLA_DV), 0.02),
        "even_conv_w": nrm((N_EVEN, CONV_WIDTH, 1, CONV_CH), CONV_WIDTH ** -0.5),
        "even_conv_b": nrm((N_EVEN, CONV_CH), 0.02),
        "even_conv_norm_g": 1.0 + nrm((N_EVEN, CONV_CH), 0.02),
        "even_conv_norm_b": nrm((N_EVEN, CONV_CH), 0.02),
        "even_w_out": nrm((N_EVEN, EVEN_MIX, D), EVEN_MIX ** -0.5),
        "odd_w_in": nrm((N_ODD, D, ODD_IN), D ** -0.5),
        "odd_q_norm_g": 1.0 + nrm((N_ODD, ATT_HEAD_DIM), 0.02),
        "odd_k_norm_g": 1.0 + nrm((N_ODD, ATT_HEAD_DIM), 0.02),
        "odd_w_out": nrm((N_ODD, ODD_MIX, D), ODD_MIX ** -0.5),
        "moe_w_group": nrm((DEPTH, D, MOE_GROUPS), D ** -0.5),
        "moe_b_group": nrm((DEPTH, MOE_GROUPS), 0.01),
        "moe_w_router": nrm((DEPTH, D, MOE_GROUPS, MOE_EXPERTS_PER_GROUP), D ** -0.5),
        "moe_b_router": nrm((DEPTH, MOE_GROUPS, MOE_EXPERTS_PER_GROUP), 0.01),
        "moe_w_gate": nrm((DEPTH, MOE_EXPERTS, D, MOE_HIDDEN), D ** -0.5),
        "moe_w_up": nrm((DEPTH, MOE_EXPERTS, D, MOE_HIDDEN), D ** -0.5),
        "moe_w_down": nrm((DEPTH, MOE_EXPERTS, MOE_HIDDEN, D), MOE_HIDDEN ** -0.5),
        "final_norm_g": 1.0 + nrm((D,), 0.02),
    }

def reference(x, c, ctx, c_ctx, ada_w, ada_b, even_w_in, even_dec_w_f, even_dec_b_f, even_dec_w_b,
              even_dec_b_b, even_gla_norm_g, even_conv_w, even_conv_b, even_conv_norm_g, even_conv_norm_b,
              even_w_out, odd_w_in, odd_q_norm_g, odd_k_norm_g, odd_w_out, moe_w_group, moe_b_group,
              moe_w_router, moe_b_router, moe_w_gate, moe_w_up, moe_w_down, final_norm_g):
    b_, t_len, d_ = x.shape
    c_len = ctx.shape[1]
    cos, sin = axial_rope_tables(t_len)
    silu_c = jax.nn.silu(c)
    silu_cc = jax.nn.silu(c_ctx)
    for l in range(DEPTH):
        last = l == DEPTH - 1
        i = l // 2
        mod = (silu_c @ ada_w[l] + ada_b[l])[:, None, :]
        sh1, sc1, g1, sh2, sc2, g2 = jnp.split(mod, 6, axis=-1)
        cmod = silu_cc @ ada_w[l] + ada_b[l]
        csh1, csc1, cg1, csh2, csc2, cg2 = jnp.split(cmod, 6, axis=-1)
        h_lat = modulate(x, sh1, sc1)
        h_ctx = modulate(ctx, csh1, csc1)
        if l % 2 == 0:
            params = (even_w_in[i], even_dec_w_f[i], even_dec_b_f[i], even_dec_w_b[i], even_dec_b_b[i],
                      even_gla_norm_g[i], even_conv_w[i], even_conv_b[i], even_conv_norm_g[i],
                      even_conv_norm_b[i], even_w_out[i])
            s_zero = jnp.zeros((b_, GLA_HEADS, GLA_DK, GLA_DV), jnp.float32)
            o_ctx, s_f, s_b = even_mixer(h_ctx, s_zero, s_zero, *params)
            o_lat, _, _ = even_mixer(h_lat, s_f, s_b, *params)
        else:
            o_lat, o_ctx = odd_mixer(h_lat, h_ctx, cos, sin, odd_w_in[i], odd_q_norm_g[i],
                                     odd_k_norm_g[i], odd_w_out[i], not last)
        x = x + g1 * o_lat
        moe_params = (moe_w_group[l], moe_b_group[l], moe_w_router[l], moe_b_router[l],
                      moe_w_gate[l], moe_w_up[l], moe_w_down[l])
        if last:
            y = hier_moe(modulate(x, sh2, sc2).reshape(-1, d_), *moe_params)
            x = x + g2 * y.reshape(b_, t_len, d_)
        else:
            ctx = ctx + cg1 * o_ctx
            tokens = jnp.concatenate([modulate(x, sh2, sc2).reshape(-1, d_),
                                      modulate(ctx, csh2, csc2).reshape(-1, d_)], axis=0)
            y = hier_moe(tokens, *moe_params)
            n_lat = b_ * t_len
            x = x + g2 * y[:n_lat].reshape(b_, t_len, d_)
            ctx = ctx + cg2 * y[n_lat:].reshape(b_, c_len, d_)
    return rms_norm(x) * final_norm_g


_drawn_inputs = setup_inputs


def setup_inputs(seed=0):
    import zlib

    import numpy as np

    out = dict(_drawn_inputs(seed))
    spreads = {}
    factors = {'even_dec_b_f': 6.455,
     'even_dec_w_b': 2.841,
     'even_dec_b_b': 8.0,
     'even_gla_norm_g': 6.479,
     'even_conv_b': 8.0,
     'even_conv_norm_g': 8.0,
     'even_conv_norm_b': 7.544,
     'odd_q_norm_g': 22.813,
     'odd_k_norm_g': 23.188,
     'moe_b_group': 13.498,
     'moe_b_router': 29.609,
     'final_norm_g': 2.736}
    for name, (base, spread) in spreads.items():
        noise = np.random.default_rng([zlib.crc32(name.encode()), seed]).standard_normal(out[name].shape)
        drawn = base * np.exp(spread * noise) if base else spread * noise
        out[name] = __import__('jax').numpy.asarray(drawn.astype(out[name].dtype))
    for name, factor in factors.items():
        out[name] = (out[name] * factor).astype(out[name].dtype)
    return out
```

```python
from contextlib import ExitStack

import numpy as np
import concourse.bass as bass
from concourse import mybir

ALU = mybir.AluOpType
ACT = mybir.ActivationFunctionType
F32 = mybir.dt.float32
I32 = mybir.dt.int32
U32 = mybir.dt.uint32
AX_X = mybir.AxisListType.X

P = 128
D = 1024
KC = D // P
NT = 4
NLAT = 2
H_GLA, DK, DV = 4, 64, 128
CHUNK = 64
NCH = NT * P // CHUNK
RANK = 16
CONV_CH, TAPS = 512, 31
HALO = TAPS // 2
SEG = 256 + 2 * HALO
NPT = CONV_CH // P
HEADS, KV, HD = 8, 2, 128
NEXP, EPG = 16, 4
HID = 512
HC = HID // P
CAP = (128, 64)
MAXOV = 7
assert all(2 * n * P // cap - 1 == MAXOV for n, cap in zip((NT, NLAT), CAP))
NTL = NEXP + MAXOV + 1
EPS = 1e-6
SLOTS = 6
BW = KC * 512
GRID_W = 64

C_ID, C_LO, C_UP, C_ONE, C_TRI, C_COS, C_SIN = 0, 128, 256, 384, 512, 640, 768
C_EPS, C_W4, C_E, C_OVI, C_TOK, C_SEL = 896, 897, 901, 917, 933, 937
C_END = 939

A_Q, A_K, A_V, A_R, A_U, A_MIX = 0, 1024, 2048, 4096, 6144, 6144 + NPT * 2 * SEG
A_END = A_MIX + 4096
M_H2, M_XG, M_XT, M_HID, M_HT, M_Y, M_SM = 0, 2048, 4096, 6144, 7168, 8192, 10240
O_Q, O_KV, O_QT, O_KT, O_P, O_PT, O_O = 0, 2048, 4096, 6144, 7168, 8192, 10240


def constant_table():
    t = np.zeros((P, C_END), np.float32)
    r = np.arange(P)
    same = (r[:, None] // CHUNK) == (r[None, :] // CHUNK)
    t[:, C_ID:C_ID + P] = np.eye(P)
    t[:, C_LO:C_LO + P] = same & (r[:, None] <= r[None, :])
    t[:, C_UP:C_UP + P] = same & (r[:, None] >= r[None, :])
    t[:, C_ONE:C_ONE + P] = 1.0
    t[:, C_TRI:C_TRI + P] = r[:, None] < r[None, :]
    for r2 in range(2):
        t[r2::32, C_SEL + r2] = 1.0
    tok = np.arange(NLAT * P)
    pairs = HD // 4
    inv = (np.float32(10000.0) ** (-np.arange(pairs, dtype=np.float32) / np.float32(pairs))).astype(np.float32)
    ang = np.concatenate([(tok // GRID_W).astype(np.float32)[:, None] * inv,
                          (tok % GRID_W).astype(np.float32)[:, None] * inv], axis=-1)
    for j in range(NLAT):
        t[:, C_COS + 64 * j:C_COS + 64 * j + 64] = np.cos(ang[j * P:(j + 1) * P])
        t[:, C_SIN + 64 * j:C_SIN + 64 * j + 64] = np.sin(ang[j * P:(j + 1) * P])
    t[:, C_EPS] = EPS
    t[:, C_W4:C_W4 + 4] = [4, 3, 2, 1]
    t[:, C_E:C_E + NEXP] = np.arange(NEXP)
    t[:, C_OVI:C_OVI + 16] = np.arange(16)
    t[:, C_TOK:C_TOK + NT] = (r[:, None] + P * np.arange(NT)[None, :]).astype(np.int32).view(np.float32)
    return t


def weight_stream():
    out = [("ada", 0, n) for n in range(12)]
    out += [("ein", 0, n) for n in ("cg", "ca", "qk", "v", "r")]
    out += [("eout", 0, 0), ("eout", 0, 1)]
    for l in range(2):
        if l == 0:
            out += [("ada", 1, n) for n in range(12)]
        out += [("g", l, 0), ("u", l, 0)]
        for e in range(1, NEXP):
            out += [("g", l, e), ("u", l, e), ("d", l, e - 1)]
        out += [("d", l, NEXP - 1)]
        if l == 0:
            out += [("oin", 0, 2), ("oin", 0, 0), ("oin", 0, 1), ("oout", 0, 0), ("oout", 0, 1)]
    return out


def hybrid_dit(nc, A, out):
    stream = weight_stream()
    at = {b: i for i, b in enumerate(stream)}
    ctx = ExitStack()
    with ctx:
        def sb(name, shape, dt=F32):
            return ctx.enter_context(nc.sbuf_tensor(name, shape, dt))

        sems = {}

        def sem(name):
            if name not in sems:
                sems[name] = ctx.enter_context(nc.semaphore(name))
            return sems[name]

        ring = sb("ring", [P, SLOTS, BW])
        x = sb("x", [P, NT, D])
        hT = sb("hT", [P, KC, 512])
        gb = sb("gb", [P, 4, D])
        mla = sb("mla", [P, 2048])
        ar = sb("ar", [P, A_END])
        cst = sb("cst", [P, C_END])
        modT = sb("modT", [P, 2, 4, KC, 2])
        cpar = sb("cpar", [P, NPT, 35])
        c_cols = sb("c_cols", [P, 2, KC])
        silu_c = sb("silu_c", [P, KC, 32])
        bias_cols = sb("bias_cols", [P, 2, 4, KC])
        ss = sb("ss", [P, 16])
        rstd = sb("rstd", [P, 16])
        lastS = sb("lastS", [P, 2, NCH])
        dec = sb("dec", [P, 2, NCH])
        sm = sb("sm", [P, 96])
        ps = ctx.enter_context(nc.psum_tensor("ps", [P, 8, 512], F32))

        slot_list = [nc.dram_tensor(f"slot_list{l}", (P * NTL, 1), I32, kind="Internal").ap() for l in range(2)]
        h2_rows = nc.dram_tensor("h2_rows", (NT * P, D), F32, kind="Internal").ap()
        y_rows = nc.dram_tensor("y_rows", ((NEXP + MAXOV) * P, D), F32, kind="Internal").ap()

        ident = cst[:, C_ID:C_ID + P]
        ones = cst[:, C_ONE:C_ONE + P]
        eps = cst[:, C_EPS:C_EPS + 1]
        modrow = mla[:, :].rearrange("r (b n) -> r b n", b=2)
        bias_row = hT[0:1, 0:4, :].rearrange("p (s h) n -> p s (h n)", s=2)
        la = mla[:, :].rearrange("p (j n) -> p j n", j=NT)

        def view(o, *dims):
            n = int(np.prod(dims))
            v = ar[:, o:o + n]
            if len(dims) == 2:
                v = v.rearrange("p (a b) -> p a b", a=dims[0])
            if len(dims) == 3:
                v = v.rearrange("p (a b c) -> p a b c", a=dims[0], b=dims[1])
            return v

        qT, kT = view(A_Q, 2, 512), view(A_K, 2, 512)
        v_tok, rT = view(A_V, NT, 512), view(A_R, 4, 512)
        xn = view(A_R, 2, D)
        u_in = view(A_U, NPT, 2, SEG)
        mix = view(A_MIX, 8, 512)
        z_all = ar[0:33, A_MIX:A_MIX + 512]
        dec_w = ar[0:33, A_MIX + 512:A_MIX + 1024]
        w_z = view(A_MIX + 1024, KC, 32)
        par_rows = ar[0:35, A_MIX + 1536:A_MIX + 2048]
        sq4 = view(A_U, 4, 512)
        states = view(A_U, 2, 7, P)
        hflat = hT[:, :, :].rearrange("p a b -> p (a b)")
        q_t = hflat[:, 0:1024].rearrange("p (d n) -> p d n", d=2)
        k_t = hflat[:, 1024:2048].rearrange("p (d n) -> p d n", d=2)
        k_e = hflat[:, 2048:3072].rearrange("p (d n) -> p d n", d=2)
        k_etok = hflat[:, 3072:4096].rearrange("p (d j n) -> p d j n", d=2, j=NT)
        res = hflat[:, 0:1024].rearrange("p (b n) -> p b n", b=2)
        h2s, xg, xgT = view(M_H2, 2, D), view(M_XG, 2, D), view(M_XT, 2, KC, P)
        hid, hidT, yb = view(M_HID, 2, HID), view(M_HT, 2, HC, P), view(M_Y, 2, D)
        yg = hflat.rearrange("p (b k n) -> p b k n", b=2, k=2)
        q_tok, kv_tok = view(O_Q, 2, D), view(O_KV, NT, 512)
        qhT, khT = view(O_QT, HEADS, 256), view(O_KT, KV, 512)
        prob, probT = view(O_P, 2, 512), view(O_PT, 2, NT, 256)
        ohT = view(O_O, HEADS, 256)
        rt = view(O_PT, 4, 512)

        moff = [M_SM]

        def small(n):
            o = moff[0]
            moff[0] += n
            assert moff[0] <= A_END
            return ar[:, o:o + n]

        w_rt = small(KC * 20)
        r_bias = small(20)
        lg = small(NT * 20)
        R = {k: small(NT * n) for k, n in dict(
            gm=1, ge=4, gx=4, gs=1, pg=1, eq=4, sc=4, mx=1, ohg=4, el=4, m1=1, oh1=4, e2=4, m2=1,
            oh2=4, dd=1, ex=1, dn=1, rd=1, rk=16, kk=16, k0=16, sl=16, tl=16, pa=16,
            f1=1, f2=1, f3=1, f4=1, M1=16, M2=16, MM=16, tmp=16).items()}
        cnt, nov, inc, inc2, exc, adj = (small(NEXP) for _ in range(6))
        te_t = small(NTL * 16)
        w1, w2 = sm[:, 0:4], sm[:, 4:8]
        posl = sm[:, 8:16].bitcast(I32)
        posy = sm[:, 16:24].bitcast(I32)
        idx = sm[:, 24:24 + NTL].bitcast(I32)
        idxc = sm[:, 24 + NTL:26 + NTL].bitcast(I32)
        ov_n = sm[0:1, 52:53].bitcast(I32)
        ov_e = sm[0:1, 53:53 + MAXOV].bitcast(I32)
        zero_i = sm[:, 64:64 + NTL].bitcast(I32)
        assert 26 + NTL <= 52 and 53 + MAXOV <= 64

        block = ctx.enter_context(nc.Block())

        def arrived(eng, i):
            eng.wait_ge(sem(f"block_in{i % SLOTS}"), 16 * (i // SLOTS + 1))

        def blk(i):
            return ring[:, i % SLOTS, :].rearrange("p (c n) -> p c n", c=KC)

        UNITS = [(k, n) for k, c in (("cg", 4), ("ca", 4), ("qk", 4), ("z", 1), ("v", 4), ("r", 4)) for n in range(c)]
        OUNITS = [("kv", j) for j in range(NT)] + [(k, j) for k in ("q0", "q1") for j in range(NLAT)]
        N_SMALL = 10
        SEQ = ([4, 5, 6, 7, 0, 1, 2, 3], [7, 6, 5, 4, 3, 2, 1, 0])

        def taken_count(u):
            eng = "dve" if UNITS[u][0] == "ca" else "act"
            return eng, sum(1 for v in UNITS[:u + 1] if (v[0] == "ca") == (eng == "dve"))

        def wait_proj(eng, u):
            kind, n = UNITS[u]
            if n == 3:
                eng.wait_ge(sem("block_used"), at["ein", 0, kind] + 1)
            else:
                eng.wait_ge(sem("proj"), sum(1 for v in UNITS[:u + 1] if v[1] != 3))

        def oproj_last(u):
            return u + 1 == len(OUNITS) or OUNITS[u + 1][0] != OUNITS[u][0]

        def wait_oproj(eng, u):
            if oproj_last(u):
                eng.wait_ge(sem("block_used"), at["oin", 0, {"kv": 2, "q0": 0, "q1": 1}[OUNITS[u][0]]] + 1)
            else:
                eng.wait_ge(sem("oproj"), sum(1 for v in range(u + 1) if not oproj_last(v)))

        def wait_res(eng, l, u):
            n = NT if l == 0 else NLAT
            h, j = u // n, u % n
            if j == n - 1:
                eng.wait_ge(sem("block_used"), at["eout" if l == 0 else "oout", 0, h] + 1)
            else:
                eng.wait_ge(sem("res_ps"), (0 if l == 0 else 2 * (NT - 1)) + (n - 1) * h + j + 1)

        def wait_expert(eng, kind, l, e):
            if isinstance(e, int):
                if e < 0:
                    l, e = l - 1, e + NEXP
                if l < 0:
                    return
                eng.wait_ge(sem("block_used"), at[kind, l, e] + 1)
            else:
                eng.wait_ge(sem("block_used"), 3 * e + (at[kind, l, 2] - 5))

        OV_XT, OV_XGT, OV_GU, OV_SILU, OV_HID, OV_HT, OV_HIDT, OV_D, OV_Y = range(1, 10)
        OV_STEPS = OV_Y

        def xgt_copy(l, p, k):
            n = CAP[l]
            return (xgT[:, p, 4 * k:4 * k + 4, 0:n],
                    ps[:, 3 + k, 0:4 * n].rearrange("p (c n) -> p c n", c=4))

        def hid_width(l):
            return HID if l == 0 else HID // 2

        def y_copy(l, p, k):
            if l == 0:
                return yb[:, p, 512 * k:512 * k + 512], ps[:, 5 + k, :]
            return yb[64 * k:64 * k + 64, p, 0:512], ps[64 * k:64 * k + 64, 5 + k, :]

        def store_y(l, tile, p, done):
            if l == 0:
                nc.scalar.dma_start(y_rows.rearrange("(t s) n -> t s n", s=P)[tile, :, :], yb[:, p, :]).then_inc(done, 16)
            else:
                for h in range(2):
                    nc.scalar.dma_start(y_rows.rearrange("(t s) n -> t s n", s=64)[tile, :, h * 512:(h + 1) * 512],
                                        yb[64 * h:64 * h + 64, p, 0:512]).then_inc(done, 16)

        def y_free(eng, l, e, p):
            if not (isinstance(e, int) and e < 2 and l == 0):
                eng.wait_ge(sem(f"y_stored{p}"), (8 * e - 8 * p) if l == 0 else 128 + 16 * e - 16 * p)

        def gate_unit(l, s, r, h):
            return (4 * (s // 3) + 2 * r + h) if l == 0 else 8 + 2 * (s // 3) + h

        def gate_slot(l, s, r):
            return (2 * (s // 3) + r) if l == 0 else s // 3

        def xn_of(k):
            return view(O_O, 2, D) if k == 2 else xn

        NORM = {(0, 0): (0, NT), (0, 1): (1, NT), (1, 0): (2, NT), (1, 1): (3, NLAT)}
        MS = {0: 1, 1: 2, 2: 3, 3: 7}
        NBASE = {0: 0, 1: NT, 2: 2 * NT, 3: 3 * NT}

        @block.sync
        def _(sp):
            def src(b):
                kind, l, n = b
                if kind == "ada":
                    return A["ada_w"][l, :, n * 512:(n + 1) * 512].rearrange("(p c) n -> p c n", c=KC)
                if kind == "ein":
                    o = {"qk": 0, "v": 512, "r": 1024, "ca": 1568, "cg": 2080}[n]
                    return A["even_w_in"][0, :, o:o + 512].rearrange("(p c) n -> p c n", c=KC)
                if kind in ("eout", "oout"):
                    w = A["even_w_out" if kind == "eout" else "odd_w_out"]
                    return w[0, :, n * 512:(n + 1) * 512].rearrange("(c p) n -> p c n", c=KC)
                if kind == "oin":
                    return A["odd_w_in"][0, :, n * 512:(n + 1) * 512].rearrange("(p c) n -> p c n", c=KC)
                raise ValueError(kind)

            def expert_src(kind, l, e):
                if kind == "d":
                    return A["moe_w_down"][l, e, :, :].rearrange("(p c) n -> p (c n)", c=HC)
                return A["moe_w_gate" if kind == "g" else "moe_w_up"][l, e, :, :].rearrange(
                    "(p c) n -> p (c n)", c=KC)

            def load(i, s, count=None, wide=False):
                if count is None:
                    count = i - SLOTS + 1
                    if count >= 1:
                        sp.wait_ge(sem("block_used"), count)
                else:
                    sp.wait_ge(sem("block_used"), count)
                dst = ring[:, i % SLOTS, :] if wide else blk(i)
                sp.dma_start(dst, s).then_inc(sem(f"block_in{i % SLOTS}"), 16)

            sp.dma_start(c_cols[:, 0, :], A["c"].rearrange("a (p c) -> p (a c)", c=KC)).then_inc(sem("c_in"), 16)
            sp.dma_start(c_cols[:, 1, :], A["c_ctx"].rearrange("(p c) -> p c", c=KC)).then_inc(sem("c_in"), 16)
            sp.dma_start(cst[:, :], A["consts"]).then_inc(sem("consts_in"), 16)

            def moe_stream(l):
                for b in [("g", l, 0), ("u", l, 0), ("g", l, 1), ("u", l, 1), ("d", l, 0)]:
                    load(at[b], expert_src(*b), wide=True)
                i0 = at[("g", l, 2)]
                with sp.Fori(0, NEXP // 2 - 1) as t:
                    for k, (kind, de) in enumerate([("g", 2), ("u", 2), ("d", 1), ("g", 3), ("u", 3), ("d", 2)]):
                        sp.wait_ge(sem("block_used"), i0 + k - SLOTS + 1 + SLOTS * t)
                        sp.dma_start(ring[:, (i0 + k) % SLOTS, :], expert_src(kind, l, 2 * t + de))\
                          .then_inc(sem(f"block_in{(i0 + k) % SLOTS}"), 16)
                load(at[("d", l, NEXP - 1)], expert_src("d", l, NEXP - 1), wide=True)

            def overflow_stream(l):
                i0 = at[("d", l, NEXP - 1)] + 1
                sp.wait_ge(sem("routed"), l + 1)
                n = sp.value_load(ov_n, min_val=0, max_val=MAXOV)
                with sp.If(n > 0):
                    sp.wait_ge(sem("block_used"), i0)
                    with sp.Fori(0, n) as t:
                        e = sp.value_load(ov_e[:, bass.ds(t, 1)], min_val=0, max_val=NEXP - 1)
                        for k, kind in enumerate("gud"):
                            sp.dma_start(ring[:, (i0 + k) % SLOTS, :], expert_src(kind, l, e))\
                              .then_inc(sem(f"ov_weights{l}"), 16)
                        sp.wait_ge(sem(f"ov_step{l}"), OV_STEPS * t + OV_D)
                        sp.sem_inc(sem("waits_passed"), 1)

            for b in stream[:at[("g", 0, 0)]]:
                load(at[b], src(b))
            moe_stream(0)
            overflow_stream(0)
            for b in stream[at[("d", 0, NEXP - 1)] + 1:at[("g", 1, 0)]]:
                load(at[b], src(b))
            moe_stream(1)
            overflow_stream(1)
            sp.wait_ge(sem("out_stored"), 16 * NLAT)

        @block.tensor
        def _(pe):
            def mm(o, l, r, start=True, stop=True):
                return nc.tensor.matmul(o, l, r, start=start, stop=stop)

            def ada(l):
                for s in range(6):
                    for h in range(2):
                        n = 2 * s + h
                        i = at[("ada", l, n)]
                        arrived(pe, i)
                        if 12 * l + n >= 2:
                            pe.wait_ge(sem("ada_added"), 12 * l + n - 1)
                        for c in range(KC):
                            g = c % 4
                            m = mm(ps[32 * g:32 * g + 32, n % 2, :], silu_c[:, c, :], blk(i)[:, c, :], c < 4, c >= 4)
                        m.then_inc(sem("block_used"), 1)
                    pe.wait_ge(sem("ada_added"), 12 * l + 2 * s + 2)
                    if s in (2, 5):
                        rows = (0, 1) if l == 0 else (0,)
                        for r in rows:
                            for h in range(2):
                                k = gate_unit(l, s, r, h)
                                if k >= 2:
                                    pe.wait_ge(sem("gate_taken"), k - 1)
                                if k in (0, 4, 8, 10):
                                    pe.wait_ge(sem("gate_bias_in"), 32 * (l + 1))
                                mm(ps[:, 3 + h, :], cst[:, C_SEL + r:C_SEL + r + 1].to_broadcast([P, P]),
                                   modrow[:, s % 2, h * 512:(h + 1) * 512], True, False)
                                m = mm(ps[:, 3 + h, :], cst[0:1, C_ONE:C_ONE + P],
                                       bias_row[:, s // 3, h * 512:(h + 1) * 512], False, True)
                                m.then_inc(sem("gate_rows"), 1)
                    else:
                        k = 4 * l + {0: 0, 1: 1, 3: 2, 4: 3}[s]
                        if k >= 1:
                            pe.wait_ge(sem("mod_taken"), k)
                        for c in range(KC):
                            m = mm(ps[:, 2, 2 * c:2 * c + 2], modrow[:, s % 2, c::KC], cst[:, C_SEL:C_SEL + 2])
                        m.then_inc(sem("mod_cols"), 1)

            def norm(l, w):
                k, n = NORM[l, w]
                for j in range(n):
                    q = NBASE[k] + j
                    pe.wait_ge(sem("xn_ready"), q + 1)
                    for h in range(2):
                        b = (2 * j + h) % 4
                        if q >= 2:
                            pe.wait_ge(sem("hT_act" if h == 0 else "hT_dve"), q - 1)
                        for cc in range(4):
                            m = nc.tensor.transpose(ps[:, b, cc * P:(cc + 1) * P], xn_of(k)[:, j % 2, 4 * h + cc::KC], ident)
                        m.then_inc(sem("xnT"), 1)
                pe.wait_ge(sem("hT_act"), NBASE[k] + n)
                pe.wait_ge(sem("hT_dve"), NBASE[k] + n)

            def even_in():
                for u, (kind, n) in enumerate(UNITS):
                    b = u % 4
                    if u >= 4:
                        eng, c = taken_count(u - 4)
                        pe.wait_ge(sem("proj_taken_" + eng), c)
                    if kind == "z":
                        pe.wait_ge(sem("small_in"), 16 * N_SMALL)
                        for c in range(KC):
                            m = mm(ps[0:32, b, :], w_z[:, c, :], hT[:, c, :], c == 0, c == KC - 1)
                        m.then_inc(sem("proj"), 1)
                        continue
                    i = at[("ein", 0, kind)]
                    if n == 0:
                        arrived(pe, i)
                    for c in range(KC):
                        if kind == "v":
                            m = mm(ps[:, b, :], hT[:, c, n * P:(n + 1) * P], blk(i)[:, c, :], c == 0, c == KC - 1)
                        else:
                            m = mm(ps[:, b, :], blk(i)[:, c, n * P:(n + 1) * P], hT[:, c, :], c == 0, c == KC - 1)
                    m.then_inc(sem("block_used" if n == 3 else "proj"), 1)
                    if (kind, n) == ("v", 3):
                        pe.wait_ge(sem("z_ready"), 2)
                        for j in range(NT):
                            m = mm(ps[:, 4 + j, :], z_all[:, j * P:(j + 1) * P], dec_w)
                            m.then_inc(sem("gate_lin"), 1)

            def conv_norm():
                eng, c = taken_count(len(UNITS) - 1)
                pe.wait_ge(sem("proj_taken_" + eng), c)
                pe.wait_ge(sem("conv_done"), NPT * TAPS)
                for i in range(NPT):
                    m = mm(ps[:, 0, :], ones, mix[:, 4 + i, :], i == 0, i == NPT - 1)
                m.then_inc(sem("cn_sum"), 1)
                pe.wait_ge(sem("cn_sq"), NPT)
                for i in range(NPT):
                    m = mm(ps[:, 1, :], ones, sq4[:, i, :], i == 0, i == NPT - 1)
                m.then_inc(sem("cn_sum"), 1)

            def gla():
                pe.wait_ge(sem("la_ready"), NT)
                for pt in range(2):
                    for d in range(2):
                        for j in range(NT):
                            m = mm(ps[:, 4 + 2 * pt + d, j * P:(j + 1) * P],
                                   la[:, j, d * 256 + pt * P:d * 256 + pt * P + P],
                                   cst[:, (C_LO, C_UP)[d]:(C_LO, C_UP)[d] + P])
                        m.then_inc(sem("cum"), 1)
                pe.wait_ge(sem("cn_scaled"), NPT)
                for pt in range(2):
                    if pt:
                        pe.wait_ge(sem("o_taken"), 2)
                    for d in range(2):
                        pe.wait_ge(sem("ke_ready"), 2 * pt + d + 1)
                        for j in range(NT):
                            m = nc.tensor.transpose(ps[:, 2 + d, j * P:(j + 1) * P], k_e[:, d, j * P:(j + 1) * P], ident)
                        m.then_inc(sem("keT"), 1)
                    if pt:
                        pe.wait_ge(sem("att_masked"), 4)
                    for d in range(2):
                        pe.wait_ge(sem("ketok_ready"), 2 * pt + (1 if d == 0 else 2))
                        for n in range(NCH):
                            lo = CHUNK * (n % 2)
                            for hh in range(2):
                                m = mm(ps[64 * hh:64 * hh + 64, 2 * d + n % 2, (n // 2) * P:(n // 2 + 1) * P],
                                       k_etok[lo:lo + 64, d, n // 2, 64 * hh:64 * hh + 64],
                                       v_tok[lo:lo + 64, n // 2, (2 * pt + hh) * P:(2 * pt + hh + 1) * P])
                        m.then_inc(sem("kv_sum"), 1)
                    pe.wait_ge(sem("state"), 14 * (pt + 1))
                    pe.wait_ge(sem("qk_ready"), 4 * (pt + 1))
                    for hh in range(2):
                        lo = 64 * hh
                        if hh:
                            pe.wait_ge(sem("att_masked"), 4 * pt + 2)
                        for d in range(2):
                            for j in range(NT):
                                m = mm(ps[:, d, j * P:(j + 1) * P], k_t[lo:lo + 64, d, j * P:(j + 1) * P],
                                       q_t[lo:lo + 64, d, j * P:(j + 1) * P])
                            m.then_inc(sem("att"), 1)
                        pe.wait_ge(sem("att_masked"), 4 * pt + 2 * hh + 2)
                        for j in range(NT):
                            todo = [(ps[:, 2 + hh, j * P:(j + 1) * P], v_tok[:, j, (2 * pt + hh) * P:(2 * pt + hh + 1) * P],
                                     k_e[:, d, j * P:(j + 1) * P]) for d in range(2)]
                            for d in range(2):
                                for n in (2 * j, 2 * j + 1):
                                    k = SEQ[d].index(n)
                                    if k:
                                        todo.append((ps[:, 2 + hh, n * CHUNK:(n + 1) * CHUNK],
                                                     states[lo:lo + 64, d, k - 1, :],
                                                     q_t[lo:lo + 64, d, n * CHUNK:(n + 1) * CHUNK]))
                            for k, (o, l, r) in enumerate(todo):
                                m = nc.tensor.matmul(o, l, r, start=(k == 0), stop=(k == len(todo) - 1),
                                                     skip_group_check=True)
                        m.then_inc(sem("o_sum"), 1)
                    for hh in range(2):
                        pe.wait_ge(sem("o_sq"), 2 * pt + hh + 1)
                        m = mm(ps[:, 4 + 2 * pt + hh, :], ones, (qT if hh == 0 else kT)[:, pt, :])
                        m.then_inc(sem("o_sumsq"), 1)

            def out_proj(l, blocks, operand, n_tiles, base):
                for h in range(2):
                    i = blocks[h]
                    arrived(pe, i)
                    for j in range(n_tiles):
                        u = n_tiles * h + j
                        if u >= 4:
                            pe.wait_ge(sem("res_taken"), base + u - 3)
                        for c in range(KC):
                            m = mm(ps[:, u % 4, :], operand(c, j), blk(i)[:, c, :], c == 0, c == KC - 1)
                        m.then_inc(sem("block_used" if j == n_tiles - 1 else "res_ps"), 1)

            def rows_and_router(l):
                k, n = NORM[l, 1]
                for j in range(n):
                    for h in range(2):
                        b = 4 + (2 * j + h) % 4
                        q = NT * l + j
                        if j >= 2:
                            pe.wait_ge(sem("h2_act" if h == 0 else "h2_dve"), q - 1)
                        for cc in range(4):
                            m = nc.tensor.transpose(ps[:, b, cc * P:(cc + 1) * P],
                                                    hT[:, 4 * h + cc, j * P:(j + 1) * P], ident)
                        m.then_inc(sem("h2_ps"), 1)
                pe.wait_ge(sem("router_in"), 64 * (l + 1))
                for j in range(n):
                    for c in range(KC):
                        m = mm(ps[:, 0, 32 * j:32 * j + 20], hT[:, c, j * P:(j + 1) * P],
                               w_rt[:, 20 * c:20 * c + 20], c == 0, c == KC - 1)
                m.then_inc(sem("logits"), 1)
                pe.wait_ge(sem("chosen"), l + 1)
                M = R["MM"]
                for j in range(n):
                    for jj in range(j):
                        mm(ps[:, 1, 16 * j:16 * j + 16], ones, M[:, 16 * jj:16 * jj + 16], jj == 0, False)
                    mm(ps[:, 1, 16 * j:16 * j + 16], cst[:, C_TRI:C_TRI + P], M[:, 16 * j:16 * j + 16], j == 0, True)
                for j in range(n):
                    m = mm(ps[:, 1, 64:80], ones, M[:, 16 * j:16 * j + 16], j == 0, j == n - 1)
                m.then_inc(sem("ranks"), 1)

            def do_xt(l, p):
                n = CAP[l]
                for c in range(KC):
                    m = nc.tensor.transpose(ps[:, 3 + c // 4, (c % 4) * n:(c % 4 + 1) * n], xg[0:n, p, c * P:(c + 1) * P],
                                            ident[0:n, 0:n])
                return m

            def do_product(l, p, bank, w):
                for c in range(KC):
                    if l == 0:
                        m = mm(ps[:, bank, :], xgT[:, p, c, :], w[:, c, :], c == 0, c == KC - 1)
                        continue
                    wv = w[:, c, :].rearrange("p (i k) -> p i k", k=4)
                    for g in range(2):
                        m = mm(ps[64 * g:64 * g + 64, bank, 0:256], xgT[:, p, c, 0:64], wv[:, :, 2 * g:2 * g + 2],
                               c == 0, c == KC - 1)
                return m

            def do_hidden_t(l, p):
                if l == 0:
                    for c in range(HC):
                        m = nc.tensor.transpose(ps[:, 2, c * P:(c + 1) * P], hid[:, p, c::HC], ident)
                else:
                    for c in range(2):
                        m = nc.tensor.transpose(ps[:, 2, c * P:(c + 1) * P], hid[:, p, c:256:2], ident)
                return m

            def do_down(l, p, w):
                if l == 0:
                    for h in range(2):
                        for c in range(HC):
                            m = mm(ps[:, 5 + h, :], hidT[:, p, c, :], w[:, c, h * 512:(h + 1) * 512], c == 0, c == HC - 1)
                    return m
                for c in range(HC):
                    for h in range(2):
                        m = mm(ps[64 * h:64 * h + 64, 5 + h, :], hidT[:, p, c % 2, 64 * (c // 2):64 * (c // 2) + 64],
                               w[:, c, h * 512:(h + 1) * 512], c == 0, c == HC - 1)
                return m

            def xt(l, e, p):
                pe.wait_ge(sem(f"xg_in{p}"), 16 * (8 * l + 1) + 8 * (e - p))
                if not (isinstance(e, int) and e == 0 and l == 0):
                    pe.wait_ge(sem("xgT_act"), NEXP * l + e)
                    pe.wait_ge(sem("xgT_dve"), NEXP * l + e)
                if l == 1:
                    pe.sem_inc(sem("waits_passed"), 1)
                do_xt(l, p).then_inc(sem("xgT_ps"), 1)

            def gate_up(l, e, p, i, t, up):
                pe.wait_ge(sem(f"block_in{i % SLOTS}"), 16 * (i // SLOTS + 1) + 16 * t)
                if not up:
                    pe.wait_ge(sem("xgT_act"), NEXP * l + e + 1)
                    pe.wait_ge(sem("xgT_dve"), NEXP * l + e + 1)
                if not (isinstance(e, int) and e == 0 and l == 0):
                    pe.wait_ge(sem("hid_ready" if up else "silu_done"), NEXP * l + e)
                do_product(l, p, 1 if up else 0, blk(i)).then_inc(sem("block_used"), 1)

            def hidden_t(l, e, p):
                pe.wait_ge(sem("hid_ready"), NEXP * l + e + 1)
                if not (isinstance(e, int) and e == 0 and l == 0):
                    pe.wait_ge(sem("hidT_ready"), NEXP * l + e)
                do_hidden_t(l, p).then_inc(sem("hidT_ps"), 1)

            def down(l, e, p, i, t):
                pe.wait_ge(sem(f"block_in{i % SLOTS}"), 16 * (i // SLOTS + 1) + 16 * t)
                pe.wait_ge(sem("hidT_ready"), NEXP * l + e + 1)
                if not (isinstance(e, int) and e == 0 and l == 0):
                    pe.wait_ge(sem("y_act"), NEXP * l + e)
                    pe.wait_ge(sem("y_dve"), NEXP * l + e)
                wd = ring[:, i % SLOTS, :].rearrange("p (c n) -> p c n", c=HC)
                do_down(l, p, wd).then_inc(sem("block_used"), 1)

            def experts(l):
                xt(l, 0, 0)
                gate_up(l, 0, 0, at["g", l, 0], 0, False)
                gate_up(l, 0, 0, at["u", l, 0], 0, True)
                xt(l, 1, 1)

                def step(e, p, i, t, last=False):
                    gate_up(l, e, p, i, t, False)
                    hidden_t(l, e - 1, 1 - p)
                    gate_up(l, e, p, i + 1, t, True)
                    if not last:
                        xt(l, e + 1, 1 - p)
                    down(l, e - 1, 1 - p, i + 2, t)
                step(1, 1, at["g", l, 1], 0)
                with pe.Fori(0, NEXP // 2 - 2) as t:
                    step(2 * t + 2, 0, at["g", l, 2], t)
                    step(2 * t + 3, 1, at["g", l, 3], t)
                step(NEXP - 2, 0, at["g", l, NEXP - 2], 0)
                step(NEXP - 1, 1, at["g", l, NEXP - 1], 0, last=True)
                hidden_t(l, NEXP - 1, 1)
                down(l, NEXP - 1, 1, at["d", l, NEXP - 1], 0)

            def overflow(l):
                i0 = at[("d", l, NEXP - 1)] + 1
                n = pe.value_load(ov_n, min_val=0, max_val=MAXOV)
                with pe.If(n > 0):
                    with pe.Fori(0, n) as t:
                        pe.wait_ge(sem(f"ov_xg{l}"), 16 * t + 16)
                        if l == 1:
                            pe.sem_inc(sem("waits_passed"), 1)
                        do_xt(l, 0).then_inc(sem(f"ov_step{l}"), 1)
                        pe.wait_ge(sem(f"ov_step{l}"), OV_STEPS * t + OV_XGT)
                        pe.wait_ge(sem(f"ov_weights{l}"), 48 * t + 48)
                        do_product(l, 0, 0, blk(i0))
                        do_product(l, 0, 1, blk(i0 + 1)).then_inc(sem(f"ov_step{l}"), 1)
                        pe.wait_ge(sem(f"ov_step{l}"), OV_STEPS * t + OV_HID)
                        do_hidden_t(l, 0).then_inc(sem(f"ov_step{l}"), 1)
                        pe.wait_ge(sem(f"ov_step{l}"), OV_STEPS * t + OV_HIDT)
                        wd = ring[:, (i0 + 2) % SLOTS, :].rearrange("p (c n) -> p c n", c=HC)
                        do_down(l, 0, wd).then_inc(sem(f"ov_step{l}"), 1)

            def odd_mixer():
                i = at["oin", 0, 2]
                arrived(pe, i)
                for u, (kind, j) in enumerate(OUNITS):
                    i = at["oin", 0, {"kv": 2, "q0": 0, "q1": 1}[kind]]
                    if j == 0:
                        arrived(pe, i)
                    if u >= 4:
                        pe.wait_ge(sem("oproj_taken"), u - 3)
                    for c in range(KC):
                        m = mm(ps[:, u % 4, :], hT[:, c, j * P:(j + 1) * P], blk(i)[:, c, :], c == 0, c == KC - 1)
                    m.then_inc(sem("block_used" if oproj_last(u) else "oproj"), 1)
                pe.wait_ge(sem("k_rot"), 1)
                for kv in range(KV):
                    for j in range(NT):
                        m = nc.tensor.transpose(ps[:, 4 + kv, j * P:(j + 1) * P], kv_tok[:, j, kv * HD:(kv + 1) * HD], ident)
                    m.then_inc(sem("qkT_ps"), 1)
                for j in range(NLAT):
                    pe.wait_ge(sem("q_rot"), j + 1)
                    for h4 in range(2):
                        b = 6 + h4
                        if j:
                            pe.wait_ge(sem("qkT_taken"), KV + h4 + 1)
                        for hh in range(4):
                            h = 4 * h4 + hh
                            m = nc.tensor.transpose(ps[:, b, hh * P:(hh + 1) * P], q_tok[:, j, h * HD:(h + 1) * HD], ident)
                        m.then_inc(sem("qkT_ps"), 1)
                pe.wait_ge(sem("qkT_taken"), KV + 4)
                pe.wait_ge(sem("oproj_taken"), len(OUNITS))

                def score(u):
                    h, j = u // 2, u % 2
                    if u >= 3:
                        pe.wait_ge(sem("prob_exp"), u - 2)
                    mm(ps[:, u % 3, :], qhT[:, h, j * P:(j + 1) * P], khT[:, h // 4, :]).then_inc(sem("score_ps"), 1)

                for u in range(3):
                    score(u)
                for u in range(2 * HEADS):
                    h, j = u // 2, u % 2
                    pe.wait_ge(sem("prob_ready"), u + 1)
                    if u >= 2:
                        pe.wait_ge(sem("probT_taken"), u - 1)
                    for c in range(NT):
                        m = nc.tensor.transpose(ps[:, 3 + u % 2, c * P:(c + 1) * P], prob[:, u % 2, c * P:(c + 1) * P], ident)
                    m.then_inc(sem("probT_ps"), 1)
                    if u + 3 < 2 * HEADS:
                        score(u + 3)
                    if j == 1:
                        if h >= 1:
                            pv(h - 1)
                pv(HEADS - 1)

            def pv(h):
                pe.wait_ge(sem("probT_taken"), 2 * h + 2)
                if h >= 2:
                    pe.wait_ge(sem("oh_taken"), h - 1)
                for c in range(NT):
                    m = mm(ps[:, 5 + h % 2, 0:256], kv_tok[:, c, 256 + (h // 4) * HD:256 + (h // 4 + 1) * HD],
                           probT[:, h % 2, c, :], c == 0, c == NT - 1)
                m.then_inc(sem("oh_ps"), 1)

            pe.wait_ge(sem("silu_ready"), 1)
            pe.wait_ge(sem("consts_in"), 16)
            ada(0)
            pe.wait_ge(sem("small_in"), 16 * N_SMALL)
            pe.wait_ge(sem("gate_taken"), 8)
            for i in range(NPT):
                m = mm(ps[:, 4, 64 * i:64 * i + 35], par_rows[:, i * P:(i + 1) * P], cst[0:35, C_ID:C_ID + 35])
            m.then_inc(sem("par_ps"), 1)
            norm(0, 0)
            even_in()
            conv_norm()
            gla()
            pe.wait_ge(sem("mix_ready"), 4)
            pe.wait_ge(sem("conv_ready"), NPT)
            out_proj(0, [at["eout", 0, 0], at["eout", 0, 1]], lambda c, j: mix[:, c, j * P:(j + 1) * P], NT, 0)
            pe.wait_ge(sem("res_taken"), 2 * NT)
            norm(0, 1)
            rows_and_router(0)
            pe.wait_ge(sem("rank_taken"), 1)
            ada(1)
            pe.wait_ge(sem("gate_taken"), 12)
            pe.wait_ge(sem("mod_taken"), 8)
            experts(0)
            overflow(0)
            pe.wait_ge(sem("combined"), NT)
            norm(1, 0)
            odd_mixer()
            pe.wait_ge(sem("oh_taken"), HEADS)
            out_proj(1, [at["oout", 0, 0], at["oout", 0, 1]], lambda c, j: ohT[:, c, j * P:(j + 1) * P], NLAT, 2 * NT)
            pe.wait_ge(sem("res_taken"), 2 * NT + 2 * NLAT)
            norm(1, 1)
            rows_and_router(1)
            pe.wait_ge(sem("rank_taken"), 2)
            experts(1)
            overflow(1)

        @block.scalar
        def _(act):
            chain = [0]

            def link(ins):
                chain[0] += 1
                ins.then_inc(sem("act_chain"), 1)
                act.wait_ge(sem("act_chain"), chain[0])

            A_ = nc.scalar.activation

            def gates(l):
                for s in (2, 5):
                    for r in ((0, 1) if l == 0 else (0,)):
                        for h in range(2):
                            act.wait_ge(sem("gate_rows"), gate_unit(l, s, r, h) + 1)
                            A_(gb[:, gate_slot(l, s, r), h * 512:(h + 1) * 512], ps[:, 3 + h, :], ACT.Copy)\
                                .then_inc(sem("gate_taken"), 1)

            def squares(n, count, wait):
                for j in range(n):
                    wait(j)
                    if count + j >= 1:
                        act.wait_ge(sem("sq_done"), count + j)
                    A_(ps[:, 6:8, :].rearrange("p a b -> p (a b)"), x[:, j, :], ACT.Square, accum_out=ss[:, j:j + 1])\
                        .then_inc(sem("sq_done"), 1)

            def root(k):
                act.wait_ge(sem("ms_ready"), MS[k])
                A_(rstd[:, 0:NT], ss[:, 8:8 + NT], ACT.Sqrt).then_inc(sem("root_done"), 1)

            def norm(l, w, wait=lambda j: None):
                k, n = NORM[l, w]
                squares(n, NBASE[k], wait)
                root(k)
                for j in range(n):
                    q = NBASE[k] + j
                    act.wait_ge(sem("xnT"), 2 * q + 1)
                    for cc in range(4):
                        r = 0 if j < NLAT else 1
                        ins = A_(hT[:, cc, j * P:(j + 1) * P], ps[:, (2 * j) % 4, cc * P:(cc + 1) * P], ACT.Identity,
                                 bias=modT[:, l, 2 * w, cc, r:r + 1], scale=modT[:, l, 2 * w + 1, cc, r:r + 1])
                    ins.then_inc(sem("hT_act"), 1)

            def rows(l):
                k, n = NORM[l, 1]
                for j in range(n):
                    q = NT * l + j
                    act.wait_ge(sem("h2_ps"), 2 * q + 1)
                    if j >= 2:
                        act.wait_ge(sem(f"h2_stored{j % 2}"), 16 * (j // 2))
                    A_(h2s[:, j % 2, 0:512], ps[:, 4 + (2 * j) % 4, :], ACT.Copy).then_inc(sem("h2_act"), 1)
                    act.wait_ge(sem("h2_act"), q + 1)
                    act.wait_ge(sem("h2_dve"), q + 1)
                    act.dma_start(h2_rows[j * P:(j + 1) * P, :], h2s[:, j % 2, :])\
                       .then_inc(sem(f"h2_stored{j % 2}"), 16)

            def router(l):
                act.wait_ge(sem("g_shift"), l + 1)
                A_(R["gx"][:, 0:4 * NORM[l, 1][1]], R["ge"][:, 0:4 * NORM[l, 1][1]], ACT.Exp).then_inc(sem("g_exp"), 1)
                act.wait_ge(sem("e_shift"), l + 1)
                A_(R["ex"][:, 0:NORM[l, 1][1]], R["dd"][:, 0:NORM[l, 1][1]], ACT.Exp).then_inc(sem("e_exp"), 1)

            def xgt_half(l, e, p):
                act.wait_ge(sem("xgT_ps"), NEXP * l + e + 1)
                wait_expert(act, "u", l, e - 2)
                A_(*xgt_copy(l, p, 0), ACT.Copy).then_inc(sem("xgT_act"), 1)

            def silu(l, e, p):
                wait_expert(act, "g", l, e)
                if not (isinstance(e, int) and e < 2 and l == 0):
                    act.wait_ge(sem("hidT_ps"), NEXP * l + e - 1)
                A_(hid[:, p, 0:hid_width(l)], ps[:, 0, 0:hid_width(l)], ACT.Silu).then_inc(sem("silu_done"), 1)

            def y_half(l, e, p):
                wait_expert(act, "d", l, e)
                y_free(act, l, e, p)
                A_(*y_copy(l, p, 0), ACT.Copy).then_inc(sem("y_act"), 1)
                act.wait_ge(sem("y_act"), NEXP * l + e + 1)
                act.wait_ge(sem("y_dve"), NEXP * l + e + 1)
                store_y(l, e, p, sem(f"y_stored{p}"))

            def experts(l):
                xgt_half(l, 0, 0)
                silu(l, 0, 0)
                xgt_half(l, 1, 1)

                def step(e, p, last=False):
                    silu(l, e, p)
                    if not last:
                        xgt_half(l, e + 1, 1 - p)
                    y_half(l, e - 1, 1 - p)
                step(1, 1)
                with act.Fori(0, NEXP // 2 - 2) as t:
                    step(2 * t + 2, 0)
                    step(2 * t + 3, 1)
                step(NEXP - 2, 0)
                step(NEXP - 1, 1, last=True)
                y_half(l, NEXP - 1, 1)

            def overflow(l):
                n = act.value_load(ov_n, min_val=0, max_val=MAXOV)
                for p in range(2):
                    act.wait_ge(sem(f"y_stored{p}"), 128 if l == 0 else 128 + 256)
                with act.If(n > 0):
                    with act.Fori(0, n) as t:
                        act.wait_ge(sem(f"ov_step{l}"), OV_STEPS * t + OV_GU)
                        A_(hid[:, 0, 0:hid_width(l)], ps[:, 0, 0:hid_width(l)], ACT.Silu).then_inc(sem(f"ov_step{l}"), 1)
                        act.wait_ge(sem(f"ov_step{l}"), OV_STEPS * t + OV_Y)
                        store_y(l, t + NEXP, 0, sem(f"ov_stored{l}"))
                        act.wait_ge(sem(f"ov_stored{l}"), 16 * (l + 1) * t + 16 * (l + 1))
                act.sem_inc(sem("y_complete"), 1)

            def even_in():
                for u, (kind, n) in enumerate(UNITS):
                    if kind == "ca":
                        continue
                    wait_proj(act, u)
                    b = ps[:, u % 4, :]
                    if kind == "cg":
                        ins = A_(mix[:, 4 + n, :], b, ACT.Sigmoid)
                    elif kind == "qk":
                        ins = A_((qT if n < 2 else kT)[:, n % 2, :], b, ACT.Copy, scale=float(DK) ** -0.5 if n < 2 else 1.0)
                    elif kind == "z":
                        ins = A_(z_all[0:32, :], ps[0:32, u % 4, :], ACT.Copy)
                    elif kind == "v":
                        ins = A_(v_tok[:, n, :], b, ACT.Copy)
                    else:
                        ins = A_(rT[:, n, :], b, ACT.Silu)
                    ins.then_inc(sem("proj_taken_act"), 1)
                    if kind == "z":
                        act.wait_ge(sem("proj_taken_act"), taken_count(u)[1])
                        act.sem_inc(sem("z_ready"), 1)
                    if (kind, n) == ("v", 3):
                        for j in range(NT):
                            act.wait_ge(sem("gate_lin"), j + 1)
                            A_(la[:, j, :], ps[:, 4 + j, :], ACT.Abs).then_inc(sem("la_act"), 1)
                        for k, (f, s, bias) in enumerate(((ACT.Exp, -1.0, 0.0), (ACT.Ln, 1.0, 1.0))):
                            for j in range(NT):
                                act.wait_ge(sem("la_act"), NT * k + j + 1)
                                A_(la[:, j, :], la[:, j, :], f, scale=s, bias=cst[:, C_ONE:C_ONE + 1] if bias else 0.0)\
                                    .then_inc(sem("la_act"), 1)

            def conv_norm():
                for i in range(NPT):
                    act.wait_ge(sem("cn_centred"), i + 1)
                    A_(sq4[:, i, :], mix[:, 4 + i, :], ACT.Square).then_inc(sem("cn_sq"), 1)
                act.wait_ge(sem("cn_sum"), 2)
                A_(ps[:, 2, :], ps[:, 1, :], ACT.Sqrt, scale=1.0 / CONV_CH, bias=eps).then_inc(sem("cn_root"), 1)
                for i in range(NPT):
                    act.wait_ge(sem("cn_scaled"), i + 1)
                    A_(mix[:, 4 + i, :], mix[:, 4 + i, :], ACT.Silu, scale=cpar[:, i, 32:33], bias=cpar[:, i, 33:34])\
                        .then_inc(sem("conv_ready"), 1)

            def gla():
                for pt in range(2):
                    for d in range(2):
                        act.wait_ge(sem("cum"), 2 * pt + d + 1)
                        if pt:
                            act.wait_ge(sem("state"), 14)
                        cum = ps[:, 4 + 2 * pt + d, :]
                        end = cum.rearrange("p (n t) -> p n t", t=CHUNK)[:, :, CHUNK - 1 if d == 0 else 0]
                        A_(lastS[:, d, :], end, ACT.Copy).then_inc(sem("last_ready"), 1)
                        A_(dec[:, d, :], end, ACT.Exp, scale=1.0 / 16).then_inc(sem("dec_ready"), 1)
                    if pt:
                        act.wait_ge(sem("o_sum"), 2)
                    for d in range(2):
                        cum = ps[:, 4 + 2 * pt + d, :]
                        A_(q_t[:, d, :], cum, ACT.Exp, scale=1.0 / 16).then_inc(sem("qk_exp"), 1)
                        A_(k_t[:, d, :], cum, ACT.Exp, scale=-1.0 / 16).then_inc(sem("qk_exp"), 1)
                    for d in range(2):
                        act.wait_ge(sem("ke_diff"), 2 * pt + d + 1)
                        A_(k_e[:, d, :], k_e[:, d, :], ACT.Exp, scale=1.0 / 16).then_inc(sem("ke_exp"), 1)
                    for d in range(2):
                        act.wait_ge(sem("keT"), 2 * pt + d + 1)
                        A_(k_etok[:, d, :, :].rearrange("p j n -> p (j n)"), ps[:, 2 + d, :], ACT.Copy)\
                            .then_inc(sem("ketok_ready"), 1)
                    for hh in range(2):
                        h = 2 * pt + hh
                        act.wait_ge(sem("o_sum"), h + 1)
                        if h == 0:
                            act.wait_ge(sem("cum"), 4)
                        A_(mix[:, h, :], ps[:, 2 + hh, :], ACT.Copy).then_inc(sem("o_copied"), 1)
                        A_((qT if hh == 0 else kT)[:, pt, :], ps[:, 2 + hh, :], ACT.Square).then_inc(sem("o_sq"), 1)
                        act.wait_ge(sem("o_sq"), h + 1)
                        act.wait_ge(sem("o_copied"), h + 1)
                        act.sem_inc(sem("o_taken"), 1)
                for h in range(4):
                    act.wait_ge(sem("o_sumsq"), h + 1)
                    A_((qT if h % 2 == 0 else kT)[:, h // 2, :], ps[:, 4 + h, :], ACT.Sqrt, scale=1.0 / DV, bias=eps)\
                        .then_inc(sem("o_root"), 1)

            def odd_mixer():
                for u, (kind, j) in enumerate(OUNITS):
                    wait_oproj(act, u)
                    dst = kv_tok[:, j, :] if kind == "kv" else q_tok[:, j, (0 if kind == "q0" else 512):][:, 0:512]
                    A_(dst, ps[:, u % 4, :], ACT.Copy).then_inc(sem("oproj_taken"), 1)
                    if u == NT - 1:
                        act.wait_ge(sem("oproj_taken"), NT)
                        A_(rt[:, 0:2, :].rearrange("p a (b c) -> p (a b) c", c=256), kv_tok[:, :, 0:256], ACT.Square)\
                            .then_inc(sem("k_sq"), 1)
                        act.wait_ge(sem("ms_ready"), 4)
                        A_(rstd[:, 0:8], ss[:, 8:16], ACT.Sqrt).then_inc(sem("root_done"), 1)
                for j in range(NLAT):
                    act.wait_ge(sem("oproj_taken"), len(OUNITS))
                    act.wait_ge(sem("k_rot"), 1) if j == 0 else act.wait_ge(sem("q_rot"), 1)
                    A_(rt[:, 0:2, :].rearrange("p a b -> p (a b)"), q_tok[:, j, :], ACT.Square).then_inc(sem("q_sq"), 1)
                    act.wait_ge(sem("ms_ready"), 5 + j)
                    A_(rstd[:, 0:8], ss[:, 8:16], ACT.Sqrt).then_inc(sem("root_done"), 1)
                for kv in range(KV):
                    act.wait_ge(sem("qkT_ps"), kv + 1)
                    A_(khT[:, kv, :], ps[:, 4 + kv, :], ACT.Copy).then_inc(sem("qkT_taken"), 1)
                for j in range(NLAT):
                    for h4 in range(2):
                        act.wait_ge(sem("qkT_ps"), KV + 2 * j + h4 + 1)
                        A_(qhT[:, 4 * h4:4 * h4 + 4, j * P:(j + 1) * P],
                           ps[:, 6 + h4, :].rearrange("p (a b) -> p a b", a=4), ACT.Copy).then_inc(sem("qkT_taken"), 1)
                scale = float(HD) ** -0.5
                for u in range(2 * HEADS):
                    act.wait_ge(sem("neg_max"), u + 1)
                    if u >= 2:
                        act.wait_ge(sem("probT_ps"), u - 1)
                    A_(prob[:, u % 2, :], ps[:, u % 3, :], ACT.Exp, bias=ss[:, u % 4:u % 4 + 1], scale=scale,
                       accum_out=rstd[:, u % 4:u % 4 + 1]).then_inc(sem("prob_exp"), 1)
                    if u % 2 == 1 and u >= 3:
                        head_out((u - 3) // 2)
                head_out(HEADS - 1)

            def head_out(h):
                act.wait_ge(sem("oh_ps"), h + 1)
                A_(ohT[:, h, :], ps[:, 5 + h % 2, 0:256], ACT.Copy).then_inc(sem("oh_taken"), 1)

            for j in range(NT):
                src = A["x"] if j < NLAT else A["ctx"]
                act.dma_start(x[:, j, :], src[0, (j % 2) * P:(j % 2 + 1) * P, :]).then_inc(sem(f"x_in{j}"), 16)
            act.wait_ge(sem("c_in"), 32)
            act.wait_ge(sem("silu_zero"), 1)
            A_(silu_c[:, :, 0:2], c_cols[:, :, :].rearrange("p r c -> p c r"), ACT.Silu).then_inc(sem("silu_ready"), 1)
            gates(0)
            norm(0, 0, lambda j: act.wait_ge(sem(f"x_in{j}"), 16))
            even_in()
            conv_norm()
            gla()
            norm(0, 1, lambda j: act.wait_ge(sem("x_added"), 2 * NT))
            rows(0)
            router(0)
            gates(1)
            experts(0)
            overflow(0)
            norm(1, 0, lambda j: act.wait_ge(sem("combined"), j + 1))
            odd_mixer()
            norm(1, 1, lambda j: act.wait_ge(sem("x_added"), 2 * NT + 2 * NLAT))
            rows(1)
            router(1)
            experts(1)
            overflow(1)
            squares(NLAT, NBASE[3] + NLAT, lambda j: act.wait_ge(sem("combined"), NT + j + 1))
            act.wait_ge(sem("ms_ready"), 8)
            A_(rstd[:, 0:NT], ss[:, 8:8 + NT], ACT.Sqrt).then_inc(sem("root_done"), 1)
            for j in range(NLAT):
                act.wait_ge(sem("final_ready"), j + 1)
                act.dma_start(out[0, j * P:(j + 1) * P, :], x[:, j, :]).then_inc(sem("out_stored"), 16)

        @block.vector
        def _(dve):
            chain = [0]

            def link(ins):
                chain[0] += 1
                ins.then_inc(sem("dve_chain"), 1)
                dve.wait_ge(sem("dve_chain"), chain[0])

            V = nc.vector

            def ada(l):
                for s in range(6):
                    for h in range(2):
                        n = 2 * s + h
                        dve.wait_ge(sem("block_used"), at["ada", l, n] + 1)
                        if s >= 2 or l:
                            t, tl = (s - 2, l) if s >= 2 else (s + 4, l - 1)
                            if t in (2, 5):
                                dve.wait_ge(sem("gate_rows"), gate_unit(tl, t, 1 if tl == 0 else 0, 1) + 1)
                            else:
                                dve.wait_ge(sem("mod_cols"), 4 * tl + {0: 0, 1: 1, 3: 2, 4: 3}[t] + 1)
                        V.tensor_copy(modrow[:, s % 2, h * 512:(h + 1) * 512], ps[:, n % 2, :]).then_inc(sem("ada_added"), 1)
                    if s not in (2, 5):
                        k = {0: 0, 1: 1, 3: 2, 4: 3}[s]
                        dve.wait_ge(sem("mod_cols"), 4 * l + k + 1)
                        if k == 0:
                            dve.wait_ge(sem("bias_cols_in"), 16 * 8)
                        V.scalar_tensor_tensor(modT[:, l, k, :, :], ps[:, 2, 0:16].rearrange("p (c r) -> p c r", r=2),
                                               float(k % 2), bias_cols[:, l, k, :].unsqueeze(2).to_broadcast([P, KC, 2]),
                                               ALU.add, ALU.add).then_inc(sem("mod_taken"), 1)

            def mean_square(n, width, count):
                V.tensor_scalar(ss[:, 8:8 + n], ss[:, 0:n], 1.0 / width, EPS, ALU.mult, ALU.add)\
                    .then_inc(sem("ms_ready"), 1)
                dve.wait_ge(sem("root_done"), count)
                link(V.reciprocal(rstd[:, 0:n], rstd[:, 0:n]))

            def norm(l, w):
                k, n = NORM[l, w]
                dve.wait_ge(sem("sq_done"), NBASE[k] + n)
                mean_square(n, D, MS[k])

                def half(j):
                    q = NBASE[k] + j
                    r = 0 if j < NLAT else 1
                    dve.wait_ge(sem("xnT"), 2 * q + 2)
                    for cc in range(4):
                        ins = V.tensor_scalar(hT[:, 4 + cc, j * P:(j + 1) * P], ps[:, (2 * j + 1) % 4, cc * P:(cc + 1) * P],
                                              modT[:, l, 2 * w + 1, 4 + cc, r:r + 1], modT[:, l, 2 * w, 4 + cc, r:r + 1],
                                              ALU.mult, ALU.add)
                    ins.then_inc(sem("hT_dve"), 1)
                for j in range(n):
                    if j >= 2:
                        dve.wait_ge(sem("xnT"), 2 * (NBASE[k] + j) - 2)
                    V.tensor_scalar(xn_of(k)[:, j % 2, :], x[:, j, :], rstd[:, j:j + 1], None, ALU.mult)\
                        .then_inc(sem("xn_ready"), 1)
                    if j:
                        half(j - 1)
                half(n - 1)

            def rows(l):
                for j in range(NORM[l, 1][1]):
                    q = NT * l + j
                    dve.wait_ge(sem("h2_ps"), 2 * q + 2)
                    if j >= 2:
                        dve.wait_ge(sem(f"h2_stored{j % 2}"), 16 * (j // 2))
                    V.tensor_copy(h2s[:, j % 2, 512:1024], ps[:, 4 + (2 * j + 1) % 4, :]).then_inc(sem("h2_dve"), 1)

            def router(l):
                n = NORM[l, 1][1]
                lgv = lg.rearrange("p (j k) -> p j k", k=20)[:, 0:n, :]

                def r(name):
                    return R[name][:, 0:n]

                def r4(name):
                    return R[name][:, 0:4 * n].rearrange("p (j k) -> p j k", k=4)

                def r16(name):
                    return R[name][:, 0:16 * n].rearrange("p (j k) -> p j k", k=16)

                def b4(name):
                    return R[name][:, 0:n].unsqueeze(2).to_broadcast([P, n, 4])

                def first_one(dst, name):
                    w4 = cst[:, C_W4:C_W4 + 4].unsqueeze(1).to_broadcast([P, n, 4])
                    link(V.tensor_tensor(r4("sc"), r4(name), w4, ALU.mult))
                    link(V.tensor_reduce(r("mx"), r4("sc"), AX_X, ALU.max))
                    link(V.tensor_tensor(r4(dst), r4("sc"), b4("mx"), ALU.is_equal))

                dve.wait_ge(sem("logits"), l + 1)
                dve.wait_ge(sem("router_in"), 64 * (l + 1))
                link(V.tensor_tensor(lgv, ps[:, 0, 0:32 * n].rearrange("p (j k) -> p j k", k=32)[:, :, 0:20],
                                     r_bias.unsqueeze(1).to_broadcast([P, n, 20]), ALU.add))
                link(V.tensor_reduce(r("gm"), lgv[:, :, 0:4], AX_X, ALU.max))
                V.tensor_tensor(r4("ge"), lgv[:, :, 0:4], b4("gm"), ALU.subtract).then_inc(sem("g_shift"), 1)
                link(V.tensor_tensor(r4("eq"), lgv[:, :, 0:4], b4("gm"), ALU.is_equal))
                first_one("ohg", "eq")
                t16 = r16("tmp").rearrange("p j (g e) -> p j g e", g=4)
                link(V.tensor_tensor(t16, lgv[:, :, 4:20].rearrange("p j (g e) -> p j g e", g=4),
                                     r4("ohg").unsqueeze(3).to_broadcast([P, n, 4, 4]), ALU.mult))
                link(V.tensor_reduce(r4("el"), t16.rearrange("p j g e -> p j e g"), AX_X, ALU.add))
                link(V.tensor_reduce(r("m1"), r4("el"), AX_X, ALU.max))
                link(V.tensor_tensor(r4("eq"), r4("el"), b4("m1"), ALU.is_equal))
                first_one("oh1", "eq")
                link(V.tensor_scalar(R["e2"][:, 0:4 * n], R["oh1"][:, 0:4 * n], -3.0e38, None, ALU.mult))
                link(V.tensor_tensor(r4("e2"), r4("e2"), r4("el"), ALU.add))
                link(V.tensor_reduce(r("m2"), r4("e2"), AX_X, ALU.max))
                link(V.tensor_tensor(r4("eq"), r4("e2"), b4("m2"), ALU.is_equal))
                first_one("oh2", "eq")
                V.tensor_tensor(r("dd"), r("m2"), r("m1"), ALU.subtract).then_inc(sem("e_shift"), 1)
                for m, o in (("M1", "oh1"), ("M2", "oh2")):
                    link(V.tensor_tensor(r16(m).rearrange("p j (g e) -> p j g e", g=4),
                                         r4("ohg").unsqueeze(3).to_broadcast([P, n, 4, 4]),
                                         r4(o).unsqueeze(2).to_broadcast([P, n, 4, 4]), ALU.mult))
                V.tensor_tensor(r16("MM"), r16("M1"), r16("M2"), ALU.add).then_inc(sem("chosen"), 1)
                dve.wait_ge(sem("g_exp"), l + 1)
                link(V.tensor_reduce(r("gs"), r4("gx"), AX_X, ALU.add))
                link(V.reciprocal(r("pg"), r("gs")))
                dve.wait_ge(sem("e_exp"), l + 1)
                link(V.tensor_scalar(r("dn"), r("ex"), 1.0, None, ALU.add))
                link(V.reciprocal(r("rd"), r("dn")))
                link(V.tensor_tensor(w1[:, 0:n], r("pg"), r("rd"), ALU.mult))
                link(V.tensor_tensor(w2[:, 0:n], w1[:, 0:n], r("ex"), ALU.mult))
                dve.wait_ge(sem("ranks"), l + 1)
                link(V.tensor_copy(R["rk"][:, 0:16 * n], ps[:, 1, 0:16 * n]))
                V.tensor_copy(cnt, ps[:, 1, 64:80]).then_inc(sem("rank_taken"), 1)
                dve.wait_ge(sem("rank_taken"), l + 1)
                cap = CAP[l]
                steps = n * P // cap - 1
                link(V.tensor_scalar(nov, cnt, float(cap), None, ALU.is_gt))
                for k in range(2, steps + 1):
                    link(V.tensor_scalar(inc, cnt, float(k * cap), None, ALU.is_gt))
                    link(V.tensor_tensor(nov, nov, inc, ALU.add))
                a, b = inc, inc2
                link(V.tensor_copy(a, nov))
                for d in (1, 2, 4, 8):
                    link(V.tensor_copy(b[:, 0:d], a[:, 0:d]))
                    link(V.tensor_tensor(b[:, d:16], a[:, d:16], a[:, 0:16 - d], ALU.add))
                    a, b = b, a
                link(V.tensor_tensor(exc, a, nov, ALU.subtract))
                link(V.tensor_copy(ov_n, a[0:1, 15:16]))
                tv = te_t[0:1, 0:16 * MAXOV].rearrange("p (i k) -> p i k", k=16)
                link(V.tensor_tensor(tv, a[0:1, :].unsqueeze(1).to_broadcast([1, MAXOV, 16]),
                                     cst[0:1, C_OVI:C_OVI + MAXOV].unsqueeze(2).to_broadcast([1, MAXOV, 16]), ALU.is_le))
                link(V.tensor_reduce(te_t[0:1, 256:256 + MAXOV], tv, AX_X, ALU.add))
                link(V.tensor_scalar(te_t[0:1, 256:256 + MAXOV], te_t[0:1, 256:256 + MAXOV], float(NEXP - 1), None, ALU.min))
                V.tensor_copy(ov_e, te_t[0:1, 256:256 + MAXOV]).then_inc(sem("routed"), 1)
                link(V.tensor_scalar(R["k0"][:, 0:16 * n], R["rk"][:, 0:16 * n], float(cap), None, ALU.is_ge))
                link(V.tensor_copy(R["kk"][:, 0:16 * n], R["k0"][:, 0:16 * n]))
                for k in range(2, steps + 1):
                    link(V.tensor_scalar(R["sl"][:, 0:16 * n], R["rk"][:, 0:16 * n], float(k * cap), None, ALU.is_ge))
                    link(V.tensor_tensor(R["kk"][:, 0:16 * n], R["kk"][:, 0:16 * n], R["sl"][:, 0:16 * n], ALU.add))
                link(V.scalar_tensor_tensor(R["sl"][:, 0:16 * n], R["kk"][:, 0:16 * n], -float(cap), R["rk"][:, 0:16 * n],
                                            ALU.mult, ALU.add))
                link(V.tensor_tensor(adj, exc, cst[:, C_E:C_E + 16], ALU.subtract))
                link(V.tensor_scalar(adj, adj, float(NEXP - 1), None, ALU.add))
                link(V.tensor_tensor(r16("tl"), r16("k0"), adj.unsqueeze(1).to_broadcast([P, n, 16]), ALU.mult))
                link(V.tensor_tensor(r16("tl"), r16("tl"), r16("kk"), ALU.add))
                link(V.tensor_tensor(r16("tl"), r16("tl"), cst[:, C_E:C_E + 16].unsqueeze(1).to_broadcast([P, n, 16]), ALU.add))
                for kind in range(2):
                    if kind == 0:
                        link(V.scalar_tensor_tensor(R["pa"][:, 0:16 * n], R["sl"][:, 0:16 * n], float(NTL),
                                                    R["tl"][:, 0:16 * n], ALU.mult, ALU.add))
                    else:
                        link(V.scalar_tensor_tensor(R["pa"][:, 0:16 * n], R["tl"][:, 0:16 * n], float(cap),
                                                    R["sl"][:, 0:16 * n], ALU.mult, ALU.add))
                    dst = (posl, posy)[kind]
                    for k, m in enumerate(("M1", "M2")):
                        link(V.tensor_tensor(r16("tmp"), r16("pa"), r16(m), ALU.mult))
                        link(V.tensor_reduce(r("f1"), r16("tmp"), AX_X, ALU.add))
                        link(V.tensor_copy(dst[:, 4 * k:4 * k + n], r("f1")))
                    dve.sem_inc(sem("positions"), 1)

            def xgt_half(l, e, p):
                dve.wait_ge(sem("xgT_ps"), NEXP * l + e + 1)
                wait_expert(dve, "u", l, e - 2)
                V.tensor_copy(*xgt_copy(l, p, 1)).then_inc(sem("xgT_dve"), 1)

            def hidden(l, e, p):
                dve.wait_ge(sem("silu_done"), NEXP * l + e + 1)
                wait_expert(dve, "u", l, e)
                hw = hid_width(l)
                V.tensor_tensor(hid[:, p, 0:hw], hid[:, p, 0:hw], ps[:, 1, 0:hw], ALU.mult).then_inc(sem("hid_ready"), 1)

            def hidden_t(l, e, p):
                dve.wait_ge(sem("hidT_ps"), NEXP * l + e + 1)
                wait_expert(dve, "d", l, e - 2)
                hw = hid_width(l)
                V.tensor_copy(hidT[:, p, :, :].rearrange("p a b -> p (a b)")[:, 0:hw], ps[:, 2, 0:hw])\
                    .then_inc(sem("hidT_ready"), 1)

            def y_half(l, e, p):
                wait_expert(dve, "d", l, e)
                y_free(dve, l, e, p)
                V.tensor_copy(*y_copy(l, p, 1)).then_inc(sem("y_dve"), 1)

            def experts(l):
                xgt_half(l, 0, 0)
                hidden(l, 0, 0)
                xgt_half(l, 1, 1)

                def step(e, p, last=False):
                    hidden_t(l, e - 1, 1 - p)
                    hidden(l, e, p)
                    if not last:
                        xgt_half(l, e + 1, 1 - p)
                    y_half(l, e - 1, 1 - p)
                step(1, 1)
                with dve.Fori(0, NEXP // 2 - 2) as t:
                    step(2 * t + 2, 0)
                    step(2 * t + 3, 1)
                step(NEXP - 2, 0)
                step(NEXP - 1, 1, last=True)
                hidden_t(l, NEXP - 1, 1)
                y_half(l, NEXP - 1, 1)

            def overflow(l):
                n = dve.value_load(ov_n, min_val=0, max_val=MAXOV)
                with dve.If(n > 0):
                    with dve.Fori(0, n) as t:
                        dve.wait_ge(sem(f"ov_step{l}"), OV_STEPS * t + OV_XT)
                        V.tensor_copy(*xgt_copy(l, 0, 0))
                        V.tensor_copy(*xgt_copy(l, 0, 1)).then_inc(sem(f"ov_step{l}"), 1)
                        dve.wait_ge(sem(f"ov_step{l}"), OV_STEPS * t + OV_SILU)
                        hw = hid_width(l)
                        V.tensor_tensor(hid[:, 0, 0:hw], hid[:, 0, 0:hw], ps[:, 1, 0:hw], ALU.mult).then_inc(sem(f"ov_step{l}"), 1)
                        dve.wait_ge(sem(f"ov_step{l}"), OV_STEPS * t + OV_HT)
                        V.tensor_copy(hidT[:, 0, :, :].rearrange("p a b -> p (a b)")[:, 0:hw], ps[:, 2, 0:hw])\
                            .then_inc(sem(f"ov_step{l}"), 1)
                        dve.wait_ge(sem(f"ov_step{l}"), OV_STEPS * t + OV_D)
                        V.tensor_copy(*y_copy(l, 0, 0))
                        V.tensor_copy(*y_copy(l, 0, 1))\
                            .then_inc(sem(f"ov_step{l}"), 1)

            def combine(l):
                for j in range(NORM[l, 1][1]):
                    b = j % 2
                    dve.wait_ge(sem(f"yg_in{b}"), 32 * (2 * l + j // 2 + 1))
                    slot = (2 + (0 if j < NLAT else 1)) if l == 0 else 1
                    link(V.tensor_scalar(yg[:, b, 0, :], yg[:, b, 0, :], w1[:, j:j + 1], None, ALU.mult))
                    link(V.scalar_tensor_tensor(yg[:, b, 0, :], yg[:, b, 1, :], w2[:, j:j + 1], yg[:, b, 0, :],
                                                ALU.mult, ALU.add))
                    link(V.tensor_tensor(yg[:, b, 0, :], yg[:, b, 0, :], gb[:, slot, :], ALU.mult))
                    V.tensor_tensor(x[:, j, :], x[:, j, :], yg[:, b, 0, :], ALU.add).then_inc(sem("combined"), 1)
                dve.wait_ge(sem("combined"), NT if l == 0 else NT + NLAT)

            def residual(l, n_tiles, base):
                for h in range(2):
                    for j in range(n_tiles):
                        u = n_tiles * h + j
                        slot = (0 if j < NLAT else 1) if l == 0 else 0
                        wait_res(dve, l, u)
                        V.tensor_tensor(res[:, u % 2, :], ps[:, u % 4, :], gb[:, slot, h * 512:(h + 1) * 512], ALU.mult)\
                            .then_inc(sem("res_taken"), 1)
                        dve.wait_ge(sem("res_taken"), base + u + 1)
                        V.tensor_tensor(x[:, j, h * 512:(h + 1) * 512], x[:, j, h * 512:(h + 1) * 512], res[:, u % 2, :],
                                        ALU.add).then_inc(sem("x_added"), 1)
                dve.wait_ge(sem("x_added"), base + 2 * n_tiles)

            def conv():
                for n in range(NPT):
                    u = UNITS.index(("ca", n))
                    wait_proj(dve, u)
                    dve.wait_ge(sem("proj_taken_act"), n + 1)
                    if n == 0:
                        dve.wait_ge(sem("margins"), 1)
                    V.tensor_tensor(u_in[:, n, :, HALO:HALO + 256], ps[:, u % 4, :].rearrange("p (s t) -> p s t", s=2),
                                    mix[:, 4 + n, :].rearrange("p (s t) -> p s t", s=2), ALU.mult)\
                        .then_inc(sem("proj_taken_dve"), 1)
                dve.wait_ge(sem("proj_taken_dve"), NPT)
                acc = [mix[:, 4 + n, :].rearrange("p (s t) -> p s t", s=2) for n in range(NPT)]
                for n in range(NPT):
                    V.tensor_scalar(acc[n], u_in[:, n, :, 0:256], cpar[:, n, 0:1], cpar[:, n, 31:32], ALU.mult, ALU.add)\
                        .then_inc(sem("conv_done"), 1)
                with dve.Fori(1, TAPS) as t:
                    for n in range(NPT):
                        dve.wait_ge(sem("conv_done"), NPT * t + (n - 3))
                        V.scalar_tensor_tensor(acc[n], u_in[:, n, :, bass.ds(t, 256)], cpar[:, n, bass.ds(t, 1)], acc[n],
                                               ALU.mult, ALU.add).then_inc(sem("conv_done"), 1)

            def gate_logs():
                for j in range(NT):
                    dve.wait_ge(sem("la_act"), 2 * NT + j + 1)
                    V.scalar_tensor_tensor(la[:, j, :], ps[:, 4 + j, :], 0.0, la[:, j, :], ALU.min, ALU.subtract)\
                        .then_inc(sem("la_ready"), 1)

            def conv_norm():
                dve.wait_ge(sem("cn_sum"), 1)
                for i in range(NPT):
                    V.scalar_tensor_tensor(mix[:, 4 + i, :], ps[:, 0, :], -1.0 / CONV_CH, mix[:, 4 + i, :],
                                           ALU.mult, ALU.add).then_inc(sem("cn_centred"), 1)
                dve.wait_ge(sem("cn_root"), 1)
                link(V.reciprocal(ps[:, 2, :], ps[:, 2, :]))
                dve.wait_ge(sem("cn_sq"), NPT)
                for i in range(NPT):
                    V.tensor_tensor(mix[:, 4 + i, :], mix[:, 4 + i, :], ps[:, 2, :], ALU.mult).then_inc(sem("cn_scaled"), 1)

            def gla():
                wait_proj(dve, len(UNITS) - 1)
                for pt in range(2):
                    for d in range(2):
                        dve.wait_ge(sem("last_ready"), 2 * pt + d + 1)
                        dve.wait_ge(sem("qk_exp"), 4 * pt + 2 * d + 2)
                        if pt:
                            dve.wait_ge(sem("o_sum"), 2)
                        V.tensor_tensor(k_e[:, d, :].rearrange("p (n t) -> p n t", t=CHUNK),
                                        lastS[:, d, :].unsqueeze(2).to_broadcast([P, NCH, CHUNK]),
                                        ps[:, 4 + 2 * pt + d, :].rearrange("p (n t) -> p n t", t=CHUNK), ALU.subtract)\
                            .then_inc(sem("ke_diff"), 1)
                    for d in range(2):
                        for k, (dst, src) in enumerate(((q_t, qT), (k_t, kT))):
                            dve.wait_ge(sem("qk_exp"), 4 * pt + 2 * d + k + 1)
                            V.tensor_tensor(dst[:, d, :], dst[:, d, :], src[:, pt, :], ALU.mult).then_inc(sem("qk_ready"), 1)
                    for d in range(2):
                        dve.wait_ge(sem("ke_exp"), 2 * pt + d + 1)
                        V.tensor_tensor(k_e[:, d, :], k_e[:, d, :], kT[:, pt, :], ALU.mult).then_inc(sem("ke_ready"), 1)
                    for d in range(2):
                        dve.wait_ge(sem("keT"), 2 * pt + d + 1)
                        V.memset(k_e[:, d, :], 0.0).then_inc(sem("att_zero"), 1)
                    dve.wait_ge(sem("dec_ready"), 2 * pt + 2)
                    for k in range(7):
                        for d in range(2):
                            if k == 0:
                                dve.wait_ge(sem("kv_sum"), 2 * pt + d + 1)
                            n = SEQ[d][k]
                            src = ps[:, 2 * d + n % 2, (n // 2) * P:(n // 2 + 1) * P]
                            if k == 0:
                                V.tensor_copy(states[:, d, 0, :], src).then_inc(sem("state"), 1)
                            else:
                                dve.wait_ge(sem("state"), 14 * pt + 2 * k + d - 1)
                                V.scalar_tensor_tensor(states[:, d, k, :], states[:, d, k - 1, :], dec[:, d, n:n + 1], src,
                                                       ALU.mult, ALU.add).then_inc(sem("state"), 1)
                    for hh in range(2):
                        if hh:
                            dve.wait_ge(sem("o_sum"), 2 * pt + 1)
                        for d in range(2):
                            dve.wait_ge(sem("att"), 4 * pt + 2 * hh + d + 1)
                            dve.wait_ge(sem("att_zero"), 2 * pt + d + 1)
                            mask = cst[:, (C_LO, C_UP)[d]:(C_LO, C_UP)[d] + P].bitcast(U32)
                            V.copy_predicated(k_e[:, d, :].rearrange("p (j n) -> p j n", j=NT),
                                              mask.unsqueeze(1).to_broadcast([P, NT, P]),
                                              ps[:, d, :].rearrange("p (j n) -> p j n", j=NT)).then_inc(sem("att_masked"), 1)
                for h in range(4):
                    rs = (qT if h % 2 == 0 else kT)[:, h // 2, :]
                    dve.wait_ge(sem("o_root"), h + 1)
                    link(V.reciprocal(rs, rs))
                    link(V.tensor_tensor(mix[:, h, :], mix[:, h, :], rs, ALU.mult))
                    V.scalar_tensor_tensor(mix[:, h, :], rT[:, h, :], cpar[:, 0, 34:35], mix[:, h, :], ALU.mult, ALU.mult)\
                        .then_inc(sem("mix_ready"), 1)

            def rotate(t, j, nh):
                tv = t.rearrange("p (h k two) -> p h k two", h=nh, two=2)
                x0, x1 = tv[:, :, :, 0], tv[:, :, :, 1]
                cos = cst[:, C_COS + 64 * j:C_COS + 64 * j + 64].unsqueeze(1).to_broadcast([P, nh, 64])
                sin = cst[:, C_SIN + 64 * j:C_SIN + 64 * j + 64].unsqueeze(1).to_broadcast([P, nh, 64])
                a, b, c, d = (w[:, 0:64 * nh].rearrange("p (h k) -> p h k", h=nh)
                              for w in (rt[:, 2, :], rt[:, 3, :], prob[:, 0, :], prob[:, 1, :]))
                V.tensor_tensor(a, x0, cos, ALU.mult)
                V.tensor_tensor(b, x1, sin, ALU.mult)
                V.tensor_tensor(c, x0, sin, ALU.mult)
                link(V.tensor_tensor(d, x1, cos, ALU.mult))
                V.tensor_tensor(x0, a, b, ALU.subtract)
                return V.tensor_tensor(x1, c, d, ALU.add)

            def heads_norm(t4, g, nj, nh, count):
                n = nj * nh
                link(V.tensor_reduce(ss[:, 0:n], rt[:, 0:2, :].rearrange("p a (b c) -> p (a b) c", c=HD), AX_X, ALU.add))
                mean_square(n, HD, count)
                rb = rstd[:, 0:n].rearrange("p (j h) -> p j h", j=nj).unsqueeze(3).to_broadcast([P, nj, nh, HD])
                link(V.tensor_tensor(t4, t4, rb, ALU.mult))
                for j in range(nj):
                    link(V.tensor_tensor(t4[:, j], t4[:, j], g.unsqueeze(1).to_broadcast([P, nh, HD]), ALU.mult))

            def odd_mixer():
                dve.wait_ge(sem("norm_g_in"), 48)
                dve.wait_ge(sem("k_sq"), 1)
                heads_norm(kv_tok[:, :, 0:256].rearrange("p j (h k) -> p j h k", h=KV), gb[:, 3, P:2 * P], NT, KV, 4)
                for j in range(NLAT):
                    ins = rotate(kv_tok[:, j, 0:256], j, KV)
                    if j == 0:
                        link(ins)
                ins.then_inc(sem("k_rot"), 1)
                for j in range(NLAT):
                    dve.wait_ge(sem("q_sq"), j + 1)
                    heads_norm(q_tok[:, j:j + 1, :].rearrange("p j (h k) -> p j h k", h=HEADS), gb[:, 3, 0:P], 1, HEADS, 5 + j)
                    rotate(q_tok[:, j, :], j, HEADS).then_inc(sem("q_rot"), 1)
                scale = float(HD) ** -0.5
                for u in range(2 * HEADS + 2):
                    if u < 2 * HEADS:
                        dve.wait_ge(sem("score_ps"), u + 1)
                        link(V.tensor_reduce(ss[:, 4 + u % 4:5 + u % 4], ps[:, u % 3, :], AX_X, ALU.max))
                        V.tensor_scalar(ss[:, u % 4:u % 4 + 1], ss[:, 4 + u % 4:5 + u % 4], -scale, None, ALU.mult)\
                            .then_inc(sem("neg_max"), 1)
                    if 1 <= u <= 2 * HEADS:
                        v = u - 1
                        dve.wait_ge(sem("prob_exp"), v + 1)
                        link(V.reciprocal(rstd[:, 4 + v % 4:5 + v % 4], rstd[:, v % 4:v % 4 + 1]))
                        V.tensor_scalar(prob[:, v % 2, :], prob[:, v % 2, :], rstd[:, 4 + v % 4:5 + v % 4], None, ALU.mult)\
                            .then_inc(sem("prob_ready"), 1)
                    if u >= 2:
                        v = u - 2
                        h, j = v // 2, v % 2
                        dve.wait_ge(sem("probT_ps"), v + 1)
                        if h >= 2:
                            dve.wait_ge(sem("oh_ps"), h - 1)
                        V.tensor_copy(probT[:, h % 2, :, j * P:(j + 1) * P], ps[:, 3 + v % 2, :].rearrange("p (c n) -> p c n", c=NT))\
                            .then_inc(sem("probT_taken"), 1)

            V.memset(silu_c[:, :, :], 0.0).then_inc(sem("silu_zero"), 1)
            ada(0)
            dve.wait_ge(sem("par_ps"), 1)
            link(V.tensor_copy(cpar[:, :, :], ps[:, 4, 0:64 * NPT].rearrange("p (i k) -> p i k", k=64)[:, :, 0:35]))
            norm(0, 0)
            conv()
            gate_logs()
            conv_norm()
            gla()
            residual(0, NT, 0)
            norm(0, 1)
            rows(0)
            router(0)
            ada(1)
            experts(0)
            overflow(0)
            combine(0)
            norm(1, 0)
            odd_mixer()
            residual(1, NLAT, 2 * NT)
            norm(1, 1)
            rows(1)
            router(1)
            experts(1)
            overflow(1)
            combine(1)
            dve.wait_ge(sem("sq_done"), NBASE[3] + 2 * NLAT)
            mean_square(NLAT, D, 8)
            for j in range(NLAT):
                V.scalar_tensor_tensor(x[:, j, :], x[:, j, :], rstd[:, j:j + 1], gb[:, 2, :], ALU.mult, ALU.mult)\
                    .then_inc(sem("final_ready"), 1)

        @block.gpsimd
        def _(pool):
            chain = [0]

            def link(ins):
                chain[0] += 1
                ins.then_inc(sem("pool_chain"), 1)
                pool.wait_ge(sem("pool_chain"), chain[0])

            G = nc.gpsimd

            def gate_bias(l):
                for k, t in enumerate((2, 5)):
                    pool.dma_start(bias_row[:, k, :], A["ada_b"][l:l + 1, t * D:(t + 1) * D]).then_inc(sem("gate_bias_in"), 16)

            def router_params(l):
                wv = w_rt.rearrange("p (c k) -> p c k", k=20)
                pool.dma_start(wv[:, :, 0:4], A["moe_w_group"][l].rearrange("(p c) g -> p c g", c=KC))\
                    .then_inc(sem("router_in"), 16)
                pool.dma_start(wv[:, :, 4:20], A["moe_w_router"][l].rearrange("(p c) g e -> p c (g e)", c=KC))\
                    .then_inc(sem("router_in"), 16)
                pool.dma_start(r_bias[:, 0:4], A["moe_b_group"][l:l + 1, :].to_broadcast([P, 4])).then_inc(sem("router_in"), 16)
                pool.dma_start(r_bias[:, 4:20], A["moe_b_router"][l:l + 1].rearrange("a g e -> a (g e)").to_broadcast([P, 16]))\
                    .then_inc(sem("router_in"), 16)

            def dispatch(l):
                n = NORM[l, 1][1]
                pool.wait_ge(sem("list_zero"), 32)
                pool.wait_ge(sem("positions"), 2 * l + 1)
                for k in range(2):
                    for j in range(n):
                        G.indirect_dma_start(slot_list[l], bass.IndirectOffsetOnAxis(ap=posl[:, 4 * k + j:4 * k + j + 1], axis=0),
                                             cst[:, C_TOK + j:C_TOK + j + 1].bitcast(I32), None).then_inc(sem("list_in"), 16)
                pool.wait_ge(sem("list_in"), 32 * NT if l == 0 else 32 * (NT + NLAT))
                pool.dma_start(idx, slot_list[l].rearrange("(p t) a -> p (t a)", t=NTL)).then_inc(sem("idx_in"), 16)
                pool.wait_ge(sem("idx_in"), 16 * (l + 1))
                for p in range(2):
                    pool.wait_ge(sem(f"h2_stored{p}"), 8 * (NT if l == 0 else NT + NLAT))

            def gather(l, e, p):
                if not (isinstance(e, int) and e < 2 and l == 0):
                    pool.wait_ge(sem("xgT_ps"), NEXP * l + e - 1)
                ex = e if isinstance(e, int) else bass.ds(e, 1)
                G.tensor_copy(idxc[:, p:p + 1], idx[:, e:e + 1] if isinstance(e, int) else idx[:, ex])\
                    .then_inc(sem("idx_col"), 1)
                pool.wait_ge(sem("idx_col"), NEXP * l + e + 1)
                pool.sem_inc(sem("waits_passed"), 1)
                G.indirect_dma_start(xg[0:CAP[l], p, :], None, h2_rows,
                                     bass.IndirectOffsetOnAxis(ap=idxc[0:CAP[l], p:p + 1], axis=0))\
                    .then_inc(sem(f"xg_in{p}"), 16)

            def overflow(l):
                n = pool.value_load(ov_n, min_val=0, max_val=MAXOV)
                with pool.If(n > 0):
                    pool.wait_ge(sem("xg_in0"), 8 * NEXP * (l + 1))
                    pool.wait_ge(sem("xgT_ps"), NEXP * (l + 1))
                    with pool.Fori(0, n) as t:
                        G.tensor_copy(idxc[:, 0:1], idx[:, bass.ds(t + NEXP, 1)]).then_inc(sem(f"ov_col{l}"), 1)
                        pool.wait_ge(sem(f"ov_col{l}"), t + 1)
                        pool.sem_inc(sem("waits_passed"), 1)
                        G.indirect_dma_start(xg[0:CAP[l], 0, :], None, h2_rows,
                                             bass.IndirectOffsetOnAxis(ap=idxc[0:CAP[l], 0:1], axis=0)).then_inc(sem(f"ov_xg{l}"), 16)
                        pool.wait_ge(sem(f"ov_step{l}"), OV_STEPS * t + OV_Y)

            def combine(l):
                pool.wait_ge(sem("y_complete"), l + 1)
                pool.wait_ge(sem("positions"), 2 * l + 2)
                for j in range(NORM[l, 1][1]):
                    if j >= 2:
                        pool.wait_ge(sem("combined"), j - 1)
                    for k in range(2):
                        G.indirect_dma_start(yg[:, j % 2, k, :], None, y_rows,
                                             bass.IndirectOffsetOnAxis(ap=posy[:, 4 * k + j:4 * k + j + 1], axis=0))\
                            .then_inc(sem(f"yg_in{j % 2}"), 16)

            gate_bias(0)
            for l in range(2):
                for k, t in enumerate((0, 1, 3, 4)):
                    pool.dma_start(bias_cols[:, l, k, :], A["ada_b"][l, t * D:(t + 1) * D].rearrange("(p c) -> p c", c=KC))\
                        .then_inc(sem("bias_cols_in"), 16)
            link(G.memset(zero_i, 0))
            link(G.memset(par_rows, 0.0))
            link(G.memset(dec_w, 0.0))
            link(G.memset(z_all[32:33, :], 1.0))
            pool.sem_inc(sem("z_ready"), 1)
            G.memset(u_in[:, :, :, :].rearrange("p a b c -> p (a b c)"), 0.0).then_inc(sem("u_zero"), 1)
            for l in range(2):
                pool.dma_start(slot_list[l].rearrange("(p t) a -> p (t a)", t=NTL), zero_i).then_inc(sem("list_zero"), 16)
            small = [(par_rows[0:31, :], A["even_conv_w"].rearrange("a w b n -> (a w b) n")),
                     (par_rows[31:32, :], A["even_conv_b"]), (par_rows[32:33, :], A["even_conv_norm_g"]),
                     (par_rows[33:34, :], A["even_conv_norm_b"]), (par_rows[34:35, 0:P], A["even_gla_norm_g"]),
                     (w_z, A["even_w_in"][0, :, 1536:1568].rearrange("(p c) n -> p c n", c=KC)),
                     (dec_w[0:16, 0:256], A["even_dec_w_f"][0]), (dec_w[16:32, 256:512], A["even_dec_w_b"][0]),
                     (dec_w[32:33, 0:256], A["even_dec_b_f"]), (dec_w[32:33, 256:512], A["even_dec_b_b"])]
            for dst, src in small:
                pool.dma_start(dst, src).then_inc(sem("small_in"), 16)
            pool.wait_ge(sem("gate_rows"), 8)
            pool.wait_ge(sem("u_zero"), 1)
            for t in range(MAXOV):
                pool.dma_start(y_rows[(NEXP + t) * P:(NEXP + t + 1) * P, :], ar[:, A_U:A_U + D]).then_inc(sem("y_zero"), 16)
            pool.wait_ge(sem("y_zero"), 16 * MAXOV)
            pool.sem_inc(sem("margins"), 1)
            wait_res(pool, 0, 2 * NT - 1)
            router_params(0)
            dispatch(0)
            pool.wait_ge(sem("logits"), 1)
            gate_bias(1)

            def gathers(l):
                gather(l, 0, 0)
                gather(l, 1, 1)
                with pool.Fori(0, NEXP // 2 - 1) as t:
                    gather(l, 2 * t + 2, 0)
                    gather(l, 2 * t + 3, 1)
            gathers(0)
            overflow(0)
            combine(0)
            pool.wait_ge(sem("combined"), NT)
            for dst, src in ((gb[:, 2, :], A["final_norm_g"].rearrange("(a n) -> a n", a=1).to_broadcast([P, D])),
                             (gb[:, 3, 0:P], A["odd_q_norm_g"].to_broadcast([P, P])),
                             (gb[:, 3, P:2 * P], A["odd_k_norm_g"].to_broadcast([P, P]))):
                pool.dma_start(dst, src).then_inc(sem("norm_g_in"), 16)
            wait_res(pool, 1, 2 * NLAT - 1)
            router_params(1)
            dispatch(1)
            gathers(1)
            overflow(1)
            combine(1)


_INS = ["x", "c", "ctx", "c_ctx", "ada_w", "ada_b", "even_w_in", "even_dec_w_f", "even_dec_b_f", "even_dec_w_b",
        "even_dec_b_b", "even_gla_norm_g", "even_conv_w", "even_conv_b", "even_conv_norm_g", "even_conv_norm_b",
        "even_w_out", "odd_w_in", "odd_q_norm_g", "odd_k_norm_g", "odd_w_out", "moe_w_group", "moe_b_group",
        "moe_w_router", "moe_b_router", "moe_w_gate", "moe_w_up", "moe_w_down", "final_norm_g"]


def kernel(**inputs):
    import concourse.bacc as bacc
    from concourse.bass_utils import run_bass_kernel_spmd

    nc = bacc.Bacc("TRN2", target_bir_lowering=False, num_devices=1)
    arrays, handles = {}, {}
    named = [(n, np.ascontiguousarray(inputs[n])) for n in _INS] + [("consts", constant_table())]
    for name, a in named:
        arrays[f"in_{name}"] = a
        handles[name] = nc.dram_tensor(f"in_{name}", a.shape, mybir.dt.from_np(a.dtype), kind="ExternalInput").ap()
    out = nc.dram_tensor("out_0", (1, 256, D), F32, kind="ExternalOutput").ap()
    hybrid_dit(nc, handles, out)
    r = run_bass_kernel_spmd(nc, [arrays], core_ids=[0])
    return r.results[0]["out_0"]
```

```python
from contextlib import ExitStack

import numpy as np
import concourse.bass as bass
from concourse import mybir

ALU = mybir.AluOpType
ACT = mybir.ActivationFunctionType
F32 = mybir.dt.float32
I32 = mybir.dt.int32
U32 = mybir.dt.uint32
AX_X = mybir.AxisListType.X

P = 128
D = 1024
KC = D // P
NT = 4
NLAT = 2
H_GLA, DK, DV = 4, 64, 128
CHUNK = 64
NCH = NT * P // CHUNK
RANK = 16
CONV_CH, TAPS = 512, 31
HALO = TAPS // 2
SEG = 256 + 2 * HALO
NPT = CONV_CH // P
HEADS, KV, HD = 8, 2, 128
NEXP, EPG = 16, 4
HID = 512
HC = HID // P
CAP = (128, 64)
MAXOV = 7
assert all(2 * n * P // cap - 1 == MAXOV for n, cap in zip((NT, NLAT), CAP))
NTL = NEXP + MAXOV + 1
EPS = 1e-6
SLOTS = 6
BW = KC * 512
GRID_W = 64
GATE_BANK = (6, 3)
ADA1 = (0, 1, 3, 4, 2, 5)

C_ID, C_LO, C_UP, C_ONE, C_TRI, C_COS, C_SIN = 0, 128, 256, 384, 512, 640, 768
C_EPS, C_W4, C_E, C_OVI, C_TOK, C_SEL = 896, 897, 901, 917, 933, 937
C_THR = 939
C_SUM = C_THR + 2 * MAXOV
C_END = C_SUM + NEXP + EPG

A_Q, A_K, A_V, A_R, A_U, A_MIX = 0, 1024, 2048, 4096, 6144, 6144 + NPT * 2 * SEG
A_END = A_MIX + 4096
M_H2, M_XG, M_XT, M_HID, M_HT, M_Y, M_SM = 0, 2048, 4096, 6144, 7168, 8192, 10240
O_Q, O_KV, O_QT, O_KT, O_P, O_PT, O_O = 0, 2048, 4096, 6144, 7168, 8192, 10240


def constant_table():
    t = np.zeros((P, C_END), np.float32)
    r = np.arange(P)
    same = (r[:, None] // CHUNK) == (r[None, :] // CHUNK)
    t[:, C_ID:C_ID + P] = np.eye(P)
    t[:, C_LO:C_LO + P] = same & (r[:, None] <= r[None, :])
    t[:, C_UP:C_UP + P] = same & (r[:, None] >= r[None, :])
    t[:, C_ONE:C_ONE + P] = 1.0
    t[:, C_TRI:C_TRI + P] = r[:, None] < r[None, :]
    for i in range(NEXP + EPG):
        t[i::32, C_SUM + i] = 1.0
    for r2 in range(2):
        t[r2::32, C_SEL + r2] = 1.0
    tok = np.arange(NLAT * P)
    pairs = HD // 4
    inv = (np.float32(10000.0) ** (-np.arange(pairs, dtype=np.float32) / np.float32(pairs))).astype(np.float32)
    ang = np.concatenate([(tok // GRID_W).astype(np.float32)[:, None] * inv,
                          (tok % GRID_W).astype(np.float32)[:, None] * inv], axis=-1)
    for j in range(NLAT):
        t[:, C_COS + 64 * j:C_COS + 64 * j + 64] = np.cos(ang[j * P:(j + 1) * P])
        t[:, C_SIN + 64 * j:C_SIN + 64 * j + 64] = np.sin(ang[j * P:(j + 1) * P])
    t[:, C_EPS] = EPS
    t[:, C_W4:C_W4 + 4] = [4, 3, 2, 1]
    t[:, C_E:C_E + NEXP] = np.arange(NEXP)
    t[:, C_OVI:C_OVI + 16] = np.arange(16)
    t[:, C_TOK:C_TOK + NT] = r[:, None] + P * np.arange(NT)[None, :]
    for l in range(2):
        t[:, C_THR + MAXOV * l:C_THR + MAXOV * (l + 1)] = CAP[l] * np.arange(1, MAXOV + 1)
    return t


def weight_stream():
    out = [("ada", 0, n) for n in range(4)] + [("ein", 0, "cg")] + [("ada", 0, n) for n in range(4, 6)]
    out += [("ein", 0, "ca")] + [("ada", 0, n) for n in range(6, 12)] + [("ein", 0, n) for n in ("qk", "v", "r")]
    out += [("ada", 1, 2 * s + h) for s in ADA1 for h in range(2)]
    out += [("eout", 0, 0), ("eout", 0, 1)]
    for l in range(2):
        out += [("g", l, 0), ("u", l, 0)]
        for e in range(1, NEXP):
            out += [("g", l, e), ("u", l, e), ("d", l, e - 1)]
        out += [("d", l, NEXP - 1)]
        if l == 0:
            out += [("oin", 0, 2), ("oin", 0, 0), ("oin", 0, 1), ("oout", 0, 0), ("oout", 0, 1)]
    return out


def hybrid_dit(nc, A, out):
    stream = weight_stream()
    at = {b: i for i, b in enumerate(stream)}
    ctx = ExitStack()
    with ctx:
        def sb(name, shape, dt=F32):
            return ctx.enter_context(nc.sbuf_tensor(name, shape, dt))

        sems = {}

        def sem(name):
            if name not in sems:
                sems[name] = ctx.enter_context(nc.semaphore(name))
            return sems[name]

        ring = sb("ring", [P, SLOTS, BW])
        x = sb("x", [P, NT, D])
        hT = sb("hT", [P, KC, 512])
        gb = sb("gb", [P, 4, D])
        mla = sb("mla", [P, 2048])
        ar = sb("ar", [P, A_END])
        cst = sb("cst", [P, C_END])
        modT = sb("modT", [P, 2, 4, KC, 2])
        cpar = sb("cpar", [P, NPT, 35])
        c_cols = sb("c_cols", [P, 2, KC])
        silu_c = sb("silu_c", [P, KC, 32])
        bias_cols = sb("bias_cols", [P, 2, 4, KC])
        ss = sb("ss", [P, 16])
        rstd = sb("rstd", [P, 16])
        lastS = sb("lastS", [P, 2, NCH])
        dec = sb("dec", [P, 2, NCH])
        sm = sb("sm", [P, 60])
        ps = ctx.enter_context(nc.psum_tensor("ps", [P, 8, 512], F32))

        h2_rows = nc.dram_tensor("h2_rows", (NT * P, D), F32, kind="Internal").ap()
        y_rows = nc.dram_tensor("y_rows", ((NEXP + MAXOV) * P, D), F32, kind="Internal").ap()

        ident = cst[:, C_ID:C_ID + P]
        ones = cst[:, C_ONE:C_ONE + P]
        eps = cst[:, C_EPS:C_EPS + 1]
        modrow = mla[:, :].rearrange("r (b n) -> r b n", b=2)
        bias_row = ar[0:1, M_XG:M_XG + 2 * D].rearrange("p (s n) -> p s n", s=2)
        la = mla[:, :].rearrange("p (j n) -> p j n", j=NT)

        def view(o, *dims):
            n = int(np.prod(dims))
            v = ar[:, o:o + n]
            if len(dims) == 2:
                v = v.rearrange("p (a b) -> p a b", a=dims[0])
            if len(dims) == 3:
                v = v.rearrange("p (a b c) -> p a b c", a=dims[0], b=dims[1])
            return v

        qT, kT = view(A_Q, 2, 512), view(A_K, 2, 512)
        v_tok, rT = view(A_V, NT, 512), view(A_R, 4, 512)
        xn = view(A_R, 2, D)
        u_in = view(A_U, NPT, 2, SEG)
        mix = view(A_MIX, 8, 512)
        z_all = ar[0:33, A_MIX:A_MIX + 512]
        dec_w = ar[0:33, A_MIX + 512:A_MIX + 1024]
        w_z = view(A_MIX + 1024, KC, 32)
        par_rows = ar[0:35, A_MIX + 1536:A_MIX + 2048]
        sq4 = view(A_U, 4, 512)
        states = view(A_U, 2, 7, P)
        hflat = hT[:, :, :].rearrange("p a b -> p (a b)")
        q_t = hflat[:, 0:1024].rearrange("p (d n) -> p d n", d=2)
        k_t = hflat[:, 1024:2048].rearrange("p (d n) -> p d n", d=2)
        k_e = hflat[:, 2048:3072].rearrange("p (d n) -> p d n", d=2)
        k_etok = hflat[:, 3072:4096].rearrange("p (d j n) -> p d j n", d=2, j=NT)
        att_sum = hflat[:, 3072:4096].rearrange("p (h n) -> p h n", h=2)
        res = hflat[:, 0:1024].rearrange("p (b n) -> p b n", b=2)
        h2s, xg, xgT = view(M_H2, 2, D), view(M_XG, 2, D), view(M_XT, 2, KC, P)
        hid, hidT, yb = view(M_HID, 2, HID), view(M_HT, 2, HC, P), view(M_Y, 2, D)
        yg = [hflat[:, 2048 * b:2048 * (b + 1)].rearrange("p (k n) -> p k n", k=2) for b in range(2)]
        yg += [view(M_XT, 2, D), view(M_HID, 2, D)]
        q_tok, kv_tok = view(O_Q, 2, D), view(O_KV, NT, 512)
        qhT, khT = view(O_QT, HEADS, 256), view(O_KT, KV, 512)
        prob, probT = view(O_P, 2, 512), view(O_PT, 2, NT, 256)
        ohT = view(O_O, HEADS, 256)
        rt = view(O_PT, 4, 512)

        moff = [M_SM]

        def small(n):
            o = moff[0]
            moff[0] += n
            assert moff[0] <= A_END
            return ar[:, o:o + n]

        w_rt, r_bias = ar[:, M_XG:M_XG + KC * 32], ar[:, M_XG + KC * 32:M_XG + KC * 32 + 20]
        lg = small(NT * 20)
        R = {k: small(NT * n) for k, n in dict(
            gm=1, ge=4, gx=4, gs=1, pg=1, eq=4, sc=4, mx=1, ohg=4, el=4, m1=1, oh1=4, e2=4, m2=1,
            oh2=4, dd=1, ex=1, dn=1, rd=1, M12=32, MM=16, t12=32, lower=32,
            ek=2, r12=2, kk=2, ke=2, sl=2, ne=2, xk=2, tile=2, py=2, tmp=16).items()}
        nov, inc, inc2 = (small(NEXP) for _ in range(3))
        cmp_c, cmp_t, ov_t = small(NEXP * MAXOV), small(2 * NT * MAXOV), small(17 * MAXOV)
        tile_hot = small(2 * NT * NTL)
        slot_hot = view(M_Y, 2 * NT, P)
        logitsT = view(M_Y + 2 * NT * P, 512)
        w1, w2 = sm[:, 0:4], sm[:, 4:8]
        posy = sm[:, 16:24].bitcast(I32)
        idx = sm[:, 24:24 + NTL].bitcast(I32)
        idxc = sm[:, 24 + NTL:26 + NTL].bitcast(I32)
        ov_n = sm[0:1, 52:53].bitcast(I32)
        ov_e = sm[0:1, 53:53 + MAXOV].bitcast(I32)
        assert 26 + NTL <= 52 and 53 + MAXOV <= 60

        block = ctx.enter_context(nc.Block())

        def arrived(eng, i):
            eng.wait_ge(sem(f"block_in{i % SLOTS}"), 16 * (i // SLOTS + 1))

        def blk(i):
            return ring[:, i % SLOTS, :].rearrange("p (c n) -> p c n", c=KC)

        UNITS = [(k, n) for k, c in (("cg", 4), ("ca", 4), ("qk", 4), ("z", 1), ("v", 4), ("r", 4)) for n in range(c)]
        OUNITS = [("kv", j) for j in range(NT)] + [(k, j) for k in ("q0", "q1") for j in range(NLAT)]
        N_SMALL = 10
        SEQ = ([4, 5, 6, 7, 0, 1, 2, 3], [7, 6, 5, 4, 3, 2, 1, 0])

        def taken_count(u):
            eng = "dve" if UNITS[u][0] == "ca" else "act"
            return eng, sum(1 for v in UNITS[:u + 1] if (v[0] == "ca") == (eng == "dve"))

        def wait_proj(eng, u):
            kind, n = UNITS[u]
            if n == 3:
                eng.wait_ge(sem("block_used"), at["ein", 0, kind] + 1)
            else:
                eng.wait_ge(sem("proj"), sum(1 for v in UNITS[:u + 1] if v[1] != 3))

        def oproj_last(u):
            return u + 1 == len(OUNITS) or OUNITS[u + 1][0] != OUNITS[u][0]

        def wait_oproj(eng, u):
            if oproj_last(u):
                eng.wait_ge(sem("block_used"), at["oin", 0, {"kv": 2, "q0": 0, "q1": 1}[OUNITS[u][0]]] + 1)
            else:
                eng.wait_ge(sem("oproj"), sum(1 for v in range(u + 1) if not oproj_last(v)))

        def wait_res(eng, l, u):
            n = NT if l == 0 else NLAT
            h, j = u // n, u % n
            if j == n - 1:
                eng.wait_ge(sem("block_used"), at["eout" if l == 0 else "oout", 0, h] + 1)
            else:
                eng.wait_ge(sem("res_ps"), (0 if l == 0 else 2 * (NT - 1)) + (n - 1) * h + j + 1)

        def wait_expert(eng, kind, l, e):
            if isinstance(e, int):
                if e < 0:
                    l, e = l - 1, e + NEXP
                if l < 0:
                    return
                eng.wait_ge(sem("block_used"), at[kind, l, e] + 1)
            else:
                eng.wait_ge(sem("block_used"), 3 * e + (at[kind, l, 2] - 5))

        OV_XT, OV_XGT, OV_GU, OV_SILU, OV_HID, OV_HT, OV_HIDT, OV_D, OV_Y = range(1, 10)
        OV_STEPS = OV_Y

        def xgt_copy(l, p, k):
            n = CAP[l]
            return (xgT[:, p, 4 * k:4 * k + 4, 0:n],
                    ps[:, 3 + k, 0:4 * n].rearrange("p (c n) -> p c n", c=4))

        def hid_width(l):
            return HID if l == 0 else HID // 2

        def y_copy(l, p, k):
            if l == 0:
                return yb[:, p, 512 * k:512 * k + 512], ps[:, 5 + k, :]
            return yb[64 * k:64 * k + 64, p, 0:512], ps[64 * k:64 * k + 64, 5 + k, :]

        def store_y(l, tile, p, done):
            if l == 0:
                nc.scalar.dma_start(y_rows.rearrange("(t s) n -> t s n", s=P)[tile, :, :], yb[:, p, :]).then_inc(done, 16)
            else:
                for h in range(2):
                    nc.scalar.dma_start(y_rows.rearrange("(t s) n -> t s n", s=64)[tile, :, h * 512:(h + 1) * 512],
                                        yb[64 * h:64 * h + 64, p, 0:512]).then_inc(done, 16)

        def y_free(eng, l, e, p):
            if not (isinstance(e, int) and e < 2 and l == 0):
                eng.wait_ge(sem(f"y_stored{p}"), (8 * e - 8 * p) if l == 0 else 128 + 16 * e - 16 * p)

        def gate_unit(l, s, r, h):
            return (4 * (s // 3) + 2 * r + h) if l == 0 else 8 + 2 * (s // 3) + h

        def gate_slot(l, s, r):
            return (2 * (s // 3) + r) if l == 0 else s // 3

        def xn_of(k):
            return view(O_O, 2, D) if k == 2 else xn

        NORM = {(0, 0): (0, NT), (0, 1): (1, NT), (1, 0): (2, NT), (1, 1): (3, NLAT)}
        MS = {0: 1, 1: 2, 2: 3, 3: 7}
        NBASE = {0: 0, 1: NT, 2: 2 * NT, 3: 3 * NT}

        @block.sync
        def _(sp):
            def src(b):
                kind, l, n = b
                if kind == "ada":
                    return A["ada_w"][l, :, n * 512:(n + 1) * 512].rearrange("(p c) n -> p c n", c=KC)
                if kind == "ein":
                    o = {"qk": 0, "v": 512, "r": 1024, "ca": 1568, "cg": 2080}[n]
                    return A["even_w_in"][0, :, o:o + 512].rearrange("(p c) n -> p c n", c=KC)
                if kind in ("eout", "oout"):
                    w = A["even_w_out" if kind == "eout" else "odd_w_out"]
                    return w[0, :, n * 512:(n + 1) * 512].rearrange("(c p) n -> p c n", c=KC)
                if kind == "oin":
                    return A["odd_w_in"][0, :, n * 512:(n + 1) * 512].rearrange("(p c) n -> p c n", c=KC)
                raise ValueError(kind)

            def expert_src(kind, l, e):
                if kind == "d":
                    return A["moe_w_down"][l, e, :, :].rearrange("(p c) n -> p (c n)", c=HC)
                return A["moe_w_gate" if kind == "g" else "moe_w_up"][l, e, :, :].rearrange(
                    "(p c) n -> p (c n)", c=KC)

            def load(i, s, count=None, wide=False):
                if count is None:
                    count = i - SLOTS + 1
                    if count >= 1:
                        sp.wait_ge(sem("block_used"), count)
                else:
                    sp.wait_ge(sem("block_used"), count)
                dst = ring[:, i % SLOTS, :] if wide else blk(i)
                sp.dma_start(dst, s).then_inc(sem(f"block_in{i % SLOTS}"), 16)

            sp.dma_start(c_cols[:, 0, :], A["c"].rearrange("a (p c) -> p (a c)", c=KC)).then_inc(sem("c_in"), 16)
            sp.dma_start(c_cols[:, 1, :], A["c_ctx"].rearrange("(p c) -> p c", c=KC)).then_inc(sem("c_in"), 16)
            sp.dma_start(cst[:, :], A["consts"]).then_inc(sem("consts_in"), 16)

            def moe_stream(l):
                for b in [("g", l, 0), ("u", l, 0), ("g", l, 1), ("u", l, 1), ("d", l, 0)]:
                    load(at[b], expert_src(*b), wide=True)
                i0 = at[("g", l, 2)]
                with sp.Fori(0, NEXP // 2 - 1) as t:
                    for k, (kind, de) in enumerate([("g", 2), ("u", 2), ("d", 1), ("g", 3), ("u", 3), ("d", 2)]):
                        sp.wait_ge(sem("block_used"), i0 + k - SLOTS + 1 + SLOTS * t)
                        sp.dma_start(ring[:, (i0 + k) % SLOTS, :], expert_src(kind, l, 2 * t + de))\
                          .then_inc(sem(f"block_in{(i0 + k) % SLOTS}"), 16)
                load(at[("d", l, NEXP - 1)], expert_src("d", l, NEXP - 1), wide=True)

            def overflow_stream(l):
                i0 = at[("d", l, NEXP - 1)] + 1
                sp.wait_ge(sem("routed"), l + 1)
                n = sp.value_load(ov_n, min_val=0, max_val=MAXOV)
                with sp.If(n > 0):
                    sp.wait_ge(sem("block_used"), i0)
                    with sp.Fori(0, n) as t:
                        e = sp.value_load(ov_e[:, bass.ds(t, 1)], min_val=0, max_val=NEXP - 1)
                        for k, kind in enumerate("gud"):
                            sp.dma_start(ring[:, (i0 + k) % SLOTS, :], expert_src(kind, l, e))\
                              .then_inc(sem(f"ov_weights{l}"), 16)
                        sp.wait_ge(sem(f"ov_step{l}"), OV_STEPS * t + OV_D)
                        sp.sem_inc(sem("waits_passed"), 1)

            for b in stream[:at[("g", 0, 0)]]:
                load(at[b], src(b))
            moe_stream(0)
            overflow_stream(0)
            for b in stream[at[("d", 0, NEXP - 1)] + 1:at[("g", 1, 0)]]:
                load(at[b], src(b))
            moe_stream(1)
            overflow_stream(1)
            sp.wait_ge(sem("out_stored"), 16 * NLAT)

        @block.tensor
        def _(pe):
            def mm(o, l, r, start=True, stop=True):
                return nc.tensor.matmul(o, l, r, start=start, stop=stop)

            def ada_product(o, i):
                for c in range(KC):
                    g = c % 4
                    m = mm(o[32 * g:32 * g + 32, :], silu_c[:, c, :], blk(i)[:, c, :], c < 4, c >= 4)
                m.then_inc(sem("block_used"), 1)

            def gate_broadcast(l, s):
                b = GATE_BANK[l]
                for r in ((0, 1) if l == 0 else (0,)):
                    for h in range(2):
                        k = gate_unit(l, s, r, h)
                        if k >= 2:
                            pe.wait_ge(sem("gate_taken"), k - 1)
                        if k in (0, 4, 8, 10):
                            pe.wait_ge(sem("gate_bias_in"), 32 * (l + 1))
                        mm(ps[:, b + h, :], cst[:, C_SEL + r:C_SEL + r + 1].to_broadcast([P, P]),
                           modrow[:, s % 2, h * 512:(h + 1) * 512], True, False)
                        m = mm(ps[:, b + h, :], cst[0:1, C_ONE:C_ONE + P],
                               bias_row[:, s // 3, h * 512:(h + 1) * 512], False, True)
                        m.then_inc(sem("gate_rows"), 1)

            def mod_columns(o, b):
                for c in range(KC):
                    m = mm(o[:, 2 * c:2 * c + 2], modrow[:, b, c::KC], cst[:, C_SEL:C_SEL + 2])
                m.then_inc(sem("mod_cols"), 1)

            def ada0(sections):
                for s in sections:
                    first = 0 if s < 2 else 4
                    for h in range(2):
                        n = 2 * s + h
                        i = at["ada", 0, n]
                        arrived(pe, i)
                        if n >= 2:
                            pe.wait_ge(sem("ada_added"), n - 1)
                        ada_product(ps[:, first + n % 2, :], i)
                    pe.wait_ge(sem("ada_added"), 2 * s + 2)
                    k = {0: 0, 1: 1, 2: 2, 3: 2, 4: 3, 5: 4}[s]
                    if k >= 1:
                        pe.wait_ge(sem("mod_taken"), k)
                    if s in (2, 5):
                        gate_broadcast(0, s)
                    else:
                        if s == 3:
                            pe.wait_ge(sem("gate_taken"), 4)
                        mod_columns(ps[:, 2 if s < 2 else 6, :], s % 2)

            def ada1(pair):
                for q in range(2):
                    for h in range(2):
                        m = 4 * pair + 2 * q + h
                        i = at["ada", 1, 2 * ADA1[2 * pair + q] + h]
                        arrived(pe, i)
                        if m >= 2:
                            pe.wait_ge(sem("ada_added"), 12 + m - 1)
                        if pair and m % 4 == 0:
                            pe.wait_ge(sem("mod_taken"), 4 + 2 * pair)
                        ada_product(ps[:, 4 + h, :], i)
                if pair < 2:
                    pe.wait_ge(sem("ada_added"), 12 + 4 * pair + 4)
                    for q in range(2):
                        mod_columns(ps[:, 4, 16 * q:16 * q + 16], q)

            def norm(l, w):
                k, n = NORM[l, w]
                for j in range(n):
                    q = NBASE[k] + j
                    pe.wait_ge(sem("xn_ready"), q + 1)
                    for h in range(2):
                        b = (2 * j + h) % 4
                        if q >= 2:
                            pe.wait_ge(sem("hT_act" if h == 0 else "hT_dve"), q - 1)
                        for cc in range(4):
                            m = nc.tensor.transpose(ps[:, b, cc * P:(cc + 1) * P], xn_of(k)[:, j % 2, 4 * h + cc::KC], ident)
                        m.then_inc(sem("xnT"), 1)
                pe.wait_ge(sem("hT_act"), NBASE[k] + n)
                pe.wait_ge(sem("hT_dve"), NBASE[k] + n)

            def even_in():
                for u, (kind, n) in enumerate(UNITS):
                    b = u % 4
                    if u >= 4:
                        eng, c = taken_count(u - 4)
                        pe.wait_ge(sem("proj_taken_" + eng), c)
                    if (kind, n) == ("ca", 0):
                        ada0(range(2, 3))
                    if (kind, n) == ("qk", 0):
                        ada0(range(3, 6))
                        pe.wait_ge(sem("small_in"), 16 * N_SMALL)
                        for i in range(NPT):
                            m = mm(ps[:, 4, 64 * i:64 * i + 35], par_rows[:, i * P:(i + 1) * P], cst[0:35, C_ID:C_ID + 35])
                        m.then_inc(sem("par_ps"), 1)
                    if kind == "z":
                        pe.wait_ge(sem("small_in"), 16 * N_SMALL)
                        for c in range(KC):
                            m = mm(ps[0:32, b, :], w_z[:, c, :], hT[:, c, :], c == 0, c == KC - 1)
                        m.then_inc(sem("proj"), 1)
                        continue
                    i = at[("ein", 0, kind)]
                    if n == 0:
                        arrived(pe, i)
                    for c in range(KC):
                        if kind == "v":
                            m = mm(ps[:, b, :], hT[:, c, n * P:(n + 1) * P], blk(i)[:, c, :], c == 0, c == KC - 1)
                        else:
                            m = mm(ps[:, b, :], blk(i)[:, c, n * P:(n + 1) * P], hT[:, c, :], c == 0, c == KC - 1)
                    m.then_inc(sem("block_used" if n == 3 else "proj"), 1)
                    if (kind, n) == ("v", 3):
                        pe.wait_ge(sem("z_ready"), 2)
                        pe.wait_ge(sem("gate_taken"), 8)
                        pe.wait_ge(sem("conv_done"), 1)
                        for j in range(NT):
                            m = mm(ps[:, 4 + j, :], z_all[:, j * P:(j + 1) * P], dec_w)
                            m.then_inc(sem("gate_lin"), 1)

            def conv_norm():
                eng, c = taken_count(len(UNITS) - 1)
                pe.wait_ge(sem("proj_taken_" + eng), c)
                pe.wait_ge(sem("conv_done"), NPT * TAPS)
                for i in range(NPT):
                    m = mm(ps[:, 0, :], ones, mix[:, 4 + i, :], i == 0, i == NPT - 1)
                m.then_inc(sem("cn_sum"), 1)
                pe.wait_ge(sem("cn_sq"), NPT)
                for i in range(NPT):
                    m = mm(ps[:, 1, :], ones, sq4[:, i, :], i == 0, i == NPT - 1)
                m.then_inc(sem("cn_sum"), 1)

            def gla():
                pe.wait_ge(sem("la_ready"), NT)
                for pt in range(2):
                    for d in range(2):
                        for j in range(NT):
                            m = mm(ps[:, 4 + 2 * pt + d, j * P:(j + 1) * P],
                                   la[:, j, d * 256 + pt * P:d * 256 + pt * P + P],
                                   cst[:, (C_LO, C_UP)[d]:(C_LO, C_UP)[d] + P])
                        m.then_inc(sem("cum"), 1)
                pe.wait_ge(sem("cn_scaled"), NPT)
                for pt in range(2):
                    if pt:
                        pe.wait_ge(sem("o_taken"), 2)
                    for d in range(2):
                        pe.wait_ge(sem("ke_ready"), 2 * pt + d + 1)
                        for j in range(NT):
                            m = nc.tensor.transpose(ps[:, 2 + d, j * P:(j + 1) * P], k_e[:, d, j * P:(j + 1) * P], ident)
                        m.then_inc(sem("keT"), 1)
                    if pt:
                        pe.wait_ge(sem("att_masked"), 4)
                    for d in range(2):
                        pe.wait_ge(sem("ketok_ready"), 2 * pt + (1 if d == 0 else 2))
                        for n in range(NCH):
                            lo = CHUNK * (n % 2)
                            for hh in range(2):
                                m = mm(ps[64 * hh:64 * hh + 64, 2 * d + n % 2, (n // 2) * P:(n // 2 + 1) * P],
                                       k_etok[lo:lo + 64, d, n // 2, 64 * hh:64 * hh + 64],
                                       v_tok[lo:lo + 64, n // 2, (2 * pt + hh) * P:(2 * pt + hh + 1) * P])
                        m.then_inc(sem("kv_sum"), 1)
                    ada1(2 * pt)
                    pe.wait_ge(sem("state"), 14 * (pt + 1))
                    pe.wait_ge(sem("qk_ready"), 4 * (pt + 1))
                    for hh in range(2):
                        lo = 64 * hh
                        if hh:
                            pe.wait_ge(sem("att_masked"), 4 * pt + 2)
                        for d in range(2):
                            for j in range(NT):
                                m = mm(ps[:, d, j * P:(j + 1) * P], k_t[lo:lo + 64, d, j * P:(j + 1) * P],
                                       q_t[lo:lo + 64, d, j * P:(j + 1) * P])
                            m.then_inc(sem("att"), 1)
                    for hh in range(2):
                        lo = 64 * hh
                        pe.wait_ge(sem("att_masked"), 4 * pt + 2 * hh + 2)
                        for j in range(NT):
                            todo = [(ps[:, 2 + hh, j * P:(j + 1) * P], v_tok[:, j, (2 * pt + hh) * P:(2 * pt + hh + 1) * P],
                                     att_sum[:, hh, j * P:(j + 1) * P])]
                            for d in range(2):
                                for n in (2 * j, 2 * j + 1):
                                    k = SEQ[d].index(n)
                                    if k:
                                        todo.append((ps[:, 2 + hh, n * CHUNK:(n + 1) * CHUNK],
                                                     states[lo:lo + 64, d, k - 1, :],
                                                     q_t[lo:lo + 64, d, n * CHUNK:(n + 1) * CHUNK]))
                            for k, (o, l, r) in enumerate(todo):
                                m = nc.tensor.matmul(o, l, r, start=(k == 0), stop=(k == len(todo) - 1),
                                                     skip_group_check=True)
                        m.then_inc(sem("o_sum"), 1)
                    if pt == 0:
                        ada1(1)
                pe.wait_ge(sem("ada_added"), 24)
                for h in range(4):
                    pe.wait_ge(sem("o_sq"), h + 1)
                    mm(ps[:, 4 + h, :], ones, (qT if h % 2 == 0 else kT)[:, h // 2, :]).then_inc(sem("o_sumsq"), 1)

            def out_proj(l, blocks, operand, n_tiles, base):
                for h in range(2):
                    i = blocks[h]
                    arrived(pe, i)
                    for j in range(n_tiles):
                        u = n_tiles * h + j
                        if u >= 4:
                            pe.wait_ge(sem("res_taken"), base + u - 3)
                        for c in range(KC):
                            m = mm(ps[:, u % 4, :], operand(c, j), blk(i)[:, c, :], c == 0, c == KC - 1)
                        m.then_inc(sem("block_used" if j == n_tiles - 1 else "res_ps"), 1)

            def even_out():
                pe.wait_ge(sem("conv_ready"), NPT)
                pe.wait_ge(sem("o_taken"), 4)
                i = at["eout", 0, 0]
                arrived(pe, i)
                for c in (4, 5, 6, 7, 0, 1, 2, 3):
                    if c < 4:
                        pe.wait_ge(sem("mix_ready"), c + 1)
                    for j in range(NT):
                        m = nc.tensor.matmul(ps[:, j, :], mix[:, c, j * P:(j + 1) * P], blk(i)[:, c, :], start=(c == 4),
                                             stop=(c == 3), skip_group_check=True)
                        if c == 3:
                            m.then_inc(sem("block_used" if j == NT - 1 else "res_ps"), 1)
                i = at["eout", 0, 1]
                arrived(pe, i)
                for j in range(NT):
                    pe.wait_ge(sem("res_taken"), j + 1)
                    for c in range(KC):
                        m = mm(ps[:, j, :], mix[:, c, j * P:(j + 1) * P], blk(i)[:, c, :], c == 0, c == KC - 1)
                    m.then_inc(sem("block_used" if j == NT - 1 else "res_ps"), 1)

            def rows_and_router(l):
                k, n = NORM[l, 1]

                def rows(tiles):
                    for j in tiles:
                        q = NT * l + j
                        if j >= 2:
                            pe.wait_ge(sem("h2_act"), q - 1)
                        for h in range(2):
                            for cc in range(4):
                                m = nc.tensor.transpose(ps[:, 4 + (2 * j + h) % 4, cc * P:(cc + 1) * P],
                                                        hT[:, 4 * h + cc, j * P:(j + 1) * P], ident)
                        m.then_inc(sem("h2_ps"), 1)

                pe.wait_ge(sem("router_in"), 64 * (l + 1))
                for c in range(KC):
                    g = c % 4
                    m = mm(ps[32 * g:32 * g + 32, 0, 0:n * P], w_rt[:, 32 * c:32 * c + 32], hT[:, c, 0:n * P],
                           c < 4, c >= 4)
                m.then_inc(sem("logits_ps"), 1)
                pe.wait_ge(sem("logitsT"), l + 1)
                for j in range(n):
                    m = mm(ps[:, 3, 32 * j:32 * j + 20], logitsT[:, j * P:(j + 1) * P], cst[:, C_SUM:C_SUM + 20])
                m.then_inc(sem("logits"), 1)
                rows(range(min(n, 2)))
                mm(ps[:, 2, 0:P], ones, cst[:, C_TRI:C_TRI + P])
                pe.wait_ge(sem("chosen"), l + 1)
                M = R["MM"]
                for j in range(n):
                    for jj in range(j):
                        mm(ps[:, 1, 16 * j:16 * j + 16], ones, M[:, 16 * jj:16 * jj + 16], jj == 0, False)
                    mm(ps[:, 1, 16 * j:16 * j + 16], cst[:, C_TRI:C_TRI + P], M[:, 16 * j:16 * j + 16], j == 0, True)
                for j in range(n):
                    m = mm(ps[:, 1, 64:80], ones, M[:, 16 * j:16 * j + 16], j == 0, j == n - 1)
                m.then_inc(sem("ranks"), 1)
                rows(range(2, n))
                pe.wait_ge(sem("slots_ready"), l + 1)
                for k in range(2 * n):
                    m = mm(ps[:, 3, 0:NTL], slot_hot[:, k, :], tile_hot[:, k * NTL:(k + 1) * NTL], k == 0, k == 2 * n - 1)
                m.then_inc(sem("idx_ps"), 1)

            def do_xt(l, p):
                n = CAP[l]
                for c in range(KC):
                    m = nc.tensor.transpose(ps[:, 3 + c // 4, (c % 4) * n:(c % 4 + 1) * n], xg[0:n, p, c * P:(c + 1) * P],
                                            ident[0:n, 0:n])
                return m

            def do_product(l, p, bank, w):
                for c in range(KC):
                    if l == 0:
                        m = mm(ps[:, bank, :], xgT[:, p, c, :], w[:, c, :], c == 0, c == KC - 1)
                        continue
                    wv = w[:, c, :].rearrange("p (i k) -> p i k", k=4)
                    for g in range(2):
                        m = mm(ps[64 * g:64 * g + 64, bank, 0:256], xgT[:, p, c, 0:64], wv[:, :, 2 * g:2 * g + 2],
                               c == 0, c == KC - 1)
                return m

            def do_hidden_t(l, p):
                if l == 0:
                    for c in range(HC):
                        m = nc.tensor.transpose(ps[:, 2, c * P:(c + 1) * P], hid[:, p, c::HC], ident)
                else:
                    for c in range(2):
                        m = nc.tensor.transpose(ps[:, 2, c * P:(c + 1) * P], hid[:, p, c:256:2], ident)
                return m

            def do_down(l, p, w):
                if l == 0:
                    for h in range(2):
                        for c in range(HC):
                            m = mm(ps[:, 5 + h, :], hidT[:, p, c, :], w[:, c, h * 512:(h + 1) * 512], c == 0, c == HC - 1)
                    return m
                for c in range(HC):
                    for h in range(2):
                        m = mm(ps[64 * h:64 * h + 64, 5 + h, :], hidT[:, p, c % 2, 64 * (c // 2):64 * (c // 2) + 64],
                               w[:, c, h * 512:(h + 1) * 512], c == 0, c == HC - 1)
                return m

            def xt(l, e, p):
                pe.wait_ge(sem(f"xg_in{p}"), 16 * (8 * l + 1) + 8 * (e - p))
                if not (isinstance(e, int) and e == 0 and l == 0):
                    pe.wait_ge(sem("xgT_act"), NEXP * l + e)
                    pe.wait_ge(sem("xgT_dve"), NEXP * l + e)
                if l == 1:
                    pe.sem_inc(sem("waits_passed"), 1)
                do_xt(l, p).then_inc(sem("xgT_ps"), 1)

            def gate_up(l, e, p, i, t, up):
                pe.wait_ge(sem(f"block_in{i % SLOTS}"), 16 * (i // SLOTS + 1) + 16 * t)
                if not up:
                    pe.wait_ge(sem("xgT_act"), NEXP * l + e + 1)
                    pe.wait_ge(sem("xgT_dve"), NEXP * l + e + 1)
                if not (isinstance(e, int) and e == 0 and l == 0):
                    pe.wait_ge(sem("hid_ready" if up else "silu_done"), NEXP * l + e)
                do_product(l, p, 1 if up else 0, blk(i)).then_inc(sem("block_used"), 1)

            def hidden_t(l, e, p):
                pe.wait_ge(sem("hid_ready"), NEXP * l + e + 1)
                if not (isinstance(e, int) and e == 0 and l == 0):
                    pe.wait_ge(sem("hidT_ready"), NEXP * l + e)
                do_hidden_t(l, p).then_inc(sem("hidT_ps"), 1)

            def down(l, e, p, i, t):
                pe.wait_ge(sem(f"block_in{i % SLOTS}"), 16 * (i // SLOTS + 1) + 16 * t)
                pe.wait_ge(sem("hidT_ready"), NEXP * l + e + 1)
                if not (isinstance(e, int) and e == 0 and l == 0):
                    pe.wait_ge(sem("y_act"), NEXP * l + e)
                    pe.wait_ge(sem("y_dve"), NEXP * l + e)
                wd = ring[:, i % SLOTS, :].rearrange("p (c n) -> p c n", c=HC)
                do_down(l, p, wd).then_inc(sem("block_used"), 1)

            def experts(l):
                xt(l, 0, 0)
                gate_up(l, 0, 0, at["g", l, 0], 0, False)
                gate_up(l, 0, 0, at["u", l, 0], 0, True)
                xt(l, 1, 1)

                def step(e, p, i, t, last=False):
                    gate_up(l, e, p, i, t, False)
                    hidden_t(l, e - 1, 1 - p)
                    gate_up(l, e, p, i + 1, t, True)
                    if not last:
                        xt(l, e + 1, 1 - p)
                    down(l, e - 1, 1 - p, i + 2, t)
                step(1, 1, at["g", l, 1], 0)
                with pe.Fori(0, NEXP // 2 - 2) as t:
                    step(2 * t + 2, 0, at["g", l, 2], t)
                    step(2 * t + 3, 1, at["g", l, 3], t)
                step(NEXP - 2, 0, at["g", l, NEXP - 2], 0)
                step(NEXP - 1, 1, at["g", l, NEXP - 1], 0, last=True)
                hidden_t(l, NEXP - 1, 1)
                down(l, NEXP - 1, 1, at["d", l, NEXP - 1], 0)

            def overflow(l):
                i0 = at[("d", l, NEXP - 1)] + 1
                n = pe.value_load(ov_n, min_val=0, max_val=MAXOV)
                with pe.If(n > 0):
                    with pe.Fori(0, n) as t:
                        pe.wait_ge(sem(f"ov_xg{l}"), 16 * t + 16)
                        if l == 1:
                            pe.sem_inc(sem("waits_passed"), 1)
                        do_xt(l, 0).then_inc(sem(f"ov_step{l}"), 1)
                        pe.wait_ge(sem(f"ov_step{l}"), OV_STEPS * t + OV_XGT)
                        pe.wait_ge(sem(f"ov_weights{l}"), 48 * t + 48)
                        do_product(l, 0, 0, blk(i0))
                        do_product(l, 0, 1, blk(i0 + 1)).then_inc(sem(f"ov_step{l}"), 1)
                        pe.wait_ge(sem(f"ov_step{l}"), OV_STEPS * t + OV_HID)
                        do_hidden_t(l, 0).then_inc(sem(f"ov_step{l}"), 1)
                        pe.wait_ge(sem(f"ov_step{l}"), OV_STEPS * t + OV_HIDT)
                        wd = ring[:, (i0 + 2) % SLOTS, :].rearrange("p (c n) -> p c n", c=HC)
                        do_down(l, 0, wd).then_inc(sem(f"ov_step{l}"), 1)

            def odd_mixer():
                i = at["oin", 0, 2]
                arrived(pe, i)
                for u, (kind, j) in enumerate(OUNITS):
                    i = at["oin", 0, {"kv": 2, "q0": 0, "q1": 1}[kind]]
                    if j == 0:
                        arrived(pe, i)
                    if u >= 4:
                        pe.wait_ge(sem("oproj_taken"), u - 3)
                    for c in range(KC):
                        m = mm(ps[:, u % 4, :], hT[:, c, j * P:(j + 1) * P], blk(i)[:, c, :], c == 0, c == KC - 1)
                    m.then_inc(sem("block_used" if oproj_last(u) else "oproj"), 1)
                pe.wait_ge(sem("k_rot"), 1)
                for kv in range(KV):
                    for j in range(NT):
                        m = nc.tensor.transpose(ps[:, 4 + kv, j * P:(j + 1) * P], kv_tok[:, j, kv * HD:(kv + 1) * HD], ident)
                    m.then_inc(sem("qkT_ps"), 1)
                for h4 in range(2):
                    pe.wait_ge(sem("q_rot"), h4 + 1)
                    for j in range(NLAT):
                        b = 6 + j
                        if h4:
                            pe.wait_ge(sem("qkT_taken"), KV + j + 1)
                        for hh in range(4):
                            h = 4 * h4 + hh
                            m = nc.tensor.transpose(ps[:, b, hh * P:(hh + 1) * P], q_tok[:, j, h * HD:(h + 1) * HD], ident)
                        m.then_inc(sem("qkT_ps"), 1)
                pe.wait_ge(sem("qkT_taken"), KV + 4)
                pe.wait_ge(sem("oproj_taken"), len(OUNITS))

                def score(u):
                    h, j = u // 2, u % 2
                    if u >= 3:
                        pe.wait_ge(sem("prob_exp"), u - 2)
                    mm(ps[:, u % 3, :], qhT[:, h, j * P:(j + 1) * P], khT[:, h // 4, :]).then_inc(sem("score_ps"), 1)

                for u in range(3):
                    score(u)
                for u in range(2 * HEADS):
                    h, j = u // 2, u % 2
                    pe.wait_ge(sem("prob_ready"), u + 1)
                    if u >= 2:
                        pe.wait_ge(sem("probT_taken"), u - 1)
                    for c in range(NT):
                        m = nc.tensor.transpose(ps[:, 3 + u % 2, c * P:(c + 1) * P], prob[:, u % 2, c * P:(c + 1) * P], ident)
                    m.then_inc(sem("probT_ps"), 1)
                    if u + 3 < 2 * HEADS:
                        score(u + 3)
                    if j == 1:
                        if h >= 1:
                            pv(h - 1)
                pv(HEADS - 1)

            def pv(h):
                pe.wait_ge(sem("probT_taken"), 2 * h + 2)
                if h >= 2:
                    pe.wait_ge(sem("oh_taken"), h - 1)
                for c in range(NT):
                    m = mm(ps[:, 5 + h % 2, 0:256], kv_tok[:, c, 256 + (h // 4) * HD:256 + (h // 4 + 1) * HD],
                           probT[:, h % 2, c, :], c == 0, c == NT - 1)
                m.then_inc(sem("oh_ps"), 1)

            pe.wait_ge(sem("silu_ready"), 1)
            pe.wait_ge(sem("consts_in"), 16)
            ada0(range(2))
            pe.wait_ge(sem("mod_taken"), 2)
            norm(0, 0)
            even_in()
            conv_norm()
            gla()
            even_out()
            pe.wait_ge(sem("res_taken"), 2 * NT)
            norm(0, 1)
            rows_and_router(0)
            experts(0)
            overflow(0)
            gate_broadcast(1, 2)
            gate_broadcast(1, 5)
            pe.wait_ge(sem("gate_taken"), 12)
            pe.wait_ge(sem("combined"), NT)
            norm(1, 0)
            odd_mixer()
            pe.wait_ge(sem("oh_taken"), HEADS)
            out_proj(1, [at["oout", 0, 0], at["oout", 0, 1]], lambda c, j: ohT[:, c, j * P:(j + 1) * P], NLAT, 2 * NT)
            pe.wait_ge(sem("res_taken"), 2 * NT + 2 * NLAT)
            norm(1, 1)
            rows_and_router(1)
            experts(1)
            overflow(1)

        @block.scalar
        def _(act):
            chain = [0]

            def link(ins):
                chain[0] += 1
                ins.then_inc(sem("act_chain"), 1)
                act.wait_ge(sem("act_chain"), chain[0])

            A_ = nc.scalar.activation

            def gates(l, sections=(2, 5)):
                for s in sections:
                    for r in ((0, 1) if l == 0 else (0,)):
                        for h in range(2):
                            act.wait_ge(sem("gate_rows"), gate_unit(l, s, r, h) + 1)
                            A_(gb[:, gate_slot(l, s, r), h * 512:(h + 1) * 512], ps[:, GATE_BANK[l] + h, :], ACT.Copy)\
                                .then_inc(sem("gate_taken"), 1)

            def ada1_rows(pair):
                for q in range(2):
                    for h in range(2):
                        act.wait_ge(sem("block_used"), at["ada", 1, 2 * ADA1[2 * pair + q] + h] + 1)
                        if pair == 0:
                            act.wait_ge(sem("cum"), 4)
                        else:
                            act.wait_ge(sem("mod_cols"), 4 + 2 * pair)
                        A_(modrow[:, q, h * 512:(h + 1) * 512], ps[:, 4 + h, :], ACT.Copy).then_inc(sem("ada_added"), 1)

            def y_scaled(l, j):
                act.wait_ge(sem(f"yg_in{j}"), 32 * (l + 1))
                A_(yg[j][:, 0, :], yg[j][:, 0, :], ACT.Identity, scale=w1[:, j:j + 1])\
                    .then_inc(sem("y_scaled"), 1)

            def squares(n, count, wait):
                for j in range(n):
                    wait(j)
                    if count + j >= 1:
                        act.wait_ge(sem("sq_done"), count + j)
                    A_(ps[:, 6:8, :].rearrange("p a b -> p (a b)"), x[:, j, :], ACT.Square, accum_out=ss[:, j:j + 1])\
                        .then_inc(sem("sq_done"), 1)

            def root(k):
                act.wait_ge(sem("ms_ready"), MS[k])
                A_(rstd[:, 0:NT], ss[:, 8:8 + NT], ACT.Sqrt).then_inc(sem("root_done"), 1)

            def norm(l, w, wait=lambda j: None):
                k, n = NORM[l, w]
                squares(n, NBASE[k], wait)
                root(k)
                if k == 0:
                    act.wait_ge(sem("mod_taken"), 2)
                for j in range(n):
                    q = NBASE[k] + j
                    act.wait_ge(sem("xnT"), 2 * q + 1)
                    for cc in range(4):
                        r = 0 if j < NLAT else 1
                        ins = A_(hT[:, cc, j * P:(j + 1) * P], ps[:, (2 * j) % 4, cc * P:(cc + 1) * P], ACT.Identity,
                                 bias=modT[:, l, 2 * w, cc, r:r + 1], scale=modT[:, l, 2 * w + 1, cc, r:r + 1])
                    ins.then_inc(sem("hT_act"), 1)

            def rows(l):
                k, n = NORM[l, 1]
                for j in range(n):
                    q = NT * l + j
                    act.wait_ge(sem("h2_ps"), q + 1)
                    if j >= 2:
                        act.wait_ge(sem(f"h2_stored{j % 2}"), 16 * (j // 2))
                    b = 4 + (2 * j) % 4
                    A_(h2s[:, j % 2, :], ps[:, b:b + 2, :].rearrange("p a b -> p (a b)"), ACT.Copy)\
                        .then_inc(sem("h2_act"), 1)
                    act.wait_ge(sem("h2_act"), q + 1)
                    act.dma_start(h2_rows[j * P:(j + 1) * P, :], h2s[:, j % 2, :])\
                       .then_inc(sem(f"h2_stored{j % 2}"), 16)

            def router(l):
                act.wait_ge(sem("g_shift"), l + 1)
                A_(R["gx"][:, 0:4 * NORM[l, 1][1]], R["ge"][:, 0:4 * NORM[l, 1][1]], ACT.Exp).then_inc(sem("g_exp"), 1)
                act.wait_ge(sem("e_shift"), l + 1)
                A_(R["ex"][:, 0:NORM[l, 1][1]], R["dd"][:, 0:NORM[l, 1][1]], ACT.Exp).then_inc(sem("e_exp"), 1)

            def xgt_half(l, e, p):
                act.wait_ge(sem("xgT_ps"), NEXP * l + e + 1)
                wait_expert(act, "u", l, e - 2)
                A_(*xgt_copy(l, p, 0), ACT.Copy).then_inc(sem("xgT_act"), 1)

            def silu(l, e, p):
                wait_expert(act, "g", l, e)
                if not (isinstance(e, int) and e < 2 and l == 0):
                    act.wait_ge(sem("hidT_ps"), NEXP * l + e - 1)
                A_(hid[:, p, 0:hid_width(l)], ps[:, 0, 0:hid_width(l)], ACT.Silu).then_inc(sem("silu_done"), 1)

            def y_half(l, e, p):
                wait_expert(act, "d", l, e)
                y_free(act, l, e, p)
                A_(*y_copy(l, p, 0), ACT.Copy).then_inc(sem("y_act"), 1)
                act.wait_ge(sem("y_act"), NEXP * l + e + 1)
                act.wait_ge(sem("y_dve"), NEXP * l + e + 1)
                store_y(l, e, p, sem(f"y_stored{p}"))

            def experts(l):
                xgt_half(l, 0, 0)
                silu(l, 0, 0)
                xgt_half(l, 1, 1)

                def step(e, p, last=False):
                    silu(l, e, p)
                    if not last:
                        xgt_half(l, e + 1, 1 - p)
                    y_half(l, e - 1, 1 - p)
                step(1, 1)
                with act.Fori(0, NEXP // 2 - 2) as t:
                    step(2 * t + 2, 0)
                    step(2 * t + 3, 1)
                step(NEXP - 2, 0)
                step(NEXP - 1, 1, last=True)
                y_half(l, NEXP - 1, 1)

            def overflow(l):
                n = act.value_load(ov_n, min_val=0, max_val=MAXOV)
                for p in range(2):
                    act.wait_ge(sem(f"y_stored{p}"), 128 if l == 0 else 128 + 256)
                with act.If(n > 0):
                    with act.Fori(0, n) as t:
                        act.wait_ge(sem(f"ov_step{l}"), OV_STEPS * t + OV_GU)
                        A_(hid[:, 0, 0:hid_width(l)], ps[:, 0, 0:hid_width(l)], ACT.Silu).then_inc(sem(f"ov_step{l}"), 1)
                        act.wait_ge(sem(f"ov_step{l}"), OV_STEPS * t + OV_Y)
                        store_y(l, t + NEXP, 0, sem(f"ov_stored{l}"))
                        act.wait_ge(sem(f"ov_stored{l}"), 16 * (l + 1) * t + 16 * (l + 1))
                act.sem_inc(sem("y_complete"), 1)

            def even_in():
                for u, (kind, n) in enumerate(UNITS):
                    if kind == "ca":
                        if n == 0:
                            gates(0, (2,))
                        if n == 3:
                            gates(0, (5,))
                        continue
                    wait_proj(act, u)
                    b = ps[:, u % 4, :]
                    if kind == "cg":
                        ins = A_(mix[:, 4 + n, :], b, ACT.Sigmoid)
                    elif kind == "qk":
                        ins = A_((qT if n < 2 else kT)[:, n % 2, :], b, ACT.Copy, scale=float(DK) ** -0.5 if n < 2 else 1.0)
                    elif kind == "z":
                        ins = A_(z_all[0:32, :], ps[0:32, u % 4, :], ACT.Copy)
                    elif kind == "v":
                        ins = A_(v_tok[:, n, :], b, ACT.Copy)
                    else:
                        ins = A_(rT[:, n, :], b, ACT.Silu)
                    ins.then_inc(sem("proj_taken_act"), 1)
                    if kind == "z":
                        act.wait_ge(sem("proj_taken_act"), taken_count(u)[1])
                        act.sem_inc(sem("z_ready"), 1)
                    if (kind, n) == ("v", 3):
                        for j in range(NT):
                            act.wait_ge(sem("gate_lin"), j + 1)
                            A_(la[:, j, :], ps[:, 4 + j, :], ACT.Abs).then_inc(sem("la_act"), 1)
                        for k, (f, s, bias) in enumerate(((ACT.Exp, -1.0, 0.0), (ACT.Ln, 1.0, 1.0))):
                            for j in range(NT):
                                act.wait_ge(sem("la_act"), NT * k + j + 1)
                                A_(la[:, j, :], la[:, j, :], f, scale=s, bias=cst[:, C_ONE:C_ONE + 1] if bias else 0.0)\
                                    .then_inc(sem("la_act"), 1)

            def conv_norm():
                for i in range(NPT):
                    act.wait_ge(sem("cn_centred"), i + 1)
                    A_(sq4[:, i, :], mix[:, 4 + i, :], ACT.Square).then_inc(sem("cn_sq"), 1)
                act.wait_ge(sem("cn_sum"), 2)
                A_(ps[:, 2, :], ps[:, 1, :], ACT.Sqrt, scale=1.0 / CONV_CH, bias=eps).then_inc(sem("cn_root"), 1)
                for i in range(NPT):
                    act.wait_ge(sem("cn_scaled"), i + 1)
                    A_(mix[:, 4 + i, :], mix[:, 4 + i, :], ACT.Silu, scale=cpar[:, i, 32:33], bias=cpar[:, i, 33:34])\
                        .then_inc(sem("conv_ready"), 1)

            def gla():
                for pt in range(2):
                    for d in range(2):
                        act.wait_ge(sem("cum"), 2 * pt + d + 1)
                        if pt:
                            act.wait_ge(sem("state"), 14)
                        cum = ps[:, 4 + 2 * pt + d, :]
                        end = cum.rearrange("p (n t) -> p n t", t=CHUNK)[:, :, CHUNK - 1 if d == 0 else 0]
                        A_(lastS[:, d, :], end, ACT.Copy).then_inc(sem("last_ready"), 1)
                        A_(dec[:, d, :], end, ACT.Exp, scale=1.0 / 16).then_inc(sem("dec_ready"), 1)
                    if pt:
                        act.wait_ge(sem("o_sum"), 2)
                    for d in range(2):
                        cum = ps[:, 4 + 2 * pt + d, :]
                        A_(q_t[:, d, :], cum, ACT.Exp, scale=1.0 / 16).then_inc(sem("qk_exp"), 1)
                        A_(k_t[:, d, :], cum, ACT.Exp, scale=-1.0 / 16).then_inc(sem("qk_exp"), 1)
                    if pt:
                        ada1_rows(1)
                    for d in range(2):
                        act.wait_ge(sem("ke_diff"), 2 * pt + d + 1)
                        A_(k_e[:, d, :], k_e[:, d, :], ACT.Exp, scale=1.0 / 16).then_inc(sem("ke_exp"), 1)
                    for d in range(2):
                        act.wait_ge(sem("keT"), 2 * pt + d + 1)
                        A_(k_etok[:, d, :, :].rearrange("p j n -> p (j n)"), ps[:, 2 + d, :], ACT.Copy)\
                            .then_inc(sem("ketok_ready"), 1)
                    ada1_rows(2 * pt)
                    for hh in range(2):
                        h = 2 * pt + hh
                        act.wait_ge(sem("o_sum"), h + 1)
                        if h == 0:
                            act.wait_ge(sem("cum"), 4)
                        A_(mix[:, h, :], ps[:, 2 + hh, :], ACT.Copy).then_inc(sem("o_copied"), 1)
                        A_((qT if hh == 0 else kT)[:, pt, :], ps[:, 2 + hh, :], ACT.Square).then_inc(sem("o_sq"), 1)
                        act.wait_ge(sem("o_sq"), h + 1)
                        act.wait_ge(sem("o_copied"), h + 1)
                        act.sem_inc(sem("o_taken"), 1)
                for h in range(4):
                    act.wait_ge(sem("o_sumsq"), h + 1)
                    A_((qT if h % 2 == 0 else kT)[:, h // 2, :], ps[:, 4 + h, :], ACT.Sqrt, scale=1.0 / DV, bias=eps)\
                        .then_inc(sem("o_root"), 1)

            def odd_mixer():
                for u, (kind, j) in enumerate(OUNITS):
                    wait_oproj(act, u)
                    dst = kv_tok[:, j, :] if kind == "kv" else q_tok[:, j, (0 if kind == "q0" else 512):][:, 0:512]
                    A_(dst, ps[:, u % 4, :], ACT.Copy).then_inc(sem("oproj_taken"), 1)
                    if u == NT - 1:
                        act.wait_ge(sem("oproj_taken"), NT)
                        A_(rt[:, 0:2, :].rearrange("p a (b c) -> p (a b) c", c=256), kv_tok[:, :, 0:256], ACT.Square)\
                            .then_inc(sem("k_sq"), 1)
                        act.wait_ge(sem("ms_ready"), 4)
                        A_(rstd[:, 0:8], ss[:, 8:16], ACT.Sqrt).then_inc(sem("root_done"), 1)
                    elif u in (NT + 1, NT + 3):
                        half = (u - NT) // 2
                        act.wait_ge(sem("oproj_taken"), u + 1)
                        act.wait_ge(sem("k_rot"), 1) if half == 0 else act.wait_ge(sem("q_rot"), 1)
                        A_(rt[:, 0:2, :], q_tok[:, :, 512 * half:512 * half + 512], ACT.Square).then_inc(sem("q_sq"), 1)
                        act.wait_ge(sem("ms_ready"), 5 + half)
                        A_(rstd[:, 0:8], ss[:, 8:16], ACT.Sqrt).then_inc(sem("root_done"), 1)
                for kv in range(KV):
                    act.wait_ge(sem("qkT_ps"), kv + 1)
                    A_(khT[:, kv, :], ps[:, 4 + kv, :], ACT.Copy).then_inc(sem("qkT_taken"), 1)
                for h4 in range(2):
                    for j in range(NLAT):
                        act.wait_ge(sem("qkT_ps"), KV + 2 * h4 + j + 1)
                        A_(qhT[:, 4 * h4:4 * h4 + 4, j * P:(j + 1) * P],
                           ps[:, 6 + j, :].rearrange("p (a b) -> p a b", a=4), ACT.Copy).then_inc(sem("qkT_taken"), 1)
                scale = float(HD) ** -0.5
                for u in range(2 * HEADS):
                    act.wait_ge(sem("neg_max"), u + 1)
                    if u >= 2:
                        act.wait_ge(sem("probT_ps"), u - 1)
                    A_(prob[:, u % 2, :], ps[:, u % 3, :], ACT.Exp, bias=ss[:, u % 4:u % 4 + 1], scale=scale,
                       accum_out=rstd[:, u % 4:u % 4 + 1]).then_inc(sem("prob_exp"), 1)
                    if u >= 2:
                        prob_t(u - 2)
                    if u % 2 == 0 and u >= 4:
                        head_out((u - 4) // 2)
                prob_t(2 * HEADS - 2)
                head_out(HEADS - 2)
                prob_t(2 * HEADS - 1)
                head_out(HEADS - 1)

            def prob_t(v):
                h, j = v // 2, v % 2
                act.wait_ge(sem("probT_ps"), v + 1)
                if h >= 2:
                    act.wait_ge(sem("oh_ps"), h - 1)
                A_(probT[:, h % 2, :, j * P:(j + 1) * P], ps[:, 3 + v % 2, :].rearrange("p (c n) -> p c n", c=NT), ACT.Copy)\
                    .then_inc(sem("probT_taken"), 1)

            def head_out(h):
                act.wait_ge(sem("oh_ps"), h + 1)
                A_(ohT[:, h, :], ps[:, 5 + h % 2, 0:256], ACT.Copy).then_inc(sem("oh_taken"), 1)

            for j in range(NT):
                src = A["x"] if j < NLAT else A["ctx"]
                act.dma_start(x[:, j, :], src[0, (j % 2) * P:(j % 2 + 1) * P, :]).then_inc(sem(f"x_in{j}"), 16)
            act.wait_ge(sem("c_in"), 32)
            act.wait_ge(sem("silu_zero"), 1)
            A_(silu_c[:, :, 0:2], c_cols[:, :, :].rearrange("p r c -> p c r"), ACT.Silu).then_inc(sem("silu_ready"), 1)
            norm(0, 0, lambda j: act.wait_ge(sem(f"x_in{j}"), 16))
            even_in()
            conv_norm()
            gla()
            norm(0, 1, lambda j: act.wait_ge(sem("x_added"), NT + j + 1))
            rows(0)
            router(0)
            experts(0)
            overflow(0)
            gates(1, (2,))
            y_scaled(0, 0)
            y_scaled(0, 1)
            gates(1, (5,))
            y_scaled(0, 2)

            def combined(j):
                act.wait_ge(sem("combined"), j + 1)
                if j == 1:
                    y_scaled(0, 3)
            norm(1, 0, combined)
            odd_mixer()
            norm(1, 1, lambda j: act.wait_ge(sem("x_added"), 2 * NT + NLAT + j + 1))
            rows(1)
            router(1)
            experts(1)
            overflow(1)
            y_scaled(1, 0)
            y_scaled(1, 1)
            squares(NLAT, NBASE[3] + NLAT, lambda j: act.wait_ge(sem("combined"), NT + j + 1))
            act.wait_ge(sem("ms_ready"), 8)
            A_(rstd[:, 0:NT], ss[:, 8:8 + NT], ACT.Sqrt).then_inc(sem("root_done"), 1)
            for j in range(NLAT):
                act.wait_ge(sem("final_ready"), j + 1)
                act.dma_start(out[0, j * P:(j + 1) * P, :], x[:, j, :]).then_inc(sem("out_stored"), 16)

        @block.vector
        def _(dve):
            chain = [0]

            def link(ins):
                chain[0] += 1
                ins.then_inc(sem("dve_chain"), 1)
                dve.wait_ge(sem("dve_chain"), chain[0])

            V = nc.vector

            def mod_column(l, k, cols):
                V.scalar_tensor_tensor(modT[:, l, k, :, :], cols.rearrange("p (c r) -> p c r", r=2),
                                       float(k % 2), bias_cols[:, l, k, :].unsqueeze(2).to_broadcast([P, KC, 2]),
                                       ALU.add, ALU.add).then_inc(sem("mod_taken"), 1)

            def ada0(sections):
                for s in sections:
                    first = 0 if s < 2 else 4
                    for h in range(2):
                        n = 2 * s + h
                        dve.wait_ge(sem("block_used"), at["ada", 0, n] + 1)
                        if s >= 2:
                            if s - 2 in (2, 5):
                                dve.wait_ge(sem("gate_rows"), gate_unit(0, s - 2, 1, 1) + 1)
                            else:
                                dve.wait_ge(sem("mod_cols"), {0: 0, 1: 1, 3: 2, 4: 3}[s - 2] + 1)
                        V.tensor_copy(modrow[:, s % 2, h * 512:(h + 1) * 512], ps[:, first + n % 2, :]).then_inc(sem("ada_added"), 1)
                    if s not in (2, 5):
                        k = {0: 0, 1: 1, 3: 2, 4: 3}[s]
                        dve.wait_ge(sem("mod_cols"), k + 1)
                        if k == 0:
                            dve.wait_ge(sem("bias_cols0_in"), 32)
                        elif k == 2:
                            dve.wait_ge(sem("bias_cols_in"), 16 * 6)
                        mod_column(0, k, ps[:, 2 if s < 2 else 6, 0:16])

            def ada1_columns(pair):
                dve.wait_ge(sem("mod_cols"), 4 + 2 * pair + 2)
                for q in range(2):
                    mod_column(1, 2 * pair + q, ps[:, 4, 16 * q:16 * q + 16])

            def mean_square(n, width, count):
                V.tensor_scalar(ss[:, 8:8 + n], ss[:, 0:n], 1.0 / width, EPS, ALU.mult, ALU.add)\
                    .then_inc(sem("ms_ready"), 1)
                dve.wait_ge(sem("root_done"), count)
                link(V.reciprocal(rstd[:, 0:n], rstd[:, 0:n]))

            def norm(l, w):
                k, n = NORM[l, w]
                dve.wait_ge(sem("sq_done"), NBASE[k] + n)
                mean_square(n, D, MS[k])

                def half(j):
                    q = NBASE[k] + j
                    r = 0 if j < NLAT else 1
                    dve.wait_ge(sem("xnT"), 2 * q + 2)
                    for cc in range(4):
                        ins = V.tensor_scalar(hT[:, 4 + cc, j * P:(j + 1) * P], ps[:, (2 * j + 1) % 4, cc * P:(cc + 1) * P],
                                              modT[:, l, 2 * w + 1, 4 + cc, r:r + 1], modT[:, l, 2 * w, 4 + cc, r:r + 1],
                                              ALU.mult, ALU.add)
                    ins.then_inc(sem("hT_dve"), 1)
                for j in range(n):
                    if j >= 2:
                        dve.wait_ge(sem("xnT"), 2 * (NBASE[k] + j) - 2)
                    V.tensor_scalar(xn_of(k)[:, j % 2, :], x[:, j, :], rstd[:, j:j + 1], None, ALU.mult)\
                        .then_inc(sem("xn_ready"), 1)
                    if j:
                        half(j - 1)
                half(n - 1)

            def router(l):
                n = NORM[l, 1][1]
                lgv = lg.rearrange("p (j k) -> p j k", k=20)[:, 0:n, :]

                def r(name):
                    return R[name][:, 0:n]

                def r4(name):
                    return R[name][:, 0:4 * n].rearrange("p (j k) -> p j k", k=4)

                def r16(name):
                    return R[name][:, 0:16 * n].rearrange("p (j k) -> p j k", k=16)

                def b4(name):
                    return R[name][:, 0:n].unsqueeze(2).to_broadcast([P, n, 4])

                def first_one(dst, name):
                    w4 = cst[:, C_W4:C_W4 + 4].unsqueeze(1).to_broadcast([P, n, 4])
                    link(V.tensor_tensor(r4("sc"), r4(name), w4, ALU.mult))
                    link(V.tensor_reduce(r("mx"), r4("sc"), AX_X, ALU.max))
                    link(V.tensor_tensor(r4(dst), r4("sc"), b4("mx"), ALU.is_equal))

                dve.wait_ge(sem("logits_ps"), l + 1)
                V.tensor_copy(logitsT[:, 0:n * P], ps[:, 0, 0:n * P]).then_inc(sem("logitsT"), 1)
                dve.wait_ge(sem("logits"), l + 1)
                dve.wait_ge(sem("router_in"), 64 * (l + 1))
                link(V.tensor_tensor(lgv, ps[:, 3, 0:32 * n].rearrange("p (j k) -> p j k", k=32)[:, :, 0:20],
                                     r_bias.unsqueeze(1).to_broadcast([P, n, 20]), ALU.add))
                link(V.tensor_reduce(r("gm"), lgv[:, :, 0:4], AX_X, ALU.max))
                V.tensor_tensor(r4("ge"), lgv[:, :, 0:4], b4("gm"), ALU.subtract).then_inc(sem("g_shift"), 1)
                link(V.tensor_tensor(r4("eq"), lgv[:, :, 0:4], b4("gm"), ALU.is_equal))
                first_one("ohg", "eq")
                t16 = r16("tmp").rearrange("p j (g e) -> p j g e", g=4)
                link(V.tensor_tensor(t16, lgv[:, :, 4:20].rearrange("p j (g e) -> p j g e", g=4),
                                     r4("ohg").unsqueeze(3).to_broadcast([P, n, 4, 4]), ALU.mult))
                link(V.tensor_reduce(r4("el"), t16.rearrange("p j g e -> p j e g"), AX_X, ALU.add))
                link(V.tensor_reduce(r("m1"), r4("el"), AX_X, ALU.max))
                link(V.tensor_tensor(r4("eq"), r4("el"), b4("m1"), ALU.is_equal))
                first_one("oh1", "eq")
                link(V.tensor_scalar(R["e2"][:, 0:4 * n], R["oh1"][:, 0:4 * n], -3.0e38, None, ALU.mult))
                link(V.tensor_tensor(r4("e2"), r4("e2"), r4("el"), ALU.add))
                link(V.tensor_reduce(r("m2"), r4("e2"), AX_X, ALU.max))
                link(V.tensor_tensor(r4("eq"), r4("e2"), b4("m2"), ALU.is_equal))
                first_one("oh2", "eq")
                V.tensor_tensor(r("dd"), r("m2"), r("m1"), ALU.subtract).then_inc(sem("e_shift"), 1)
                def r12(name):
                    return R[name][:, 0:2 * n].rearrange("p (k j) -> p k j", k=2)

                def r32(name):
                    return R[name].rearrange("p (k j e) -> p k j e", k=2, e=16)[:, :, 0:n, :]

                def over_experts(ap):
                    return ap.unsqueeze(1).unsqueeze(1).to_broadcast([P, 2, n, 16])

                for k, o in enumerate(("oh1", "oh2")):
                    link(V.tensor_tensor(r32("M12")[:, k].rearrange("p j (g e) -> p j g e", g=4),
                                         r4("ohg").unsqueeze(3).to_broadcast([P, n, 4, 4]),
                                         r4(o).unsqueeze(2).to_broadcast([P, n, 4, 4]), ALU.mult))
                V.tensor_tensor(r16("MM"), r32("M12")[:, 0], r32("M12")[:, 1], ALU.add).then_inc(sem("chosen"), 1)
                experts_row = over_experts(cst[:, C_E:C_E + 16])
                link(V.tensor_tensor(r32("t12"), r32("M12"), experts_row, ALU.mult))
                link(V.tensor_reduce(r12("ek"), r32("t12"), AX_X, ALU.add))
                V.tensor_scalar(r12("ne"), r12("ek"), -1.0, float(NEXP - 1), ALU.mult, ALU.add)
                link(V.tensor_tensor(r32("lower"), experts_row, r12("ek").unsqueeze(3).to_broadcast([P, 2, n, 16]), ALU.is_lt))
                dve.wait_ge(sem("ranks"), l + 1)
                cap = CAP[l]
                thr = cst[:, C_THR + MAXOV * l:C_THR + MAXOV * (l + 1)].unsqueeze(1)
                cc = cmp_c.rearrange("p (e k) -> p e k", e=NEXP)
                ct = cmp_t[:, 0:2 * n * MAXOV].rearrange("p (t k) -> p t k", t=2 * n)
                ranks = ps[:, 1, 0:16 * n].rearrange("p (j e) -> p j e", e=16).unsqueeze(1).to_broadcast([P, 2, n, 16])
                V.tensor_tensor(r32("t12"), r32("M12"), ranks, ALU.mult)
                link(V.tensor_tensor(cc, ps[:, 1, 64:80].unsqueeze(2).to_broadcast([P, NEXP, MAXOV]),
                                     thr.to_broadcast([P, NEXP, MAXOV]), ALU.is_gt))
                V.tensor_reduce(r12("r12"), r32("t12"), AX_X, ALU.add)
                link(V.tensor_reduce(nov, cc, AX_X, ALU.add))
                V.tensor_tensor(r32("t12"), r32("lower"), over_experts(nov), ALU.mult)
                link(V.tensor_tensor(ct, R["r12"][:, 0:2 * n].unsqueeze(2).to_broadcast([P, 2 * n, MAXOV]),
                                     thr.to_broadcast([P, 2 * n, MAXOV]), ALU.is_ge))
                V.tensor_reduce(r12("xk"), r32("t12"), AX_X, ALU.add)
                link(V.tensor_reduce(R["kk"][:, 0:2 * n], ct, AX_X, ALU.add))
                V.scalar_tensor_tensor(r12("sl"), r12("kk"), -float(cap), r12("r12"), ALU.mult, ALU.add)
                V.tensor_tensor(r12("ke"), r12("kk"), r12("ek"), ALU.add)
                link(V.tensor_tensor(r12("xk"), r12("xk"), r12("ne"), ALU.add))
                link(V.scalar_tensor_tensor(r12("xk"), r12("kk"), 0.0, r12("xk"), ALU.is_gt, ALU.mult))
                link(V.tensor_tensor(r12("tile"), r12("xk"), r12("ke"), ALU.add))
                th = tile_hot[:, 0:2 * n * NTL].rearrange("p (t k) -> p t k", t=2 * n)
                th4 = tile_hot[:, 0:2 * n * NTL].rearrange("p (k j t) -> p k j t", k=2, t=NTL)
                V.tensor_tensor(slot_hot[:, 0:2 * n, :], ps[:, 2, 0:P].unsqueeze(1).to_broadcast([P, 2 * n, P]),
                                R["sl"][:, 0:2 * n].unsqueeze(2).to_broadcast([P, 2 * n, P]), ALU.is_equal)
                link(V.tensor_tensor(th, ps[:, 2, 0:NTL].unsqueeze(1).to_broadcast([P, 2 * n, NTL]),
                                     R["tile"][:, 0:2 * n].unsqueeze(2).to_broadcast([P, 2 * n, NTL]), ALU.is_equal))
                V.tensor_tensor(th4, th4, cst[:, C_TOK:C_TOK + n].unsqueeze(1).unsqueeze(3).to_broadcast([P, 2, n, NTL]),
                                ALU.mult).then_inc(sem("slots_ready"), 1)
                link(V.scalar_tensor_tensor(r12("py"), r12("tile"), float(cap), r12("sl"), ALU.mult, ALU.add))
                V.tensor_copy(posy.rearrange("p (k j) -> p k j", k=2)[:, :, 0:n], r12("py")).then_inc(sem("positions"), 1)
                dve.wait_ge(sem("idx_ps"), l + 1)
                V.tensor_copy(idx, ps[:, 3, 0:NTL]).then_inc(sem("idx_ready"), 1)
                dve.wait_ge(sem("g_exp"), l + 1)
                link(V.tensor_reduce(r("gs"), r4("gx"), AX_X, ALU.add))
                link(V.reciprocal(r("pg"), r("gs")))
                dve.wait_ge(sem("e_exp"), l + 1)
                link(V.tensor_scalar(r("dn"), r("ex"), 1.0, None, ALU.add))
                link(V.reciprocal(r("rd"), r("dn")))
                link(V.tensor_tensor(w1[:, 0:n], r("pg"), r("rd"), ALU.mult))
                link(V.tensor_tensor(w2[:, 0:n], w1[:, 0:n], r("ex"), ALU.mult))
                a, b = inc, inc2
                link(V.tensor_copy(a, nov))
                for d in (1, 2, 4, 8):
                    link(V.tensor_copy(b[:, 0:d], a[:, 0:d]))
                    link(V.tensor_tensor(b[:, d:16], a[:, d:16], a[:, 0:16 - d], ALU.add))
                    a, b = b, a
                link(V.tensor_copy(ov_n, a[0:1, 15:16]))
                tv = ov_t[0:1, 0:16 * MAXOV].rearrange("p (i k) -> p i k", k=16)
                te = ov_t[0:1, 16 * MAXOV:17 * MAXOV]
                link(V.tensor_tensor(tv, a[0:1, :].unsqueeze(1).to_broadcast([1, MAXOV, 16]),
                                     cst[0:1, C_OVI:C_OVI + MAXOV].unsqueeze(2).to_broadcast([1, MAXOV, 16]), ALU.is_le))
                link(V.tensor_reduce(te, tv, AX_X, ALU.add))
                link(V.tensor_scalar(te, te, float(NEXP - 1), None, ALU.min))
                V.tensor_copy(ov_e, te).then_inc(sem("routed"), 1)

            def xgt_half(l, e, p):
                dve.wait_ge(sem("xgT_ps"), NEXP * l + e + 1)
                wait_expert(dve, "u", l, e - 2)
                V.tensor_copy(*xgt_copy(l, p, 1)).then_inc(sem("xgT_dve"), 1)

            def hidden(l, e, p):
                dve.wait_ge(sem("silu_done"), NEXP * l + e + 1)
                wait_expert(dve, "u", l, e)
                hw = hid_width(l)
                V.tensor_tensor(hid[:, p, 0:hw], hid[:, p, 0:hw], ps[:, 1, 0:hw], ALU.mult).then_inc(sem("hid_ready"), 1)

            def hidden_t(l, e, p):
                dve.wait_ge(sem("hidT_ps"), NEXP * l + e + 1)
                wait_expert(dve, "d", l, e - 2)
                hw = hid_width(l)
                V.tensor_copy(hidT[:, p, :, :].rearrange("p a b -> p (a b)")[:, 0:hw], ps[:, 2, 0:hw])\
                    .then_inc(sem("hidT_ready"), 1)

            def y_half(l, e, p):
                wait_expert(dve, "d", l, e)
                y_free(dve, l, e, p)
                V.tensor_copy(*y_copy(l, p, 1)).then_inc(sem("y_dve"), 1)

            def experts(l):
                xgt_half(l, 0, 0)
                hidden(l, 0, 0)
                xgt_half(l, 1, 1)

                def step(e, p, last=False):
                    hidden_t(l, e - 1, 1 - p)
                    hidden(l, e, p)
                    if not last:
                        xgt_half(l, e + 1, 1 - p)
                    y_half(l, e - 1, 1 - p)
                step(1, 1)
                with dve.Fori(0, NEXP // 2 - 2) as t:
                    step(2 * t + 2, 0)
                    step(2 * t + 3, 1)
                step(NEXP - 2, 0)
                step(NEXP - 1, 1, last=True)
                hidden_t(l, NEXP - 1, 1)
                y_half(l, NEXP - 1, 1)

            def overflow(l):
                n = dve.value_load(ov_n, min_val=0, max_val=MAXOV)
                with dve.If(n > 0):
                    with dve.Fori(0, n) as t:
                        dve.wait_ge(sem(f"ov_step{l}"), OV_STEPS * t + OV_XT)
                        V.tensor_copy(*xgt_copy(l, 0, 0))
                        V.tensor_copy(*xgt_copy(l, 0, 1)).then_inc(sem(f"ov_step{l}"), 1)
                        dve.wait_ge(sem(f"ov_step{l}"), OV_STEPS * t + OV_SILU)
                        hw = hid_width(l)
                        V.tensor_tensor(hid[:, 0, 0:hw], hid[:, 0, 0:hw], ps[:, 1, 0:hw], ALU.mult).then_inc(sem(f"ov_step{l}"), 1)
                        dve.wait_ge(sem(f"ov_step{l}"), OV_STEPS * t + OV_HT)
                        V.tensor_copy(hidT[:, 0, :, :].rearrange("p a b -> p (a b)")[:, 0:hw], ps[:, 2, 0:hw])\
                            .then_inc(sem(f"ov_step{l}"), 1)
                        dve.wait_ge(sem(f"ov_step{l}"), OV_STEPS * t + OV_D)
                        V.tensor_copy(*y_copy(l, 0, 0))
                        V.tensor_copy(*y_copy(l, 0, 1))\
                            .then_inc(sem(f"ov_step{l}"), 1)

            def combine(l):
                for j in range(NORM[l, 1][1]):
                    dve.wait_ge(sem("y_scaled"), NT * l + j + 1)
                    slot = (2 + (0 if j < NLAT else 1)) if l == 0 else 1
                    link(V.scalar_tensor_tensor(yg[j][:, 0, :], yg[j][:, 1, :], w2[:, j:j + 1], yg[j][:, 0, :],
                                                ALU.mult, ALU.add))
                    link(V.tensor_tensor(yg[j][:, 0, :], yg[j][:, 0, :], gb[:, slot, :], ALU.mult))
                    V.tensor_tensor(x[:, j, :], x[:, j, :], yg[j][:, 0, :], ALU.add).then_inc(sem("combined"), 1)
                dve.wait_ge(sem("combined"), NT if l == 0 else NT + NLAT)

            def residual(l, n_tiles, base):
                for h in range(2):
                    for j in range(n_tiles):
                        u = n_tiles * h + j
                        slot = (0 if j < NLAT else 1) if l == 0 else 0
                        wait_res(dve, l, u)
                        V.tensor_tensor(res[:, u % 2, :], ps[:, u % 4, :], gb[:, slot, h * 512:(h + 1) * 512], ALU.mult)\
                            .then_inc(sem("res_taken"), 1)
                        dve.wait_ge(sem("res_taken"), base + u + 1)
                        V.tensor_tensor(x[:, j, h * 512:(h + 1) * 512], x[:, j, h * 512:(h + 1) * 512], res[:, u % 2, :],
                                        ALU.add).then_inc(sem("x_added"), 1)
                dve.wait_ge(sem("x_added"), base + 2 * n_tiles)

            def conv():
                for n in range(NPT):
                    u = UNITS.index(("ca", n))
                    wait_proj(dve, u)
                    dve.wait_ge(sem("proj_taken_act"), n + 1)
                    if n == 0:
                        dve.wait_ge(sem("margins"), 1)
                    V.tensor_tensor(u_in[:, n, :, HALO:HALO + 256], ps[:, u % 4, :].rearrange("p (s t) -> p s t", s=2),
                                    mix[:, 4 + n, :].rearrange("p (s t) -> p s t", s=2), ALU.mult)\
                        .then_inc(sem("proj_taken_dve"), 1)
                ada0(range(3, 6))
                dve.wait_ge(sem("par_ps"), 1)
                link(V.tensor_copy(cpar[:, :, :], ps[:, 4, 0:64 * NPT].rearrange("p (i k) -> p i k", k=64)[:, :, 0:35]))
                dve.wait_ge(sem("proj_taken_dve"), NPT)
                acc = [mix[:, 4 + n, :].rearrange("p (s t) -> p s t", s=2) for n in range(NPT)]
                for n in range(NPT):
                    V.tensor_scalar(acc[n], u_in[:, n, :, 0:256], cpar[:, n, 0:1], cpar[:, n, 31:32], ALU.mult, ALU.add)\
                        .then_inc(sem("conv_done"), 1)
                with dve.Fori(1, TAPS) as t:
                    for n in range(NPT):
                        dve.wait_ge(sem("conv_done"), NPT * t + (n - 3))
                        V.scalar_tensor_tensor(acc[n], u_in[:, n, :, bass.ds(t, 256)], cpar[:, n, bass.ds(t, 1)], acc[n],
                                               ALU.mult, ALU.add).then_inc(sem("conv_done"), 1)

            def gate_logs():
                for j in range(NT):
                    dve.wait_ge(sem("la_act"), 2 * NT + j + 1)
                    V.scalar_tensor_tensor(la[:, j, :], ps[:, 4 + j, :], 0.0, la[:, j, :], ALU.min, ALU.subtract)\
                        .then_inc(sem("la_ready"), 1)

            def conv_norm():
                dve.wait_ge(sem("cn_sum"), 1)
                for i in range(NPT):
                    V.scalar_tensor_tensor(mix[:, 4 + i, :], ps[:, 0, :], -1.0 / CONV_CH, mix[:, 4 + i, :],
                                           ALU.mult, ALU.add).then_inc(sem("cn_centred"), 1)
                dve.wait_ge(sem("cn_root"), 1)
                link(V.reciprocal(ps[:, 2, :], ps[:, 2, :]))
                dve.wait_ge(sem("cn_sq"), NPT)
                for i in range(NPT):
                    V.tensor_tensor(mix[:, 4 + i, :], mix[:, 4 + i, :], ps[:, 2, :], ALU.mult).then_inc(sem("cn_scaled"), 1)

            def gla():
                wait_proj(dve, len(UNITS) - 1)
                for pt in range(2):
                    for d in range(2):
                        dve.wait_ge(sem("last_ready"), 2 * pt + d + 1)
                        dve.wait_ge(sem("qk_exp"), 4 * pt + 2 * d + 2)
                        if pt:
                            dve.wait_ge(sem("o_sum"), 2)
                        V.tensor_tensor(k_e[:, d, :].rearrange("p (n t) -> p n t", t=CHUNK),
                                        lastS[:, d, :].unsqueeze(2).to_broadcast([P, NCH, CHUNK]),
                                        ps[:, 4 + 2 * pt + d, :].rearrange("p (n t) -> p n t", t=CHUNK), ALU.subtract)\
                            .then_inc(sem("ke_diff"), 1)
                    for d in range(2):
                        for k, (dst, src) in enumerate(((q_t, qT), (k_t, kT))):
                            dve.wait_ge(sem("qk_exp"), 4 * pt + 2 * d + k + 1)
                            V.tensor_tensor(dst[:, d, :], dst[:, d, :], src[:, pt, :], ALU.mult).then_inc(sem("qk_ready"), 1)
                    for d in range(2):
                        dve.wait_ge(sem("ke_exp"), 2 * pt + d + 1)
                        V.tensor_tensor(k_e[:, d, :], k_e[:, d, :], kT[:, pt, :], ALU.mult).then_inc(sem("ke_ready"), 1)
                    for d in range(2):
                        dve.wait_ge(sem("keT"), 2 * pt + d + 1)
                        V.memset(k_e[:, d, :], 0.0).then_inc(sem("att_zero"), 1)
                    if pt:
                        ada1_columns(1)
                    dve.wait_ge(sem("dec_ready"), 2 * pt + 2)
                    for k in range(7):
                        for d in range(2):
                            if k == 0:
                                dve.wait_ge(sem("kv_sum"), 2 * pt + d + 1)
                            n = SEQ[d][k]
                            src = ps[:, 2 * d + n % 2, (n // 2) * P:(n // 2 + 1) * P]
                            if k == 0:
                                V.tensor_copy(states[:, d, 0, :], src).then_inc(sem("state"), 1)
                            else:
                                dve.wait_ge(sem("state"), 14 * pt + 2 * k + d - 1)
                                V.scalar_tensor_tensor(states[:, d, k, :], states[:, d, k - 1, :], dec[:, d, n:n + 1], src,
                                                       ALU.mult, ALU.add).then_inc(sem("state"), 1)
                    if pt == 0:
                        ada1_columns(0)
                    for hh in range(2):
                        for d in range(2):
                            dve.wait_ge(sem("att"), 4 * pt + 2 * hh + d + 1)
                            dve.wait_ge(sem("att_zero"), 2 * pt + d + 1)
                            mask = cst[:, (C_LO, C_UP)[d]:(C_LO, C_UP)[d] + P].bitcast(U32)
                            ins = V.copy_predicated(k_e[:, d, :].rearrange("p (j n) -> p j n", j=NT),
                                                    mask.unsqueeze(1).to_broadcast([P, NT, P]),
                                                    ps[:, d, :].rearrange("p (j n) -> p j n", j=NT))
                            if d == 0:
                                ins.then_inc(sem("att_masked"), 1)
                            else:
                                link(ins)
                        V.tensor_tensor(att_sum[:, hh, :], k_e[:, 0, :], k_e[:, 1, :], ALU.add).then_inc(sem("att_masked"), 1)
                for h in range(4):
                    rs = (qT if h % 2 == 0 else kT)[:, h // 2, :]
                    dve.wait_ge(sem("o_root"), h + 1)
                    link(V.reciprocal(rs, rs))
                    link(V.tensor_tensor(mix[:, h, :], mix[:, h, :], rs, ALU.mult))
                    V.scalar_tensor_tensor(mix[:, h, :], rT[:, h, :], cpar[:, 0, 34:35], mix[:, h, :], ALU.mult, ALU.mult)\
                        .then_inc(sem("mix_ready"), 1)

            def rotate(t, j, nh):
                tv = t.rearrange("p (h k two) -> p h k two", h=nh, two=2)
                x0, x1 = tv[:, :, :, 0], tv[:, :, :, 1]
                cos = cst[:, C_COS + 64 * j:C_COS + 64 * j + 64].unsqueeze(1).to_broadcast([P, nh, 64])
                sin = cst[:, C_SIN + 64 * j:C_SIN + 64 * j + 64].unsqueeze(1).to_broadcast([P, nh, 64])
                a, b, c, d = (w[:, 64 * nh * j:64 * nh * (j + 1)].rearrange("p (h k) -> p h k", h=nh)
                              for w in (rt[:, 2, :], rt[:, 3, :], prob[:, 0, :], prob[:, 1, :]))
                V.tensor_tensor(a, x0, cos, ALU.mult)
                V.tensor_tensor(b, x1, sin, ALU.mult)
                V.tensor_tensor(c, x0, sin, ALU.mult)
                link(V.tensor_tensor(d, x1, cos, ALU.mult))
                V.tensor_tensor(x0, a, b, ALU.subtract)
                return V.tensor_tensor(x1, c, d, ALU.add)

            def heads_norm(t4, g, nj, nh, count):
                n = nj * nh
                link(V.tensor_reduce(ss[:, 0:n], rt[:, 0:2, :].rearrange("p a (b c) -> p (a b) c", c=HD), AX_X, ALU.add))
                mean_square(n, HD, count)
                rb = rstd[:, 0:n].rearrange("p (j h) -> p j h", j=nj).unsqueeze(3).to_broadcast([P, nj, nh, HD])
                link(V.tensor_tensor(t4, t4, rb, ALU.mult))
                for j in range(nj):
                    link(V.tensor_tensor(t4[:, j], t4[:, j], g.unsqueeze(1).to_broadcast([P, nh, HD]), ALU.mult))

            def odd_mixer():
                dve.wait_ge(sem("norm_g_in"), 48)
                dve.wait_ge(sem("k_sq"), 1)
                heads_norm(kv_tok[:, :, 0:256].rearrange("p j (h k) -> p j h k", h=KV), gb[:, 3, P:2 * P], NT, KV, 4)
                for j in range(NLAT):
                    ins = rotate(kv_tok[:, j, 0:256], j, KV)
                    if j == 0:
                        link(ins)
                ins.then_inc(sem("k_rot"), 1)
                for half in range(2):
                    dve.wait_ge(sem("q_sq"), half + 1)
                    qh = q_tok[:, :, 512 * half:512 * half + 512]
                    heads_norm(qh.rearrange("p j (h k) -> p j h k", h=4), gb[:, 3, 0:P], NLAT, 4, 5 + half)
                    for j in range(NLAT):
                        ins = rotate(qh[:, j, :], j, 4)
                    ins.then_inc(sem("q_rot"), 1)
                scale = float(HD) ** -0.5
                for u in range(2 * HEADS + 1):
                    if u < 2 * HEADS:
                        dve.wait_ge(sem("score_ps"), u + 1)
                        link(V.tensor_reduce(ss[:, 4 + u % 4:5 + u % 4], ps[:, u % 3, :], AX_X, ALU.max))
                        V.tensor_scalar(ss[:, u % 4:u % 4 + 1], ss[:, 4 + u % 4:5 + u % 4], -scale, None, ALU.mult)\
                            .then_inc(sem("neg_max"), 1)
                    if 1 <= u <= 2 * HEADS:
                        v = u - 1
                        dve.wait_ge(sem("prob_exp"), v + 1)
                        link(V.reciprocal(rstd[:, 4 + v % 4:5 + v % 4], rstd[:, v % 4:v % 4 + 1]))
                        V.tensor_scalar(prob[:, v % 2, :], prob[:, v % 2, :], rstd[:, 4 + v % 4:5 + v % 4], None, ALU.mult)\
                            .then_inc(sem("prob_ready"), 1)

            V.memset(silu_c[:, :, :], 0.0).then_inc(sem("silu_zero"), 1)
            ada0(range(2))
            norm(0, 0)
            ada0(range(2, 3))
            conv()
            gate_logs()
            conv_norm()
            gla()
            residual(0, NT, 0)
            norm(0, 1)
            router(0)
            experts(0)
            overflow(0)
            combine(0)
            norm(1, 0)
            odd_mixer()
            residual(1, NLAT, 2 * NT)
            norm(1, 1)
            router(1)
            experts(1)
            overflow(1)
            combine(1)
            dve.wait_ge(sem("sq_done"), NBASE[3] + 2 * NLAT)
            mean_square(NLAT, D, 8)
            for j in range(NLAT):
                V.scalar_tensor_tensor(x[:, j, :], x[:, j, :], rstd[:, j:j + 1], gb[:, 2, :], ALU.mult, ALU.mult)\
                    .then_inc(sem("final_ready"), 1)

        @block.gpsimd
        def _(pool):
            chain = [0]

            def link(ins):
                chain[0] += 1
                ins.then_inc(sem("pool_chain"), 1)
                pool.wait_ge(sem("pool_chain"), chain[0])

            G = nc.gpsimd

            def gate_bias(l):
                for k, t in enumerate((2, 5)):
                    pool.dma_start(bias_row[:, k, :], A["ada_b"][l:l + 1, t * D:(t + 1) * D]).then_inc(sem("gate_bias_in"), 16)

            def router_params(l):
                wv = w_rt.rearrange("p (c k) -> p c k", k=32)
                link(G.memset(w_rt, 0.0))
                pool.dma_start(wv[:, :, 0:4], A["moe_w_group"][l].rearrange("(p c) g -> p c g", c=KC))\
                    .then_inc(sem("router_in"), 16)
                pool.dma_start(wv[:, :, 4:20], A["moe_w_router"][l].rearrange("(p c) g e -> p c (g e)", c=KC))\
                    .then_inc(sem("router_in"), 16)
                pool.dma_start(r_bias[:, 0:4], A["moe_b_group"][l:l + 1, :].to_broadcast([P, 4])).then_inc(sem("router_in"), 16)
                pool.dma_start(r_bias[:, 4:20], A["moe_b_router"][l:l + 1].rearrange("a g e -> a (g e)").to_broadcast([P, 16]))\
                    .then_inc(sem("router_in"), 16)

            def dispatch(l):
                pool.wait_ge(sem("idx_ready"), l + 1)
                for p in range(2):
                    pool.wait_ge(sem(f"h2_stored{p}"), 8 * (NT if l == 0 else NT + NLAT))

            def gather(l, e, p):
                if not (isinstance(e, int) and e < 2 and l == 0):
                    pool.wait_ge(sem("xgT_ps"), NEXP * l + e - 1)
                ex = e if isinstance(e, int) else bass.ds(e, 1)
                G.tensor_copy(idxc[:, p:p + 1], idx[:, e:e + 1] if isinstance(e, int) else idx[:, ex])\
                    .then_inc(sem("idx_col"), 1)
                pool.wait_ge(sem("idx_col"), NEXP * l + e + 1)
                pool.sem_inc(sem("waits_passed"), 1)
                G.indirect_dma_start(xg[0:CAP[l], p, :], None, h2_rows,
                                     bass.IndirectOffsetOnAxis(ap=idxc[0:CAP[l], p:p + 1], axis=0))\
                    .then_inc(sem(f"xg_in{p}"), 16)

            def overflow(l):
                n = pool.value_load(ov_n, min_val=0, max_val=MAXOV)
                with pool.If(n > 0):
                    pool.wait_ge(sem("xg_in0"), 8 * NEXP * (l + 1))
                    pool.wait_ge(sem("xgT_ps"), NEXP * (l + 1))
                    with pool.Fori(0, n) as t:
                        G.tensor_copy(idxc[:, 0:1], idx[:, bass.ds(t + NEXP, 1)]).then_inc(sem(f"ov_col{l}"), 1)
                        pool.wait_ge(sem(f"ov_col{l}"), t + 1)
                        pool.sem_inc(sem("waits_passed"), 1)
                        G.indirect_dma_start(xg[0:CAP[l], 0, :], None, h2_rows,
                                             bass.IndirectOffsetOnAxis(ap=idxc[0:CAP[l], 0:1], axis=0)).then_inc(sem(f"ov_xg{l}"), 16)
                        pool.wait_ge(sem(f"ov_step{l}"), OV_STEPS * t + OV_Y)

            def combine(l):
                pool.wait_ge(sem("y_complete"), l + 1)
                pool.wait_ge(sem("positions"), l + 1)
                for j in range(NORM[l, 1][1]):
                    for k in range(2):
                        G.indirect_dma_start(yg[j][:, k, :], None, y_rows,
                                             bass.IndirectOffsetOnAxis(ap=posy[:, 4 * k + j:4 * k + j + 1], axis=0))\
                            .then_inc(sem(f"yg_in{j}"), 16)

            for l in range(2):
                for k, t in enumerate((0, 1, 3, 4)):
                    pool.dma_start(bias_cols[:, l, k, :], A["ada_b"][l, t * D:(t + 1) * D].rearrange("(p c) -> p c", c=KC))\
                        .then_inc(sem("bias_cols0_in" if (l, k) in ((0, 0), (0, 1)) else "bias_cols_in"), 16)
            gate_bias(0)
            link(G.memset(par_rows, 0.0))
            link(G.memset(dec_w, 0.0))
            link(G.memset(z_all[32:33, :], 1.0))
            pool.sem_inc(sem("z_ready"), 1)
            G.memset(u_in[:, :, :, :].rearrange("p a b c -> p (a b c)"), 0.0).then_inc(sem("u_zero"), 1)
            small = [(par_rows[0:31, :], A["even_conv_w"].rearrange("a w b n -> (a w b) n")),
                     (par_rows[31:32, :], A["even_conv_b"]), (par_rows[32:33, :], A["even_conv_norm_g"]),
                     (par_rows[33:34, :], A["even_conv_norm_b"]), (par_rows[34:35, 0:P], A["even_gla_norm_g"]),
                     (w_z, A["even_w_in"][0, :, 1536:1568].rearrange("(p c) n -> p c n", c=KC)),
                     (dec_w[0:16, 0:256], A["even_dec_w_f"][0]), (dec_w[16:32, 256:512], A["even_dec_w_b"][0]),
                     (dec_w[32:33, 0:256], A["even_dec_b_f"]), (dec_w[32:33, 256:512], A["even_dec_b_b"])]
            for dst, src in small:
                pool.dma_start(dst, src).then_inc(sem("small_in"), 16)
            pool.wait_ge(sem("gate_rows"), 1)
            pool.wait_ge(sem("u_zero"), 1)
            for t in range(MAXOV):
                pool.dma_start(y_rows[(NEXP + t) * P:(NEXP + t + 1) * P, :], ar[:, A_U:A_U + D]).then_inc(sem("y_zero"), 16)
            pool.wait_ge(sem("y_zero"), 16 * MAXOV)
            pool.sem_inc(sem("margins"), 1)
            pool.wait_ge(sem("o_sum"), 4)
            router_params(0)
            dispatch(0)

            def gathers(l):
                gather(l, 0, 0)
                gather(l, 1, 1)
                with pool.Fori(0, NEXP // 2 - 1) as t:
                    gather(l, 2 * t + 2, 0)
                    gather(l, 2 * t + 3, 1)
            gathers(0)
            overflow(0)
            pool.wait_ge(sem("xgT_ps"), NEXP)
            gate_bias(1)
            combine(0)
            pool.wait_ge(sem("combined"), NT)
            for dst, src in ((gb[:, 2, :], A["final_norm_g"].rearrange("(a n) -> a n", a=1).to_broadcast([P, D])),
                             (gb[:, 3, 0:P], A["odd_q_norm_g"].to_broadcast([P, P])),
                             (gb[:, 3, P:2 * P], A["odd_k_norm_g"].to_broadcast([P, P]))):
                pool.dma_start(dst, src).then_inc(sem("norm_g_in"), 16)
            pool.wait_ge(sem("oh_taken"), HEADS)
            router_params(1)
            dispatch(1)
            gathers(1)
            overflow(1)
            combine(1)


_INS = ["x", "c", "ctx", "c_ctx", "ada_w", "ada_b", "even_w_in", "even_dec_w_f", "even_dec_b_f", "even_dec_w_b",
        "even_dec_b_b", "even_gla_norm_g", "even_conv_w", "even_conv_b", "even_conv_norm_g", "even_conv_norm_b",
        "even_w_out", "odd_w_in", "odd_q_norm_g", "odd_k_norm_g", "odd_w_out", "moe_w_group", "moe_b_group",
        "moe_w_router", "moe_b_router", "moe_w_gate", "moe_w_up", "moe_w_down", "final_norm_g"]


def kernel(**inputs):
    import concourse.bacc as bacc
    from concourse.bass_utils import run_bass_kernel_spmd

    nc = bacc.Bacc("TRN2", target_bir_lowering=False, num_devices=1)
    arrays, handles = {}, {}
    named = [(n, np.ascontiguousarray(inputs[n])) for n in _INS] + [("consts", constant_table())]
    for name, a in named:
        arrays[f"in_{name}"] = a
        handles[name] = nc.dram_tensor(f"in_{name}", a.shape, mybir.dt.from_np(a.dtype), kind="ExternalInput").ap()
    out = nc.dram_tensor("out_0", (1, 256, D), F32, kind="ExternalOutput").ap()
    hybrid_dit(nc, handles, out)
    r = run_bass_kernel_spmd(nc, [arrays], core_ids=[0])
    return r.results[0]["out_0"]
```
